# Optimizing a Trainium2 kernel written in Bass

```python
import math
import jax, jax.numpy as jnp
from jax import lax
import numpy as np

D_MODEL = 1024
BATCH = 1
SEQ = 4096
DEPTH = 1

MIX_W = D_MODEL
GROUP_W = MIX_W // 4
HEAD_DIM = 64
EPS = 1e-6
NEG_INF = -1e30
ATTN_Q_HEADS = GROUP_W // HEAD_DIM
ATTN_KV_HEADS = 2
WINDOW = 128
SSM_GROUP = 16
SSM_GROUPS = GROUP_W // SSM_GROUP
SSM_STATE = 64
SSM_DT_MIN = 1e-3
SSM_DT_MAX = 1e-1
MLSTM_HEADS = GROUP_W // HEAD_DIM
MLSTM_CHUNK = 128
MLSTM_CONV = 4
SGU_GROUPS = 4
SGU_GROUP_W = GROUP_W // SGU_GROUPS
SGU_CHUNK = 128
IN_SPLITS = (GROUP_W, ATTN_KV_HEADS * HEAD_DIM, ATTN_KV_HEADS * HEAD_DIM,
             GROUP_W,
             GROUP_W, GROUP_W, GROUP_W, MLSTM_HEADS, MLSTM_HEADS, GROUP_W,
             GROUP_W, GROUP_W)
IN_W = 2312
N_EXPERT_GROUPS = 4
EXPERTS_PER_GROUP = 8
N_EXPERTS = N_EXPERT_GROUPS * EXPERTS_PER_GROUP
TOP_K = 2
D_EXPERT = D_MODEL // 2
MOE_BLOCK = 128

kernel_name = 'hymba_style_hybrid_hier_moe'

def rmsnorm(x, g):
    xf = x.astype(jnp.float32)
    y = xf * lax.rsqrt(jnp.mean(xf * xf, axis=-1, keepdims=True) + EPS)
    return (y * g.astype(jnp.float32)).astype(x.dtype)

def layernorm(x, g, b):
    xf = x.astype(jnp.float32)
    mu = jnp.mean(xf, axis=-1, keepdims=True)
    var = jnp.mean(jnp.square(xf - mu), axis=-1, keepdims=True)
    y = (xf - mu) * lax.rsqrt(var + EPS)
    return (y * g.astype(jnp.float32) + b.astype(jnp.float32)).astype(x.dtype)

def causal_depthwise_conv(x, w):
    k = w.shape[0]
    return lax.conv_general_dilated(x, w.astype(x.dtype)[:, None, :], window_strides=(1,),
                                    padding=[(k - 1, 0)], dimension_numbers=('NWC', 'WIO', 'NWC'),
                                    feature_group_count=x.shape[-1])

def sliding_window_sink_attention(q, k, v, sinks):
    bsz, seq, hq, dh = q.shape
    hkv = k.shape[2]
    rep = hq // hkv
    nb = seq // WINDOW
    qb = q.reshape(bsz, nb, WINDOW, hkv, rep, dh)

    def with_prev(t):
        t = t.reshape(bsz, nb, WINDOW, hkv, dh)
        prev = jnp.pad(t[:, :-1], ((0, 0), (1, 0), (0, 0), (0, 0), (0, 0)))
        return jnp.concatenate([prev, t], axis=2)

    kk = with_prev(k)
    vv = with_prev(v)
    scores = jnp.einsum('bnqgrd,bnkgd->bngrqk', qb, kk).astype(jnp.float32) * (dh ** -0.5)
    qi = jnp.arange(WINDOW)[:, None] + WINDOW
    kj = jnp.arange(2 * WINDOW)[None, :]
    band = (kj <= qi) & (kj > qi - WINDOW)
    valid = band[None] & ((jnp.arange(nb)[:, None, None] > 0) | (kj >= WINDOW)[None])
    scores = jnp.where(valid[None, :, None, None], scores, NEG_INF)
    sink = jnp.broadcast_to(sinks.astype(jnp.float32).reshape(hkv, rep)[None, None, :, :, None, None],
                            scores.shape[:-1] + (1,))
    p = jax.nn.softmax(jnp.concatenate([scores, sink], axis=-1), axis=-1)[..., :-1]
    o = jnp.einsum('bngrqk,bnkgd->bnqgrd', p.astype(v.dtype), vv)
    return o.reshape(bsz, seq, hq * dh)

def _ssm_combine(e1, e2):
    a1, b1 = e1
    a2, b2 = e2
    return a2 * a1, a2 * b1 + b2

def s5_mixer(u, a_re, a_im, b_re, b_im, c_re, c_im, d_skip, log_dt, glu_w, glu_b):
    bsz, seq, _ = u.shape
    f32 = jnp.float32
    uf = u.astype(f32).reshape(bsz, seq, SSM_GROUPS, SSM_GROUP)
    a = lax.complex(a_re.astype(f32), a_im.astype(f32))
    dt = jnp.exp(log_dt.astype(f32))[:, None]
    a_bar = jnp.exp(a * dt)
    b_mat = lax.complex(b_re.astype(f32), b_im.astype(f32))
    b_bar = ((a_bar - 1.0) / a)[..., None] * b_mat
    bu = jnp.einsum('bsgh,gph->bsgp', uf.astype(jnp.complex64), b_bar)
    a_seq = jnp.broadcast_to(a_bar, bu.shape)
    _, states = lax.associative_scan(_ssm_combine, (a_seq, bu), axis=1)
    c_mat = lax.complex(c_re.astype(f32), c_im.astype(f32))
    y = jnp.einsum('bsgp,ghp->bsgh', states, c_mat).real + d_skip.astype(f32).reshape(SSM_GROUPS, SSM_GROUP) * uf
    y = jax.nn.gelu(y.reshape(bsz, seq, GROUP_W))
    y = y * jax.nn.sigmoid(y @ glu_w.astype(f32) + glu_b.astype(f32))
    return y.astype(u.dtype)

def mlstm_chunkwise(q, k, v, i_pre, f_pre):
    bsz, seq, nh, dh = q.shape
    L = MLSTM_CHUNK
    nc = seq // L
    f32 = jnp.float32
    q = q.astype(f32)
    k = k.astype(f32) * (dh ** -0.5)
    v = v.astype(f32)
    log_f = jax.nn.log_sigmoid(f_pre.astype(f32))
    log_i = i_pre.astype(f32)

    def to_chunks(t):
        return jnp.moveaxis(t.reshape((bsz, nc, L) + t.shape[2:]), 1, 0)

    causal = jnp.tril(jnp.ones((L, L), dtype=bool))

    def step(carry, inp):
        c_st, n_st, m_st = carry
        qc, kc, vc, ic, fc = inp
        b = jnp.cumsum(fc, axis=1).transpose(0, 2, 1)
        ih = ic.transpose(0, 2, 1)
        log_d = jnp.where(causal, b[..., :, None] - b[..., None, :] + ih[..., None, :], -jnp.inf)
        log_inter = b + m_st[..., None]
        m_t = jnp.maximum(log_inter, jnp.max(log_d, axis=-1))
        w_intra = jnp.exp(log_d - m_t[..., None]) * jnp.einsum('blhd,bshd->bhls', qc, kc)
        w_inter = jnp.exp(log_inter - m_t)
        num = (jnp.einsum('bhls,bshd->blhd', w_intra, vc)
               + jnp.einsum('bhl,bhvk,blhk->blhv', w_inter, c_st, qc))
        den = jnp.sum(w_intra, axis=-1) + w_inter * jnp.einsum('bhk,blhk->bhl', n_st, qc)
        h = num / jnp.maximum(jnp.abs(den), jnp.exp(-m_t)).transpose(0, 2, 1)[..., None]
        m_new = m_t[..., -1]
        w_s = jnp.exp(b[..., -1:] - b + ih - m_new[..., None])
        decay = jnp.exp(b[..., -1] + m_st - m_new)
        c_new = decay[..., None, None] * c_st + jnp.einsum('bhs,bshv,bshk->bhvk', w_s, vc, kc)
        n_new = decay[..., None] * n_st + jnp.einsum('bhs,bshk->bhk', w_s, kc)
        return (c_new, n_new, m_new), h

    init = (jnp.zeros((bsz, nh, dh, dh), f32), jnp.zeros((bsz, nh, dh), f32), jnp.zeros((bsz, nh), f32))
    xs = (to_chunks(q), to_chunks(k), to_chunks(v), to_chunks(log_i), to_chunks(log_f))
    _, hs = lax.scan(step, init, xs)
    return jnp.moveaxis(hs, 0, 1).reshape(bsz, seq, nh, dh)

def mlstm_mixer(cq, ck, cv, ci, cf, co, conv_w, gate_b, norm_g):
    bsz, seq, _ = cq.shape
    qk = jax.nn.silu(causal_depthwise_conv(jnp.concatenate([cq, ck], axis=-1), conv_w))
    q, k = jnp.split(qk, 2, axis=-1)
    shp = (bsz, seq, MLSTM_HEADS, HEAD_DIM)
    gb = gate_b.astype(jnp.float32)
    h = mlstm_chunkwise(q.reshape(shp), k.reshape(shp), cv.reshape(shp),
                        ci.astype(jnp.float32) + gb[:MLSTM_HEADS], cf.astype(jnp.float32) + gb[MLSTM_HEADS:])
    h = h * lax.rsqrt(jnp.mean(h * h, axis=-1, keepdims=True) + EPS)
    h = h * norm_g.astype(jnp.float32).reshape(MLSTM_HEADS, HEAD_DIM)
    out = jax.nn.sigmoid(co.astype(jnp.float32)) * h.reshape(bsz, seq, GROUP_W)
    return out.astype(cq.dtype)

def sgu_mixer(gu, gv, ln_g, ln_b, w_s, b_s):
    bsz, seq, _ = gu.shape
    nc = seq // SGU_CHUNK
    u = jax.nn.gelu(gu)
    v = layernorm(jax.nn.gelu(gv), ln_g, ln_b)
    vb = v.reshape(bsz, nc, SGU_CHUNK, SGU_GROUPS, SGU_GROUP_W)
    w = w_s.astype(v.dtype) * jnp.tril(jnp.ones((SGU_CHUNK, SGU_CHUNK), v.dtype))
    mixed = jnp.einsum('gts,bnsgc->bntgc', w, vb) + b_s.astype(v.dtype).T[None, None, :, :, None]
    return u * mixed.reshape(bsz, seq, GROUP_W)

def hier_moe(h, wg, bg, we, be, w_gate, w_up, w_down):
    bsz, seq, d = h.shape
    n = bsz * seq
    xf = h.reshape(n, d)
    g_logits = (xf @ wg + bg).astype(jnp.float32)
    g_prob = jax.nn.softmax(g_logits, axis=-1)
    g_sel = jnp.argmax(g_logits, axis=-1)
    p_g = jnp.take_along_axis(g_prob, g_sel[:, None], axis=1)[:, 0]
    e_logits = (xf @ we + be).astype(jnp.float32).reshape(n, N_EXPERT_GROUPS, EXPERTS_PER_GROUP)
    e_in = jnp.take_along_axis(e_logits, g_sel[:, None, None], axis=1)[:, 0]
    top_v, top_i = lax.top_k(e_in, TOP_K)
    w_pair = jax.nn.softmax(top_v, axis=-1) * p_g[:, None]
    expert_id = (g_sel[:, None] * EXPERTS_PER_GROUP + top_i).reshape(-1).astype(jnp.int32)
    tok = jnp.repeat(jnp.arange(n, dtype=jnp.int32), TOP_K)
    wts = w_pair.reshape(-1)
    m = n * TOP_K
    order = jnp.argsort(expert_id)
    se, st, sw = expert_id[order], tok[order], wts[order]
    counts = jnp.bincount(expert_id, length=N_EXPERTS)
    padded = ((counts + MOE_BLOCK - 1) // MOE_BLOCK) * MOE_BLOCK
    pad_end = jnp.cumsum(padded)
    pad_start = pad_end - padded
    start = jnp.cumsum(counts) - counts
    dest = pad_start[se] + jnp.arange(m, dtype=jnp.int32) - start[se]
    p_tot = ((m + MOE_BLOCK - 1) // MOE_BLOCK) * MOE_BLOCK + N_EXPERTS * MOE_BLOCK
    nblk = p_tot // MOE_BLOCK
    pad_tok = jnp.full((p_tot,), n, jnp.int32).at[dest].set(st)
    pad_w = jnp.zeros((p_tot,), jnp.float32).at[dest].set(sw)
    blk_e = jnp.minimum(jnp.searchsorted(pad_end, jnp.arange(nblk, dtype=jnp.int32) * MOE_BLOCK, side='right'),
                        N_EXPERTS - 1)
    x_ext = jnp.concatenate([xf, jnp.zeros((1, d), xf.dtype)], axis=0)

    def run_block(args):
        tb, wb, e = args
        xb = x_ext[tb]
        y = (jax.nn.silu(xb @ w_gate[e]) * (xb @ w_up[e])) @ w_down[e]
        return y * wb[:, None].astype(y.dtype)

    yb = lax.map(run_block, (pad_tok.reshape(nblk, MOE_BLOCK), pad_w.reshape(nblk, MOE_BLOCK), blk_e))
    out = jnp.zeros((n + 1, d), yb.dtype).at[pad_tok].add(yb.reshape(p_tot, d))[:n]
    return out.reshape(bsz, seq, d).astype(h.dtype)

def setup_inputs(seed: int = 0) -> dict:
    key = jax.random.key(seed)
    ks = jax.random.split(key, 40)
    f32 = jnp.float32

    def nrm(k, shape, scale):
        return jax.random.normal(k, shape, f32) * scale

    P, G, H = SSM_STATE, SSM_GROUPS, SSM_GROUP
    return {
        'x': nrm(ks[0], (BATCH, SEQ, D_MODEL), 1.0),
        'norm_mix_g': 1.0 + nrm(ks[1], (DEPTH, D_MODEL), 0.02),
        'w_in': nrm(ks[2], (DEPTH, D_MODEL, IN_W), D_MODEL ** -0.5),
        'attn_sinks': nrm(ks[3], (DEPTH, ATTN_Q_HEADS), 0.5),
        'ssm_a_re': -0.5 + nrm(ks[4], (DEPTH, G, P), 0.01),
        'ssm_a_im': math.pi * jnp.arange(P, dtype=f32) + nrm(ks[5], (DEPTH, G, P), 0.01),
        'ssm_b_re': nrm(ks[6], (DEPTH, G, P, H), (2 * H) ** -0.5),
        'ssm_b_im': nrm(ks[7], (DEPTH, G, P, H), (2 * H) ** -0.5),
        'ssm_c_re': nrm(ks[8], (DEPTH, G, H, P), P ** -0.5),
        'ssm_c_im': nrm(ks[9], (DEPTH, G, H, P), P ** -0.5),
        'ssm_d': nrm(ks[10], (DEPTH, GROUP_W), 1.0),
        'ssm_log_dt': jax.random.uniform(ks[11], (DEPTH, G), f32, math.log(SSM_DT_MIN), math.log(SSM_DT_MAX)),
        'ssm_glu_w': nrm(ks[12], (DEPTH, GROUP_W, GROUP_W), GROUP_W ** -0.5),
        'ssm_glu_b': nrm(ks[13], (DEPTH, GROUP_W), 0.01),
        'mlstm_conv_w': nrm(ks[14], (DEPTH, MLSTM_CONV, 2 * GROUP_W), MLSTM_CONV ** -0.5),
        'mlstm_gate_b': jnp.concatenate([nrm(ks[15], (DEPTH, MLSTM_HEADS), 0.1),
                                         jnp.linspace(3.0, 6.0, MLSTM_HEADS, dtype=f32)[None, :]
                                         + nrm(ks[16], (DEPTH, MLSTM_HEADS), 0.1)], axis=-1),
        'mlstm_norm_g': 1.0 + nrm(ks[17], (DEPTH, GROUP_W), 0.02),
        'sgu_ln_g': 1.0 + nrm(ks[18], (DEPTH, GROUP_W), 0.02),
        'sgu_ln_b': nrm(ks[19], (DEPTH, GROUP_W), 0.02),
        'sgu_w': nrm(ks[20], (DEPTH, SGU_GROUPS, SGU_CHUNK, SGU_CHUNK), SGU_CHUNK ** -0.5),
        'sgu_b': 1.0 + nrm(ks[21], (DEPTH, SGU_GROUPS, SGU_CHUNK), 0.02),
        'w_out': nrm(ks[22], (DEPTH, MIX_W, D_MODEL), MIX_W ** -0.5),
        'norm_ffn_g': 1.0 + nrm(ks[23], (DEPTH, D_MODEL), 0.02),
        'router_group_w': nrm(ks[24], (DEPTH, D_MODEL, N_EXPERT_GROUPS), D_MODEL ** -0.5),
        'router_group_b': nrm(ks[25], (DEPTH, N_EXPERT_GROUPS), 0.01),
        'router_expert_w': nrm(ks[26], (DEPTH, D_MODEL, N_EXPERTS), D_MODEL ** -0.5),
        'router_expert_b': nrm(ks[27], (DEPTH, N_EXPERTS), 0.01),
        'expert_w_gate': nrm(ks[28], (DEPTH, N_EXPERTS, D_MODEL, D_EXPERT), D_MODEL ** -0.5),
        'expert_w_up': nrm(ks[29], (DEPTH, N_EXPERTS, D_MODEL, D_EXPERT), D_MODEL ** -0.5),
        'expert_w_down': nrm(ks[30], (DEPTH, N_EXPERTS, D_EXPERT, D_MODEL), D_EXPERT ** -0.5),
        'norm_final_g': 1.0 + nrm(ks[31], (D_MODEL,), 0.02),
    }

def reference(x, norm_mix_g, w_in, attn_sinks, ssm_a_re, ssm_a_im, ssm_b_re, ssm_b_im, ssm_c_re, ssm_c_im,
              ssm_d, ssm_log_dt, ssm_glu_w, ssm_glu_b, mlstm_conv_w, mlstm_gate_b, mlstm_norm_g,
              sgu_ln_g, sgu_ln_b, sgu_w, sgu_b, w_out, norm_ffn_g, router_group_w, router_group_b,
              router_expert_w, router_expert_b, expert_w_gate, expert_w_up, expert_w_down, norm_final_g):
    bsz, seq, _ = x.shape
    split_idx = np.cumsum(IN_SPLITS)[:-1].tolist()
    for l in range(DEPTH):
        h = rmsnorm(x, norm_mix_g[l])
        z = h @ w_in[l]
        aq, ak, av, su, cq, ck, cv, ci, cf, co, gu, gv = jnp.split(z, split_idx, axis=-1)
        y_a = sliding_window_sink_attention(aq.reshape(bsz, seq, ATTN_Q_HEADS, HEAD_DIM),
                                            ak.reshape(bsz, seq, ATTN_KV_HEADS, HEAD_DIM),
                                            av.reshape(bsz, seq, ATTN_KV_HEADS, HEAD_DIM), attn_sinks[l])
        y_b = s5_mixer(su, ssm_a_re[l], ssm_a_im[l], ssm_b_re[l], ssm_b_im[l], ssm_c_re[l], ssm_c_im[l],
                       ssm_d[l], ssm_log_dt[l], ssm_glu_w[l], ssm_glu_b[l])
        y_c = mlstm_mixer(cq, ck, cv, ci, cf, co, mlstm_conv_w[l], mlstm_gate_b[l], mlstm_norm_g[l])
        y_d = sgu_mixer(gu, gv, sgu_ln_g[l], sgu_ln_b[l], sgu_w[l], sgu_b[l])
        mix = jnp.concatenate([y_a.astype(x.dtype), y_b.astype(x.dtype), y_c.astype(x.dtype), y_d.astype(x.dtype)], axis=-1)
        x = x + mix @ w_out[l]
        h = rmsnorm(x, norm_ffn_g[l])
        x = x + hier_moe(h, router_group_w[l], router_group_b[l], router_expert_w[l], router_expert_b[l],
                         expert_w_gate[l], expert_w_up[l], expert_w_down[l])
    return rmsnorm(x, norm_final_g)


_drawn_inputs = setup_inputs


def setup_inputs(seed=0):
    import zlib

    import numpy as np

    out = dict(_drawn_inputs(seed))
    spreads = {}
    factors = {'attn_sinks': 23.412,
     'ssm_a_re': 200.0,
     'ssm_b_re': 140.728,
     'ssm_glu_b': 64.0,
     'mlstm_norm_g': 17.326,
     'sgu_ln_g': 21.398,
     'sgu_ln_b': 20.523,
     'sgu_b': 14.916,
     'router_group_b': 14.017,
     'router_expert_b': 15.715,
     'norm_final_g': 24.034,
     'ssm_a_im': 52.448,
     'ssm_b_im': 64.0,
     'ssm_c_re': 61.008,
     'ssm_c_im': 64.0,
     'ssm_log_dt': 51.712,
     'norm_ffn_g': 4.262}
    for name, (base, spread) in spreads.items():
        noise = np.random.default_rng([zlib.crc32(name.encode()), seed]).standard_normal(out[name].shape)
        drawn = base * np.exp(spread * noise) if base else spread * noise
        out[name] = __import__('jax').numpy.asarray(drawn.astype(out[name].dtype))
    for name, factor in factors.items():
        out[name] = (out[name] * factor).astype(out[name].dtype)
    return out
```

```python
from contextlib import ExitStack

import concourse.bass as bass
from concourse import mybir

F32 = mybir.dt.float32
I32 = mybir.dt.int32
ALU = mybir.AluOpType
ACT = mybir.ActivationFunctionType
AX = mybir.AxisListType

P = 128
SEQ = 4096
D = 1024
TILES = SEQ // P
KD = D // P
GW = 256
HEADS = 4
DH = 64
EPS = 1e-6
GELU_A = 0.044715
GELU_B = 0.7978845608028654

AQ, AK, CQK, AV, CV, CO, GU, GV, SU, GATES = 0, 256, 384, 896, 1024, 1280, 1536, 1792, 2048, 2304
ZW = 2312
ZCHUNK = 512
ZCHUNKS = [(c, min(ZCHUNK, ZW - c)) for c in range(0, ZW, ZCHUNK)]

GROUPS, GH, STATE = 16, 16, 64
L = 16
CH = SEQ // L
CT = CH // P
LEVELS = 8

NG, NE_G = 4, 8
NE = NG * NE_G
FE = 512
KF = FE // P
BLOCKS = SEQ * 2 // P + NE - 1


class Chain:

    def __init__(self, engine, sem, per_tile=0):
        self.engine, self.sem, self.per_tile, self.base, self.n = engine, sem, per_tile, 0, 0

    def tile(self, t):
        if self.n and self.per_tile:
            assert self.n == self.per_tile, (self.n, self.per_tile)
        self.base, self.n = t * self.per_tile, 0

    def __call__(self, instruction):
        self.n += 1
        instruction.then_inc(self.sem, 1)
        self.engine.wait_ge(self.sem, self.base + self.n)


class Bank:

    def __init__(self, full, free, uses):
        self.full, self.free, self.uses = full, free, uses

    def wait_free(self, pe, t, use):
        pe.wait_ge(self.free, t * self.uses + use + 1)

    def wait_full(self, engine, t, use):
        engine.wait_ge(self.full, t * self.uses + use + 1)


def end_phase(nc, semaphores):
    nc.clear_and_free_semaphores(semaphores)
    nc.all_engine_barrier()


def pass_wait(engine, passed):
    engine.sem_inc(passed, 1)


def bc(ap, n):
    return ap.unsqueeze(2).to_broadcast([ap.shape[0], ap.shape[1], n])


def project_and_mix(nc, io, u_dram, mix_dram):
    semaphores = []
    with ExitStack() as ctx:
        ctx.callback(end_phase, nc, semaphores)

        def sb(name, shape, dt=F32):
            return ctx.enter_context(nc.sbuf_tensor(name, shape, dt))

        def sem(name):
            semaphores.append(nc.alloc_semaphore(name=name))
            return semaphores[-1]

        ident = sb("a_ident", [P, P])
        w_in = sb("w_in_sb", [P, KD, ZW])
        g_mix = sb("g_mix_sb", [P, KD])
        gate_b = sb("gate_b_sb", [P, 8])
        sinks = sb("sinks_sb", [P, HEADS])
        conv_w = sb("conv_w_sb", [P, 4, 4])
        norm_c = sb("norm_c_sb", [P, GW])
        ln_g = sb("ln_g_sb", [P, GW])
        ln_b = sb("ln_b_sb", [P, GW])
        sgu_w = sb("sgu_w_sb", [P, HEADS, P])
        sgu_b = sb("sgu_b_sb", [P, HEADS])
        tri = sb("tri_sb", [P, P])
        causal = sb("causal_sb", [P, P])
        mask_even = sb("mask_even", [P, 2, P])
        mask_even_std = sb("mask_even_std", [P, 2, P])
        mask_odd = sb("mask_odd", [P, 2, P])
        sel = sb("sel_sb", [HEADS, HEADS, P])
        half = sb("half_sb", [HEADS, P])
        slotmask = sb("slotmask_sb", [HEADS, 2])
        xb = [sb(f"a_x{j}", [P, D]) for j in range(2)]
        xn = sb("a_xn", [P, D])
        xsq = sb("xsq", [P, D])
        xT = sb("a_xT", [P, KD, P])
        ss = sb("a_ss", [P, 1])
        rs = sb("a_rs", [P, 1])
        minus_half = sb("a_minus_half", [P, HEADS])
        eps, eps_twice = sb("a_eps", [P, 1]), sb("eps_twice", [P, 1])
        z = [sb(f"z{j}", [P, ZW]) for j in range(2)]
        qT = sb("qT", [P, 2, P])
        kT = sb("kT", [P, 2, P])
        va = sb("va", [P, 2, P])
        scores = sb("scores", [P, HEADS, 2 * P])
        smax = sb("smax", [P, HEADS])
        snmax = sb("snmax", [P, HEADS])
        ssink = sb("ssink", [P, HEADS])
        esink = sb("esink", [P, HEADS])
        den = sb("den", [P, HEADS])
        rden = sb("rden", [P, HEADS])
        probs = sb("probs", [P, HEADS, 2 * P])
        pT = sb("pT", [P, HEADS, 2, P])
        cx = sb("cx", [P, 4, P + 3])
        cv = sb("cv", [P, 4, P])
        cth = sb("cth", [P, 4, P])
        qk = sb("qk", [P, 4, P])
        k_tok = sb("k_tok", [P, HEADS, DH])
        kw = sb("kw", [P, HEADS, DH])
        v1 = sb("v1", [P, HEADS, DH + 1])
        gates = sb("gates", [P, 8])
        fa = sb("fa", [P, 4])
        fy = sb("fy", [P, 4])
        fq = sb("fq", [P, 4])
        fq2 = sb("fq2", [P, 4])
        fp = sb("fp", [P, 4])
        nlogf = sb("nlogf", [P, 4])
        zero_row = sb("zero_row", [HEADS, P])
        m_row = sb("m_row", [HEADS, P])
        mt_row = sb("mt_row", [HEADS, P])
        m_prev = sb("m_prev", [HEADS, 1])
        wi_row = sb("wi_row", [HEADS, P])
        em_row = sb("em_row", [HEADS, P])
        wi_last = sb("wi_last", [HEADS, 2])
        gcol = sb("gcol", [P, 4])
        cols = sb("cols", [P, 10])
        earg = sb("earg", [P, HEADS, P])
        et = sb("et", [P, HEADS, P])
        wT = sb("wT", [P, HEADS, P])
        cn = sb("cn", [P, 2, DH + 1])
        inter = sb("inter", [P, HEADS, DH + 1])
        num = sb("num", [P, HEADS, DH + 1])
        dena = sb("dena", [P, HEADS])
        rdc = sb("rdc", [P, HEADS])
        hc = sb("hc", [P, HEADS, DH])
        hsq = sb("hsq", [P, HEADS, DH])
        hss = sb("hss", [P, HEADS])
        hrs = sb("hrs", [P, HEADS])
        coth = sb("coth", [P, GW])
        gco = sb("gco", [P, GW])
        gsq = sb("gsq", [P, 2 * GW])
        gin = sb("gin", [P, 2 * GW])
        gth = sb("gth", [P, 2 * GW])
        ge = sb("ge", [P, 2 * GW])
        bst = sb("bst", [P, 6])
        mv = sb("mv", [P, 2])
        lrs = sb("lrs", [P, 1])
        vn = sb("vn", [P, GW])
        mix = [sb(f"mix{j}", [P, 3 * GW]) for j in range(2)]

        b = [ctx.enter_context(nc.psum_tensor(f"a_bank{n}", [P, 512], F32)) for n in range(8)]
        uses = [4, 3, 3, 3, 4, 1, 1, 3]
        bank = [Bank(sem(f"a_full{n}"), sem(f"a_free{n}"), uses[n]) for n in range(8)]

        weights_in = sem("weights_in")
        consts_set = sem("consts_set")
        w_scaled = sem("w_scaled")
        x_in = [sem(f"a_x_in{j}") for j in range(2)]
        sq_done = sem("sq_done")
        xn_ready = sem("xn_ready")
        z_ready = sem("z_ready")
        su_out = [sem(f"su_out{j}") for j in range(2)]
        mix_out = [sem(f"mix_out{j}") for j in range(2)]
        mix_ready = sem("mix_ready")
        qkT_ready = sem("qkT_ready")
        cx_ready = sem("cx_ready")
        conv_ready = sem("conv_ready")
        cth_ready = sem("cth_ready")
        qk_ready = sem("qk_ready")
        gates_ready = sem("gates_ready")
        fa_ready = sem("fa_ready")
        fy_ready = sem("fy_ready")
        nlogf_ready = sem("nlogf_ready")
        m_ready = sem("m_ready")
        rows_ready = sem("rows_ready")
        wi_last_ready = sem("wi_last_ready")
        k_tok_ready = sem("k_tok_ready")
        v1_ready = sem("v1_ready")
        va_ready = sem("va_ready")
        earg_ready = sem("earg_ready")
        et_ready = sem("et_ready")
        wT_ready = sem("wT_ready")
        cn_ready = sem("cn_ready")
        snmax_ready = sem("snmax_ready")
        probs_ready = sem("probs_ready")
        esink_ready = sem("esink_ready")
        pT_ready = sem("pT_ready")
        gin_ready = sem("gin_ready")
        gth_ready = sem("gth_ready")
        ge_ready = sem("ge_ready")
        var_ready = sem("var_ready")
        lrs_ready = sem("lrs_ready")
        vn_ready = sem("vn_ready")
        vnb_ready = sem("vnb_ready")
        coth_ready = sem("coth_ready")
        hc_ready = sem("hc_ready")
        rs_ready = sem("rs_ready")
        conv_tail = sem("conv_tail")
        mask_kept = sem("mask_kept")
        hsq_ready = sem("hsq_ready")
        hss_ready = sem("hss_ready")
        hrs_ready = sem("hrs_ready")
        pool_passed, dve_passed = sem("a_pool_passed"), sem("a_dve_passed")
        dve_chain = sem("a_dve_chain")
        act_chain = sem("a_act_chain")
        pool_norm_chain = sem("a_pool_norm_chain")
        pool_mix_chain = sem("a_pool_mix_chain")

        LOADS = [(ident, io["ident"]), (w_in, io["w_in"]), (g_mix, io["g_mix"]), (gate_b, io["gate_b"]),
                 (sinks, io["sinks"]), (conv_w, io["conv_w"]), (norm_c, io["norm_c"]), (ln_g, io["ln_g"]),
                 (ln_b, io["ln_b"]), (sgu_w, io["sgu_w"]), (sgu_b, io["sgu_b"]), (tri, io["tri"]),
                 (causal, io["causal"]), (mask_even, io["mask_first"]), (mask_even_std, io["mask_even"]),
                 (mask_odd, io["mask_odd"]), (sel, io["sel"]), (half, io["half"]), (slotmask, io["slotmask"])]
        ALL_IN = 16 * len(LOADS)
        x_tiles = io["x"].rearrange("(t p) d -> t p d", p=P)
        u_tiles = u_dram.rearrange("(t p) d -> t p d", p=P)
        mix_tiles = mix_dram.rearrange("(t p) d -> t p d", p=P)
        heads_of = lambda ap, e: ap.rearrange("p (s e) l -> p e s l", e=2)[:, e]

        def run_slots(engine, slot, prologue):
            prologue()
            with engine.Fori(0, TILES // 2 - 1) as i:
                slot(i * 2, 0, i, True)
                slot(i * 2 + 1, 1, i, True)
            slot(TILES - 2, 0, TILES // 2 - 1, True)
            slot(TILES - 1, 1, TILES // 2 - 1, False)

        block = ctx.enter_context(nc.Block())

        @block.sync
        def _(sp):
            for dst, src in LOADS:
                sp.dma_start(dst[:], src).then_inc(weights_in, 16)

            def load_x(t, j):
                sp.wait_ge(xn_ready, t + 1)
                sp.dma_start(xb[j][:], x_tiles[bass.ds(t, 1)].rearrange("a p d -> (a p) d")).then_inc(x_in[j], 16)

            def slot(t, j, i, project):
                if project:
                    if not (isinstance(t, int) and t + 2 >= TILES):
                        load_x(t + 2, j)
                sp.wait_ge(z_ready, (t + 1) * len(ZCHUNKS))
                sp.dma_start(u_tiles[bass.ds(t, 1)].rearrange("a p d -> (a p) d"),
                             z[j][:, SU:SU + GW]).then_inc(su_out[j], 16)
                sp.wait_ge(mix_ready, t + 2)
                sp.dma_start(mix_tiles[bass.ds(t, 1)].rearrange("a p d -> (a p) d"), mix[j][:]).then_inc(mix_out[j], 16)

            def prologue():
                load_x(0, 0)
                load_x(1, 1)

            run_slots(sp, slot, prologue)
            for j in range(2):
                sp.wait_ge(su_out[j], 16 * (TILES // 2 + 1))
                sp.wait_ge(mix_out[j], 16 * (TILES // 2 + 1))

        @block.gpsimd
        def _(pool):
            norm_chain = Chain(pool, pool_norm_chain, 1)
            chain = Chain(pool, pool_mix_chain, 5)
            pool.sem_inc(xn_ready, 2)
            for j in range(2):
                pool.sem_inc(su_out[j], 16)
                pool.sem_inc(mix_out[j], 16)
            nc.gpsimd.memset(minus_half[:], -0.5).then_inc(consts_set, 1)
            nc.gpsimd.memset(eps[:], EPS).then_inc(consts_set, 1)
            nc.gpsimd.memset(eps_twice[:], 4 * EPS).then_inc(consts_set, 1)
            nc.gpsimd.memset(v1[:, :, DH:DH + 1], 1.0).then_inc(consts_set, 1)
            nc.gpsimd.memset(va[:, 1, :], 0.0).then_inc(consts_set, 1)
            nc.gpsimd.memset(zero_row[:], 0.0).then_inc(consts_set, 1)
            nc.gpsimd.memset(mt_row[:], 0.0).then_inc(consts_set, 1)
            nc.gpsimd.memset(cx[:, :, 0:3], 0.0).then_inc(consts_set, 1)
            nc.gpsimd.memset(kT[:, 1, :], 0.0).then_inc(consts_set, 1)
            nc.gpsimd.memset(cn[:], 0.0).then_inc(cn_ready, 1)
            pool.wait_ge(consts_set, 9)
            pool.wait_ge(weights_in, ALL_IN)

            def project(t, j, i):
                norm_chain.tile(t)
                pool.wait_ge(sq_done, t + 1)
                norm_chain(nc.gpsimd.tensor_tensor(rs[:], ss[:], eps[:], ALU.add))
                nc.gpsimd.tensor_tensor(rs[:], rs[:], minus_half[:, 0:1], ALU.pow).then_inc(rs_ready, 1)
                pool.wait_ge(rs_ready, t + 1)
                if not (isinstance(t, int) and t == 0):
                    bank[0].wait_full(pool, t - 1, 0)
                    bank[1].wait_full(pool, t - 1, 0)
                pass_wait(pool, pool_passed)
                nc.gpsimd.tensor_scalar(xn[:], xb[j][:], rs[:, 0:1], None, ALU.mult).then_inc(xn_ready, 1)

            def slot(t, j, i, projecting):
                chain.tile(t)
                if projecting:
                    project(t + 1, 1 - j, None)
                zt = z[j]
                pool.wait_ge(z_ready, (t + 1) * len(ZCHUNKS))
                pool.wait_ge(mix_ready, t + 1)
                pass_wait(pool, pool_passed)
                nc.gpsimd.tensor_copy(va[:, j, :], zt[:, AV:AV + P]).then_inc(va_ready, 1)
                nc.gpsimd.tensor_copy(v1[:, :, 0:DH], zt[:, CV:CV + GW].rearrange("p (h d) -> p h d", h=HEADS))\
                    .then_inc(v1_ready, 1)
                guv = zt[:, GU:GU + 2 * GW]
                chain(nc.gpsimd.tensor_tensor(gsq[:], guv, guv, ALU.mult))
                pass_wait(pool, pool_passed)
                chain(nc.gpsimd.tensor_scalar(gsq[:], gsq[:], GELU_A, 1.0, ALU.mult, ALU.add))
                nc.gpsimd.tensor_tensor(gin[:], gsq[:], guv, ALU.mult).then_inc(gin_ready, 1)
                pool.wait_ge(var_ready, t + 1)
                chain(nc.gpsimd.tensor_tensor(lrs[:], mv[:, 1:2], eps_twice[:], ALU.add))
                nc.gpsimd.tensor_tensor(lrs[:], lrs[:], minus_half[:, 0:1], ALU.pow).then_inc(lrs_ready, 1)
                pool.wait_ge(vn_ready, t + 1)
                chain(nc.gpsimd.tensor_tensor(vn[:], vn[:], ln_g[:], ALU.mult))
                nc.gpsimd.tensor_tensor(vn[:], vn[:], ln_b[:], ALU.add).then_inc(vnb_ready, 1)
                pool.wait_ge(hc_ready, t + 1)
                nc.gpsimd.tensor_tensor(hsq[:], hc[:], hc[:], ALU.mult).then_inc(hsq_ready, 1)
                pool.wait_ge(hss_ready, t + 1)
                pass_wait(pool, pool_passed)
                chain(nc.gpsimd.tensor_scalar(hrs[:], hss[:], 1.0 / DH, EPS, ALU.mult, ALU.add))
                nc.gpsimd.tensor_tensor(hrs[:], hrs[:], minus_half[:], ALU.pow).then_inc(hrs_ready, 1)

            run_slots(pool, slot, lambda: project(0, 0, 0))

        @block.scalar
        def _(act):
            chain = Chain(act, act_chain)
            act.wait_ge(consts_set, 9)
            act.wait_ge(weights_in, ALL_IN)

            def square(t, j, i):
                act.wait_ge(x_in[j], (i + 1) * 16)
                nc.scalar.activation(xsq[:], xb[j][:], ACT.Square, scale=D ** -0.5, accum_out=ss[:]).then_inc(sq_done, 1)

            def evac_xT(t):
                bank[0].wait_full(act, t, 0)
                nc.scalar.activation(xT[:, 0:4, :], b[0][:].rearrange("p (k n) -> p k n", k=4), ACT.Copy)\
                    .then_inc(bank[0].free, 1)

            def evac_z(t, j, n):
                c, w = ZCHUNKS[n]
                k, use = (0, 1 + n // 2) if n % 2 == 0 else (1, 1 + n // 2)
                bank[k].wait_full(act, t, use)
                nc.scalar.activation(z[j][:, c:c + w], b[k][:, 0:w], ACT.Copy).then_inc(bank[k].free, 1)
                bank[k].wait_free(act, t, use + 1)
                act.sem_inc(z_ready, 1)

            def slot(t, j, i, projecting):
                tp, jp = t + 1, 1 - j
                ip = i if j == 0 else i + 1
                zt = z[j]
                if projecting:
                    act.wait_ge(xn_ready, t + 3)
                    square(tp, jp, ip)
                bank[2].wait_full(act, t, 0)
                nc.scalar.activation(qT[:], b[2][:, 0:2 * P].rearrange("p (c n) -> p c n", c=2), ACT.Copy)\
                    .then_inc(qkT_ready, 1)
                nc.scalar.activation(kT[:, j, :], b[2][:, 2 * P:3 * P], ACT.Copy).then_inc(bank[2].free, 1)
                bank[3].wait_full(act, t, 0)
                act.wait_ge(conv_tail, t + 1)
                nc.scalar.activation(cx[:, :, 3:P + 3], b[3][:].rearrange("p (c n) -> p c n", c=4), ACT.Copy)\
                    .then_inc(bank[3].free, 1)
                act.wait_ge(gates_ready, t + 1)
                nc.scalar.activation(fa[:], gates[:, 4:8], ACT.Abs).then_inc(fa_ready, 1)
                act.wait_ge(fa_ready, t + 1)
                nc.scalar.activation(fy[:], fa[:], ACT.Exp, scale=-1.0).then_inc(fy_ready, 1)
                if projecting:
                    evac_xT(tp)
                nc.scalar.activation(coth[:], zt[:, CO:CO + GW], ACT.Tanh, scale=0.5).then_inc(coth_ready, 1)
                act.wait_ge(gin_ready, t + 1)
                nc.scalar.activation(gth[:], gin[:], ACT.Tanh, scale=GELU_B).then_inc(gth_ready, 1)
                if projecting:
                    act.wait_ge(mix_ready, t + 1)
                    act.wait_ge(su_out[jp], (ip + 1) * 16)
                    evac_z(tp, jp, 0)
                act.wait_ge(conv_ready, t + 1)
                nc.scalar.activation(cth[:], cv[:], ACT.Tanh, scale=0.5).then_inc(cth_ready, 1)
                act.wait_ge(m_ready, 2 * (t + 1))
                nc.scalar.activation(wi_row[:], m_row[:], ACT.Exp, bias=m_prev[:, 0:1], scale=-1.0).then_inc(rows_ready, 1)
                nc.scalar.activation(em_row[:], mt_row[:], ACT.Exp, scale=-1.0).then_inc(rows_ready, 1)
                if projecting:
                    evac_z(tp, jp, 1)
                act.wait_ge(snmax_ready, t + 1)
                for h in range(HEADS):
                    nc.scalar.activation(probs[:, h, :], scores[:, h, :], ACT.Exp, bias=snmax[:, h:h + 1],
                                         scale=DH ** -0.5, accum_out=den[:, h:h + 1]).then_inc(probs_ready, 1)
                nc.scalar.activation(esink[:], ssink[:], ACT.Exp).then_inc(esink_ready, 1)
                bank[7].wait_full(act, t, 0)
                nc.scalar.activation(k_tok[:], b[7][:, 0:GW].rearrange("p (h d) -> p h d", h=HEADS), ACT.Copy)\
                    .then_inc(bank[7].free, 1)
                act.wait_ge(earg_ready, t + 1)
                for h in range(HEADS):
                    nc.scalar.activation(et[:, h, :], earg[:, h, :], ACT.Exp, bias=gcol[:, h:h + 1])\
                        .then_inc(et_ready, 1)
                if projecting:
                    evac_z(tp, jp, 2)
                bank[2].wait_full(act, t, 2)
                nc.scalar.activation(pT[:, 0:2].rearrange("p h s n -> p (h s n)"), b[2][:], ACT.Copy)\
                    .then_inc(bank[2].free, 1)
                bank[3].wait_full(act, t, 2)
                nc.scalar.activation(pT[:, 2:4].rearrange("p h s n -> p (h s n)"), b[3][:], ACT.Copy)\
                    .then_inc(bank[3].free, 1)
                if projecting:
                    evac_z(tp, jp, 3)
                    evac_z(tp, jp, 4)

            def prologue():
                square(0, 0, 0)
                evac_xT(0)
                for n in range(len(ZCHUNKS)):
                    evac_z(0, 0, n)

            run_slots(act, slot, prologue)

        @block.vector
        def _(dve):
            chain = Chain(dve, dve_chain, 50)
            for k in bank:
                dve.sem_inc(k.free, 1)
            dve.sem_inc(mix_ready, 1)
            dve.sem_inc(conv_tail, 1)
            dve.sem_inc(mask_kept, 1)
            dve.wait_ge(consts_set, 9)
            dve.wait_ge(weights_in, ALL_IN)
            for k in range(KD):
                nc.vector.tensor_scalar(w_in[:, k, :], w_in[:, k, :], g_mix[:, k:k + 1], None, ALU.mult)\
                    .then_inc(w_scaled, 1)
            nc.vector.tensor_tensor(sgu_w[:], sgu_w[:], tri[:].unsqueeze(1).to_broadcast([P, HEADS, P]), ALU.mult)\
                .then_inc(w_scaled, 1)

            def evac_xT(t):
                bank[1].wait_full(dve, t, 0)
                nc.vector.tensor_copy(xT[:, 4:8, :], b[1][:].rearrange("p (k n) -> p k n", k=4))\
                    .then_inc(bank[1].free, 1)

            def slot(t, j, i, projecting):
                chain.tile(t)
                zt, mx = z[j], mix[j]
                dve.wait_ge(z_ready, (t + 1) * len(ZCHUNKS))
                nc.vector.tensor_tensor(gates[:], zt[:, GATES:GATES + 8], gate_b[:], ALU.add).then_inc(gates_ready, 1)
                dve.wait_ge(gates_ready, t + 1)
                dve.wait_ge(fy_ready, t + 1)
                chain(nc.vector.tensor_scalar(fp[:], fy[:], 2.0, None, ALU.add))
                chain(nc.vector.reciprocal(fp[:], fp[:]))
                chain(nc.vector.tensor_tensor(fq[:], fy[:], fp[:], ALU.mult))
                chain(nc.vector.tensor_tensor(fq2[:], fq[:], fq[:], ALU.mult))
                chain(nc.vector.tensor_scalar(fp[:], fq2[:], 1.0 / 17, None, ALU.mult))
                for c in (15, 13, 11, 9, 7, 5, 3):
                    chain(nc.vector.scalar_tensor_tensor(fp[:], fp[:], 1.0 / c, fq2[:], ALU.add, ALU.mult))
                chain(nc.vector.scalar_tensor_tensor(fp[:], fp[:], 1.0, fq[:], ALU.add, ALU.mult))
                chain(nc.vector.tensor_scalar(fq[:], gates[:, 4:8], -1.0, 0.0, ALU.mult, ALU.max))
                nc.vector.scalar_tensor_tensor(nlogf[:], fp[:], 2.0, fq[:], ALU.mult, ALU.add).then_inc(nlogf_ready, 1)
                if projecting:
                    evac_xT(t + 1)
                bank[4].wait_full(dve, t, 0)
                nc.vector.tensor_copy(m_prev[:], mt_row[:, P - 1:P]).then_inc(m_ready, 1)
                chain(nc.vector.tensor_tensor_scan(m_row[:], zero_row[:], b[4][0:HEADS, P:2 * P],
                                                   mt_row[:, P - 1:P], ALU.add, ALU.max))
                chain(nc.vector.tensor_copy(gcol[:], b[4][:, 2 * P:2 * P + 4]))
                nc.vector.tensor_tensor(mt_row[:], m_row[:], b[4][0:HEADS, 0:P], ALU.subtract)\
                    .then_inc(bank[4].free, 1)
                bank[4].wait_free(dve, t, 1)
                dve.sem_inc(m_ready, 1)
                mask = mask_even if j == 0 else mask_odd
                dve.wait_ge(mask_kept, i + 1)
                for e in range(2):
                    bank[2 + e].wait_full(dve, t, 1)
                    nc.vector.tensor_tensor(scores[:, 2 * e:2 * e + 2, :],
                                            b[2 + e][:].rearrange("p (h n) -> p h n", h=2),
                                            mask[:].rearrange("p s n -> p (s n)").unsqueeze(1)
                                            .to_broadcast([P, 2, 2 * P]), ALU.add).then_inc(bank[2 + e].free, 1)
                bank[2].wait_free(dve, t, 2)
                bank[3].wait_free(dve, t, 2)
                chain(nc.vector.tensor_reduce(smax[:], scores[:], AX.X, ALU.max))
                chain(nc.vector.scalar_tensor_tensor(smax[:], smax[:], DH ** -0.5, sinks[:], ALU.mult, ALU.max))
                chain(nc.vector.tensor_tensor(ssink[:], sinks[:], smax[:], ALU.subtract))
                if j == 0:
                    nc.vector.tensor_copy(mask_even[:], mask_even_std[:]).then_inc(mask_kept, 1)
                nc.vector.tensor_scalar(snmax[:], smax[:], -1.0, None, ALU.mult).then_inc(snmax_ready, 1)
                bank[3].wait_free(dve, t, 1)
                for c in range(4):
                    chain(nc.vector.tensor_scalar(cv[:, c, :], cx[:, c, 0:P], conv_w[:, c, 0:1], None, ALU.mult))
                for tap in range(1, 4):
                    for c in range(4):
                        ins = nc.vector.scalar_tensor_tensor(cv[:, c, :], cx[:, c, tap:tap + P],
                                                             conv_w[:, c, tap:tap + 1], cv[:, c, :], ALU.mult, ALU.add)
                        if tap == 3 and c == 3:
                            ins.then_inc(conv_ready, 1)
                        else:
                            chain(ins)
                dve.wait_ge(conv_ready, t + 1)
                nc.vector.tensor_copy(cx[:, :, 0:3], cx[:, :, P:P + 3]).then_inc(conv_tail, 1)
                dve.wait_ge(cth_ready, t + 1)
                nc.vector.scalar_tensor_tensor(qk[:], cth[:], 1.0, cv[:], ALU.add, ALU.mult).then_inc(qk_ready, 1)
                dve.wait_ge(gth_ready, t + 1)
                nc.vector.scalar_tensor_tensor(ge[:], gth[:], 1.0, zt[:, GU:GU + 2 * GW], ALU.add, ALU.mult)\
                    .then_inc(ge_ready, 1)
                dve.wait_ge(ge_ready, t + 1)
                chain(nc.vector.bn_stats(bst[:], ge[:, GW:2 * GW]))
                pass_wait(dve, dve_passed)
                nc.vector.bn_aggr(mv[:], bst[:]).then_inc(var_ready, 1)
                dve.wait_ge(rows_ready, 2 * (t + 1))
                nc.vector.tensor_scalar(wi_last[:], slotmask[:], wi_row[:, P - 1:P], None, ALU.mult)\
                    .then_inc(wi_last_ready, 1)
                bank[4].wait_full(dve, t, 1)
                nc.vector.tensor_tensor(earg[:], causal[:].unsqueeze(1).to_broadcast([P, HEADS, P]),
                                        b[4][:].rearrange("p (h n) -> p h n", h=HEADS), ALU.subtract)\
                    .then_inc(bank[4].free, 1)
                bank[4].wait_free(dve, t, 2)
                dve.sem_inc(earg_ready, 1)
                dve.wait_ge(lrs_ready, t + 1)
                dve.wait_ge(var_ready, t + 1)
                nc.vector.tensor_scalar(vn[:], ge[:, GW:2 * GW], mv[:, 0:1], lrs[:, 0:1], ALU.subtract, ALU.mult)\
                    .then_inc(vn_ready, 1)
                bank[7].wait_full(dve, t, 1)
                nc.vector.tensor_copy(cols[:], b[7][:, 0:10]).then_inc(bank[7].free, 1)
                bank[7].wait_free(dve, t, 2)
                dve.wait_ge(et_ready, 4 * (t + 1))
                for e in range(2):
                    bank[5 + e].wait_full(dve, t, 0)
                    chain(nc.vector.tensor_tensor(heads_of(wT[:], e), heads_of(et[:], e),
                                                  b[5 + e][:, 0:2 * P].rearrange("p (s n) -> p s n", s=2), ALU.mult))
                    nc.vector.tensor_tensor(heads_of(inter[:], e),
                                            b[5 + e][:, 2 * P:2 * P + 130].rearrange("p (s n) -> p s n", s=2),
                                            bc(cols[:, e:4:2], DH + 1), ALU.mult).then_inc(bank[5 + e].free, 1)
                bank[6].wait_free(dve, t + 1, 0)
                bank[7].wait_free(dve, t, 1)
                nc.vector.tensor_tensor(kw[:], k_tok[:], et[:, :, P - 1:P].to_broadcast([P, HEADS, DH]), ALU.mult)\
                    .then_inc(wT_ready, 1)
                dve.wait_ge(coth_ready, t + 1)
                chain(nc.vector.scalar_tensor_tensor(gco[:], coth[:], 1.0, norm_c[:], ALU.add, ALU.mult))
                bank[7].wait_full(dve, t, 2)
                bank[5].wait_free(dve, t + 1, 0)
                chain(nc.vector.tensor_tensor(num[:], b[7][:, 0:260].rearrange("p (h n) -> p h n", h=HEADS), inter[:],
                                              ALU.add))
                for s in range(2):
                    ins = nc.vector.scalar_tensor_tensor(cn[:, s, :], cn[:, s, :], cols[:, 8 + s:9 + s],
                                                         b[7][:, 260 + 65 * s:325 + 65 * s], ALU.mult, ALU.add)
                    if s == 0:
                        chain(ins)
                    else:
                        ins.then_inc(bank[7].free, 1)
                bank[7].wait_free(dve, t + 1, 0)
                dve.sem_inc(cn_ready, 1)
                den_c = num[:, :, DH]
                chain(nc.vector.tensor_scalar(dena[:], cols[:, 4:8], 32.0, None, ALU.mult))
                chain(nc.vector.tensor_tensor(dena[:], dena[:], den_c, ALU.max))
                chain(nc.vector.scalar_tensor_tensor(dena[:], den_c, -1.0, dena[:], ALU.mult, ALU.max))
                chain(nc.vector.reciprocal(rdc[:], dena[:]))
                nc.vector.tensor_tensor(hc[:], num[:, :, 0:DH], bc(rdc[:], DH), ALU.mult).then_inc(hc_ready, 1)
                dve.wait_ge(esink_ready, t + 1)
                dve.wait_ge(probs_ready, 4 * (t + 1))
                chain(nc.vector.tensor_tensor(den[:], den[:], esink[:], ALU.add))
                chain(nc.vector.reciprocal(rden[:], den[:]))
                dve.wait_ge(mix_out[j], (i + 1) * 16)
                bank[4].wait_full(dve, t, 2)
                for g in range(HEADS):
                    ins = nc.vector.scalar_tensor_tensor(mx[:, 2 * GW + 64 * g:2 * GW + 64 * g + 64],
                                                         b[4][:, 64 * g:64 * g + 64], sgu_b[:, g:g + 1],
                                                         ge[:, 64 * g:64 * g + 64], ALU.add, ALU.mult)
                    if g < 3:
                        chain(ins)
                    else:
                        ins.then_inc(bank[4].free, 1)
                bank[4].wait_free(dve, t, 3)
                dve.wait_ge(hsq_ready, t + 1)
                nc.vector.tensor_reduce(hss[:], hsq[:], AX.X, ALU.add).then_inc(hss_ready, 1)
                chain(nc.vector.tensor_tensor(hc[:], hc[:], gco[:].rearrange("p (h d) -> p h d", h=HEADS), ALU.mult))
                bank[4].wait_full(dve, t, 3)
                nc.vector.tensor_tensor(mx[:, 0:GW].rearrange("p (h d) -> p h d", h=HEADS),
                                        b[4][:, 0:GW].rearrange("p (h d) -> p h d", h=HEADS), bc(rden[:], DH),
                                        ALU.mult).then_inc(bank[4].free, 1)
                bank[4].wait_free(dve, t + 1, 0)
                dve.wait_ge(hrs_ready, t + 1)
                nc.vector.tensor_tensor(mx[:, GW:2 * GW].rearrange("p (h d) -> p h d", h=HEADS), hc[:],
                                        bc(hrs[:], DH), ALU.mult).then_inc(mix_ready, 1)

            run_slots(dve, slot, lambda: evac_xT(0))

        @block.tensor
        def _(pe):
            pe.wait_ge(weights_in, ALL_IN)
            pe.wait_ge(w_scaled, KD + 1)

            def transpose_x(t):
                pe.wait_ge(xn_ready, t + 3)
                for k in range(2):
                    bank[k].wait_free(pe, t, 0)
                    for c in range(4):
                        ins = nc.tensor.transpose(b[k][:, c * P:(c + 1) * P], xn[:, (4 * k + c) * P:(4 * k + c + 1) * P],
                                                  ident[:])
                    ins.then_inc(bank[k].full, 1)

            def project(t, n):
                c, w = ZCHUNKS[n]
                k, use = n % 2, 1 + n // 2
                if n == 0:
                    bank[1].wait_free(pe, t, 1)
                bank[k].wait_free(pe, t, use)
                for d in range(KD):
                    ins = nc.tensor.matmul(b[k][:, 0:w], xT[:, d, :], w_in[:, d, c:c + w], start=d == 0, stop=d == KD - 1)
                ins.then_inc(bank[k].full, 1)

            def slot(t, j, i, projecting):
                tp = t + 1
                zt = z[j]
                pe.wait_ge(z_ready, (t + 1) * len(ZCHUNKS))
                bank[2].wait_free(pe, t, 0)
                for c in range(3):
                    ins = nc.tensor.transpose(b[2][:, c * P:(c + 1) * P], zt[:, AQ + c * P:AQ + (c + 1) * P], ident[:])
                ins.then_inc(bank[2].full, 1)
                bank[3].wait_free(pe, t, 0)
                for c in range(4):
                    ins = nc.tensor.transpose(b[3][:, c * P:(c + 1) * P], zt[:, CQK + c * P:CQK + (c + 1) * P], ident[:])
                ins.then_inc(bank[3].full, 1)
                if projecting:
                    transpose_x(tp)
                bank[4].wait_free(pe, t, 0)
                pe.wait_ge(nlogf_ready, t + 1)
                nc.tensor.matmul(b[4][0:HEADS, 0:P], nlogf[:], tri[:], start=True, stop=True)
                nc.tensor.matmul(b[4][0:HEADS, P:2 * P], nlogf[:], tri[:], start=True, stop=False)
                nc.tensor.matmul(b[4][0:HEADS, P:2 * P], gates[:, 0:4], ident[:], start=False, stop=True)
                nc.tensor.matmul(b[4][:, 2 * P:2 * P + 4], tri[:], nlogf[:], start=True, stop=False)
                nc.tensor.matmul(b[4][:, 2 * P:2 * P + 4], ident[:], gates[:, 0:4], start=False, stop=True)\
                    .then_inc(bank[4].full, 1)
                for e in range(2):
                    bank[2 + e].wait_free(pe, t, 1)
                    for c in range(2):
                        ins = nc.tensor.matmul(b[2 + e][:, c * 2 * P:(c + 1) * 2 * P], qT[64 * e:64 * e + 64, c, :],
                                               kT[64 * e:64 * e + 64].rearrange("p s n -> p (s n)"),
                                               start=True, stop=True)
                    ins.then_inc(bank[2 + e].full, 1)
                if projecting:
                    project(tp, 0)
                bank[4].wait_free(pe, t, 1)
                for h in range(HEADS):
                    ins = nc.tensor.matmul(b[4][:, h * P:(h + 1) * P], sel[:, h, :], m_row[:], start=True, stop=True)
                ins.then_inc(bank[4].full, 1)
                pe.wait_ge(qk_ready, t + 1)
                pe.wait_ge(cn_ready, t + 1)
                for e in range(2):
                    bank[5 + e].wait_free(pe, t, 0)
                    rows = slice(64 * e, 64 * e + 64)
                    for s in range(2):
                        nc.tensor.matmul(b[5 + e][:, s * P:(s + 1) * P], qk[rows, 2 + s, :], qk[rows, s, :],
                                         start=True, stop=True)
                    for s in range(2):
                        ins = nc.tensor.matmul(b[5 + e][:, 2 * P + 65 * s:2 * P + 65 * s + 65], qk[rows, s, :],
                                               cn[rows, s, :], start=True, stop=True)
                    ins.then_inc(bank[5 + e].full, 1)
                bank[7].wait_free(pe, t, 0)
                for s in range(2):
                    ins = nc.tensor.transpose(b[7][:, s * P:(s + 1) * P], qk[:, 2 + s, :], ident[:])
                ins.then_inc(bank[7].full, 1)
                if projecting:
                    project(tp, 1)
                bank[7].wait_free(pe, t, 1)
                pe.wait_ge(rows_ready, 2 * (t + 1))
                pe.wait_ge(wi_last_ready, t + 1)
                nc.tensor.matmul(b[7][:, 0:4], wi_row[:], ident[0:4, 0:4], start=True, stop=True)
                nc.tensor.matmul(b[7][:, 4:8], em_row[:], ident[0:4, 0:4], start=True, stop=True)
                nc.tensor.matmul(b[7][:, 8:10], half[:], wi_last[:], start=True, stop=True).then_inc(bank[7].full, 1)
                if projecting:
                    project(tp, 2)
                pe.wait_ge(vnb_ready, t + 1)
                bank[4].wait_free(pe, t, 2)
                for g in range(HEADS):
                    ins = nc.tensor.matmul(b[4][:, 64 * g:64 * g + 64], sgu_w[:, g, :], vn[:, 64 * g:64 * g + 64],
                                           start=True, stop=True)
                ins.then_inc(bank[4].full, 1)
                pe.wait_ge(wT_ready, t + 1)
                pe.wait_ge(v1_ready, t + 1)
                bank[7].wait_free(pe, t, 2)
                for h in range(HEADS):
                    nc.tensor.matmul(b[7][:, 65 * h:65 * h + 65], wT[:, h, :], v1[:, h, :], start=True, stop=True)
                for h in range(HEADS):
                    lo, s = 64 * (h % 2), h // 2
                    ins = nc.tensor.matmul(b[7][lo:lo + 64, 260 + 65 * s:325 + 65 * s], kw[:, h, :], v1[:, h, :],
                                           start=True, stop=True)
                ins.then_inc(bank[7].full, 1)
                pe.wait_ge(probs_ready, 4 * (t + 1))
                for e in range(2):
                    bank[2 + e].wait_free(pe, t, 2)
                    for n in range(4):
                        ins = nc.tensor.transpose(b[2 + e][:, n * P:(n + 1) * P],
                                                  probs[:, 2 * e + n // 2, (n % 2) * P:(n % 2 + 1) * P], ident[:])
                    ins.then_inc(bank[2 + e].full, 1)
                if projecting:
                    project(tp, 3)
                pe.wait_ge(va_ready, t + 1)
                bank[3].wait_free(pe, t + 1, 0)
                bank[4].wait_free(pe, t, 3)
                for h in range(HEADS):
                    for s in range(2):
                        ins = nc.tensor.matmul(b[4][:, 64 * h:64 * h + 64], pT[:, h, s, :],
                                               va[:, s, 64 * (h // 2):64 * (h // 2) + 64], start=s == 0, stop=s == 1)
                ins.then_inc(bank[4].full, 1)
                if projecting:
                    project(tp, 4)

            def prologue():
                transpose_x(0)
                for n in range(len(ZCHUNKS)):
                    project(0, n)

            run_slots(pe, slot, prologue)


def state_space(nc, io, u_dram, y_dram):
    semaphores = []
    with ExitStack() as ctx:
        ctx.callback(end_phase, nc, semaphores)

        def sb(name, shape, dt=F32):
            return ctx.enter_context(nc.sbuf_tensor(name, shape, dt))

        def sem(name):
            semaphores.append(nc.alloc_semaphore(name=name))
            return semaphores[-1]

        G = GROUPS
        ZM = 2 * L - 9
        PAD = P
        ident = sb("s_ident", [P, P])
        swap = sb("swap_sb", [P, P])
        sign = sb("sign_sb", [P, 1])
        idt = sb("idt_sb", [P, 3 * P])
        dskip = sb("dskip_sb", [P, G])
        are, aim, ldt = sb("are", [P, G]), sb("aim", [P, G]), sb("ldt", [P, G])
        b1, b2 = sb("b1", [P, G, GH]), sb("b2", [P, G, GH])
        c1, c2 = sb("c1", [P, G, GH]), sb("c2", [P, G, GH])
        dt = sb("dt", [P, G])
        ex, en, en2, ei = sb("ex", [P, G]), sb("en", [P, G]), sb("en2", [P, G]), sb("ei", [P, G], I32)
        ep, es = sb("ep", [P, G]), sb("es", [P, G])
        mag, th, sn, cs = sb("mag", [P, G]), sb("th", [P, G]), sb("sn", [P, G]), sb("cs", [P, G])
        pr, pi = sb("pr", [P, L + 1, G]), sb("pi", [P, L + 1, G])
        t1, t2 = sb("t1", [P, 8 * G]), sb("t2", [P, 8 * G])
        qr, qi = sb("qr", [P, LEVELS, G]), sb("qi", [P, LEVELS, G])
        cr, ci = sb("cr", [P, G]), sb("ci", [P, G])
        bb1, bb2 = sb("bb1", [P, G, GH]), sb("bb2", [P, G, GH])
        tb = sb("tb", [P, G, GH])
        zz = sb("zz", [P, G, ZM, GH])
        oo = sb("oo", [P, G, L, GH])
        u = sb("u_sb", [P, CT, L, GW])
        y = sb("y_sb", [P, CT, L, GW])
        zg = [sb(f"zg{e}", [P, ZM, GH]) for e in range(2)]
        ug = [sb(f"ug{e}", [P, CT, L, GH]) for e in range(2)]
        uT = [sb(f"uT{e}", [P, 2, CT * P]) for e in range(2)]
        rg = [sb(f"rg{e}", [P, 2, P]) for e in range(2)]
        tg = [sb(f"tg{e}", [P, 3 * P]) for e in range(2)]
        st = [[sb(f"st{e}{n}", [P, PAD + CH]) for n in range(2)] for e in range(2)]

        b = [ctx.enter_context(nc.psum_tensor(f"s_bank{n}", [P, 512], F32)) for n in range(8)]
        uses = [2, 2, 1 + LEVELS, 1]
        bank = [[Bank(sem(f"s_full{e}{n}"), sem(f"s_free{e}{n}"), uses[n]) for n in range(4)] for e in range(2)]

        consts_in = sem("s_consts_in")
        u_in = sem("s_u_in")
        y_out = sem("s_y_out")
        pads_set = sem("pads_set")
        sin_arg = sem("sin_arg")
        sin_done = sem("sin_done")
        coeffs = sem("coeffs")
        group_copied = [sem(f"group_copied{e}") for e in range(2)]
        uT_ready = [sem(f"uT_ready{e}") for e in range(2)]
        level_done = [sem(f"level_done{e}") for e in range(2)]
        chain_sem = sem("s_dve_chain")
        pool_passed = sem("s_pool_passed")
        half_sem = [sem(f"half_level{e}") for e in range(2)]

        LOADS = [(ident, io["ident"]), (swap, io["swap"]), (sign, io["sign"]), (idt, io["idt"]),
                 (dskip, io["dskip"]), (are, io["are"]), (aim, io["aim"]), (ldt, io["ldt"]),
                 (b1, io["b1"]), (b2, io["b2"]), (c1, io["c1"]), (c2, io["c2"])]
        ALL_IN = 16 * len(LOADS)
        u_v = u_dram.rearrange("(t c l) w -> t c l w", c=P, l=L)
        y_v = y_dram.rearrange("(t c l) w -> t c l w", c=P, l=L)
        PAIRS = G // 2

        block = ctx.enter_context(nc.Block())

        @block.sync
        def _(sp):
            for dst, src in LOADS:
                sp.dma_start(dst[:], src).then_inc(consts_in, 16)
            for t in range(CT):
                sp.dma_start(u[:, t], u_v[t]).then_inc(u_in, 16)
            for e in range(2):
                bank[e][0].wait_free(sp, PAIRS, 0)
            for t in range(CT):
                sp.dma_start(y_v[t], y[:, t]).then_inc(y_out, 16)
            sp.wait_ge(y_out, 16 * CT)

        @block.gpsimd
        def _(pool):
            for e in range(2):
                for n in range(2):
                    nc.gpsimd.memset(st[e][n][:, 0:PAD], 0.0).then_inc(pads_set, 1)
            nc.gpsimd.memset(zz[:, :, L:ZM, :], 0.0).then_inc(pads_set, 1)
            pool.wait_ge(u_in, 16 * CT)
            pool.wait_ge(coeffs, 1)
            pool.wait_ge(pads_set, 5)
            with pool.Fori(0, PAIRS) as i:
                for e in range(2):
                    bank[e][1].wait_free(pool, i, 0)
                    pass_wait(pool, pool_passed)
                    nc.gpsimd.tensor_copy(zg[e][:], zz[:, bass.ds(i * 2 + e, 1), :, :].rearrange("p a m h -> p (a m) h"))\
                        .then_inc(group_copied[e], 1)
                    nc.gpsimd.tensor_copy(ug[e][:].rearrange("p t l h -> p (t l) h"),
                                          u[:, :, :, bass.ds((i * 2 + e) * GH, GH)].rearrange("p t l h -> p (t l) h"))\
                        .then_inc(group_copied[e], 1)

        @block.scalar
        def _(act):
            act.wait_ge(sin_arg, 1)
            nc.scalar.activation(sn[:], th[:], ACT.Sin).then_inc(sin_done, 1)
            nc.scalar.activation(cs[:], th[:], ACT.Sin, scale=0.5).then_inc(sin_done, 1)
            with act.Fori(0, PAIRS) as i:
                for e in range(2):
                    bank[e][0].wait_full(act, i, 0)
                    nc.scalar.activation(uT[e][:], b[4 * e][:].rearrange("p (k n) -> p k n", k=2), ACT.Copy)\
                        .then_inc(bank[e][0].free, 1)
                    bank[e][1].wait_full(act, i, 0)
                    nc.scalar.activation(rg[e][:], b[4 * e + 1][:, 0:2 * P].rearrange("p (k n) -> p k n", k=2), ACT.Copy)\
                        .then_inc(bank[e][1].free, 1)
                for e in range(2):
                    bank[e][2].wait_full(act, i, 0)
                    nc.scalar.activation(st[e][0][:, PAD:PAD + CH], b[4 * e + 2][:, 0:CH], ACT.Copy)\
                        .then_inc(bank[e][2].free, 1)
                for e in range(2):
                    bank[e][0].wait_full(act, i, 1)
                    nc.scalar.activation(y[:, :, :, bass.ds((i * 2 + e) * GH, GH)].rearrange("p t l h -> p (t l) h"),
                                         b[4 * e][:].rearrange("p (a h) -> p a h", h=GH), ACT.Copy)\
                        .then_inc(bank[e][0].free, 1)

        @block.vector
        def _(dve):
            chain = Chain(dve, chain_sem)
            for e in range(2):
                for k in bank[e]:
                    dve.sem_inc(k.free, 1)
            dve.wait_ge(consts_in, ALL_IN)
            V = nc.vector

            def rint(out, x):
                chain(V.tensor_scalar(out, x, 12582912.0, None, ALU.add))
                chain(V.tensor_scalar(out, out, 12582912.0, None, ALU.subtract))

            def exp(out, x):
                chain(V.tensor_scalar(ex[:], x, -104.0, 89.0, ALU.max, ALU.min))
                chain(V.tensor_scalar(en[:], ex[:], 1.4426950408889634, None, ALU.mult))
                rint(en[:], en[:])
                chain(V.scalar_tensor_tensor(ex[:], en[:], -0.693359375, ex[:], ALU.mult, ALU.add))
                chain(V.scalar_tensor_tensor(ex[:], en[:], 2.12194440e-4, ex[:], ALU.mult, ALU.add))
                chain(V.tensor_scalar(ep[:], ex[:], 1.0 / 40320, None, ALU.mult))
                for c in (5040, 720, 120, 24, 6, 2, 1):
                    chain(V.scalar_tensor_tensor(ep[:], ep[:], 1.0 / c, ex[:], ALU.add, ALU.mult))
                chain(V.tensor_scalar(ep[:], ep[:], 1.0, None, ALU.add))
                chain(V.tensor_scalar(en2[:], en[:], 0.5, None, ALU.mult))
                rint(en2[:], en2[:])
                chain(V.tensor_tensor(en[:], en[:], en2[:], ALU.subtract))
                for n in (en, en2):
                    chain(V.tensor_scalar(es[:], n[:], 127.0, 8388608.0, ALU.add, ALU.mult))
                    chain(V.tensor_copy(ei[:], es[:]))
                    chain(V.tensor_tensor(ep[:], ep[:], ei[:].bitcast(F32), ALU.mult))
                chain(V.tensor_copy(out, ep[:]))

            def cmul(outr, outi, ar, ai, br, bi, sr, si):
                chain(V.tensor_tensor(sr, ai, bi, ALU.mult))
                chain(V.tensor_tensor(si, ar, bi, ALU.mult))
                chain(V.tensor_tensor(outr, ar, br, ALU.mult))
                chain(V.tensor_tensor(outi, ai, br, ALU.mult))
                chain(V.tensor_tensor(outr, outr, sr, ALU.subtract))
                chain(V.tensor_tensor(outi, outi, si, ALU.add))

            flat = lambda a: a[:].rearrange("p g h -> p (g h)")
            chain(V.tensor_scalar(flat(b2), flat(b2), sign[:, 0:1], None, ALU.mult))
            chain(V.tensor_scalar(flat(c1), flat(c1), sign[:, 0:1], -1.0, ALU.mult, ALU.mult))
            chain(V.tensor_scalar(flat(c2), flat(c2), -1.0, None, ALU.mult))
            exp(dt[:], ldt[:])
            chain(V.tensor_tensor(mag[:], are[:], dt[:], ALU.mult))
            exp(mag[:], mag[:])
            chain(V.tensor_tensor(th[:], aim[:], dt[:], ALU.mult))
            chain(V.tensor_scalar(en[:], th[:], 0.15915494309189535, None, ALU.mult))
            rint(en[:], en[:])
            chain(V.scalar_tensor_tensor(th[:], en[:], -6.28125, th[:], ALU.mult, ALU.add))
            chain(V.scalar_tensor_tensor(th[:], en[:], -0.0019340515136718750, th[:], ALU.mult, ALU.add))
            chain(V.scalar_tensor_tensor(th[:], en[:], -1.2556659146e-06, th[:], ALU.mult, ALU.add))
            V.tensor_scalar(th[:], th[:], 3.1415925, -3.1415925, ALU.min, ALU.max).then_inc(sin_arg, 1)
            dve.wait_ge(sin_done, 2)
            chain(V.tensor_tensor(cs[:], cs[:], cs[:], ALU.mult))
            chain(V.tensor_scalar(cs[:], cs[:], -2.0, 1.0, ALU.mult, ALU.add))
            chain(V.memset(pr[:, 0, :], 1.0))
            chain(V.memset(pi[:, 0, :], 0.0))
            chain(V.tensor_tensor(pr[:, 1, :], mag[:], cs[:], ALU.mult))
            chain(V.tensor_tensor(pi[:, 1, :], mag[:], sn[:], ALU.mult))
            n = 1
            while n < L:
                shape = [P, n, G]
                s1 = t1[:, 0:n * G].rearrange("p (n g) -> p n g", g=G)
                s2 = t2[:, 0:n * G].rearrange("p (n g) -> p n g", g=G)
                cmul(pr[:, n + 1:2 * n + 1, :], pi[:, n + 1:2 * n + 1, :], pr[:, 1:n + 1, :], pi[:, 1:n + 1, :],
                     pr[:, n:n + 1, :].to_broadcast(shape), pi[:, n:n + 1, :].to_broadcast(shape), s1, s2)
                n *= 2
            chain(V.tensor_copy(qr[:, 0, :], pr[:, L, :]))
            chain(V.tensor_copy(qi[:, 0, :], pi[:, L, :]))
            for n in range(1, LEVELS):
                cmul(qr[:, n, :], qi[:, n, :], qr[:, n - 1, :], qi[:, n - 1, :], qr[:, n - 1, :], qi[:, n - 1, :],
                     t1[:, 0:G], t2[:, 0:G])
            chain(V.tensor_scalar(qi[:].rearrange("p n g -> p (n g)"), qi[:].rearrange("p n g -> p (n g)"),
                                  sign[:, 0:1], None, ALU.mult))
            chain(V.tensor_tensor(t1[:, 0:G], are[:], are[:], ALU.mult))
            chain(V.tensor_tensor(t2[:, 0:G], aim[:], aim[:], ALU.mult))
            chain(V.tensor_tensor(t1[:, 0:G], t1[:, 0:G], t2[:, 0:G], ALU.add))
            chain(V.reciprocal(t1[:, 0:G], t1[:, 0:G]))
            chain(V.tensor_tensor(t2[:, 0:G], are[:], t1[:, 0:G], ALU.mult))
            chain(V.scalar_tensor_tensor(t1[:, 0:G], aim[:], -1.0, t1[:, 0:G], ALU.mult, ALU.mult))
            chain(V.tensor_scalar(ex[:], pr[:, 1, :], 1.0, None, ALU.subtract))
            cmul(cr[:], ci[:], ex[:], pi[:, 1, :], t2[:, 0:G], t1[:, 0:G], en[:], en2[:])
            wide = [P, G, GH]
            crb, cib = cr[:].unsqueeze(2).to_broadcast(wide), ci[:].unsqueeze(2).to_broadcast(wide)
            chain(V.tensor_tensor(bb1[:], b1[:], crb, ALU.mult))
            chain(V.tensor_tensor(tb[:], b2[:], cib, ALU.mult))
            chain(V.tensor_tensor(bb1[:], bb1[:], tb[:], ALU.add))
            chain(V.tensor_tensor(bb2[:], b2[:], crb, ALU.mult))
            chain(V.tensor_tensor(tb[:], b1[:], cib, ALU.mult))
            chain(V.tensor_tensor(bb2[:], bb2[:], tb[:], ALU.subtract))
            for m in range(L):
                for out, n, x, xi in ((zz[:, :, m, :], L - 1 - m, bb1, bb2), (oo[:, :, m, :], m + 1, c1, c2)):
                    chain(V.tensor_tensor(out, x[:], pr[:, n, :].unsqueeze(2).to_broadcast(wide), ALU.mult))
                    chain(V.tensor_tensor(tb[:], xi[:], pi[:, n, :].unsqueeze(2).to_broadcast(wide), ALU.mult))
                    chain(V.tensor_tensor(out, out, tb[:], ALU.add))
            dve.sem_inc(coeffs, 1)
            dve.wait_ge(pads_set, 5)
            with dve.Fori(0, PAIRS) as i:
                for e in range(2):
                    bank[e][1].wait_full(dve, i, 1)
                    V.scalar_tensor_tensor(tg[e][:], idt[:], dskip[:, bass.ds(i * 2 + e, 1)],
                                           b[4 * e + 1][:, 0:3 * P], ALU.mult, ALU.add).then_inc(bank[e][1].free, 1)
                for e in range(2):
                    bank[e][2].wait_free(dve, i, 1)
                for n in range(LEVELS):
                    d = 1 << n
                    for e in range(2):
                        x, out = st[e][n % 2], st[e][(n + 1) % 2]
                        now = slice(PAD, PAD + CH)
                        before = slice(PAD - d, PAD + CH - d)
                        g = i * 2 + e
                        V.scalar_tensor_tensor(out[:, now], x[:, before], qr[:, n, bass.ds(g, 1)], x[:, now],
                                               ALU.mult, ALU.add).then_inc(half_sem[e], 1)
                    for e in range(2):
                        out = st[e][(n + 1) % 2]
                        g = i * 2 + e
                        bank[e][2].wait_full(dve, i, 1 + n)
                        dve.wait_ge(half_sem[e], i * LEVELS + n + 1)
                        V.scalar_tensor_tensor(out[:, PAD:PAD + CH], b[4 * e + 2][:, 0:CH], qi[:, n, bass.ds(g, 1)],
                                               out[:, PAD:PAD + CH], ALU.mult, ALU.add).then_inc(bank[e][2].free, 1)
                    for e in range(2):
                        bank[e][2].wait_free(dve, i, 2 + n)

        @block.tensor
        def _(pe):
            pe.wait_ge(coeffs, 1)
            with pe.Fori(0, PAIRS) as i:
                for e in range(2):
                    B0, B1, B2, B3 = b[4 * e:4 * e + 4]
                    pe.wait_ge(group_copied[e], 2 * (i + 1))
                    bank[e][0].wait_free(pe, i, 0)
                    for k in range(2):
                        for t in range(CT):
                            ins = nc.tensor.transpose(B0[:, (k * CT + t) * P:(k * CT + t + 1) * P],
                                                      ug[e][:, t, 8 * k:8 * k + 8, :], ident[:])
                    ins.then_inc(bank[e][0].full, 1)
                    bank[e][1].wait_free(pe, i, 0)
                    for k in range(2):
                        ins = nc.tensor.transpose(B1[:, k * P:(k + 1) * P], zg[e][:, 8 * k:8 * k + 8, :], ident[:])
                    ins.then_inc(bank[e][1].full, 1)
                for e in range(2):
                    B0, B1, B2, B3 = b[4 * e:4 * e + 4]
                    bank[e][0].wait_free(pe, i, 1)
                    bank[e][1].wait_free(pe, i, 1)
                    bank[e][2].wait_free(pe, i, 0)
                    for k in range(2):
                        ins = nc.tensor.matmul(B2[:, 0:CH], rg[e][:, k, :], uT[e][:, k, :], start=k == 0, stop=k == 1)
                    ins.then_inc(bank[e][2].full, 1)
                    for k in range(2):
                        for n in range(8 * k, L):
                            at = n * GH if k == 0 else 2 * P + (n - 8) * GH
                            m = L - 1 - n + 8 * k
                            ins = nc.tensor.matmul(B1[:, at:at + GH], zg[e][:, m:m + 8, :],
                                                   c1[:, bass.ds(i * 2 + e, 1), :].rearrange("p a h -> p (a h)"),
                                                   start=True, stop=True)
                    ins.then_inc(bank[e][1].full, 1)
                for n in range(LEVELS):
                    for e in range(2):
                        bank[e][2].wait_free(pe, i, 1 + n)
                        nc.tensor.matmul(b[4 * e + 2][:, 0:CH], swap[:], st[e][n % 2][:, PAD - (1 << n):PAD - (1 << n) + CH],
                                         start=True, stop=True).then_inc(bank[e][2].full, 1)
                for e in range(2):
                    bank[e][1].wait_free(pe, i + 1, 0)
                    bank[e][2].wait_free(pe, i + 1, 0)
                    out = b[4 * e]
                    for t in range(CT):
                        c = slice(t * P, (t + 1) * P)
                        nc.tensor.matmul(out[:, t * 2 * P:(t + 1) * 2 * P], uT[e][:, 0, c], tg[e][:, 0:2 * P],
                                         start=True, stop=False)
                        nc.tensor.matmul(out[:, t * 2 * P + P:(t + 1) * 2 * P], uT[e][:, 1, c], tg[e][:, 2 * P:3 * P],
                                         start=False, stop=False)
                        last = LEVELS % 2
                        ins = nc.tensor.matmul(out[:, t * 2 * P:(t + 1) * 2 * P],
                                               st[e][last][:, PAD - 1 + t * P:PAD - 1 + (t + 1) * P],
                                               oo[:, bass.ds(i * 2 + e, 1), :, :].rearrange("p a l h -> p (a l h)"),
                                               start=False, stop=True)
                    ins.then_inc(bank[e][0].full, 1)


def merge_and_route(nc, io, mix_dram, y_dram, x2_dram, xn_dram, logits):
    semaphores = []
    with ExitStack() as ctx:
        ctx.callback(end_phase, nc, semaphores)

        def sb(name, shape, dt=F32):
            return ctx.enter_context(nc.sbuf_tensor(name, shape, dt))

        def sem(name):
            semaphores.append(nc.alloc_semaphore(name=name))
            return semaphores[-1]

        R = NG + NE
        ident = sb("m_ident", [P, P])
        w_out = sb("w_out_sb", [P, KD, D])
        glu_w = sb("glu_w_sb", [P, 2, GW])
        glu_b = sb("glu_b_sb", [P, GW])
        w_r = sb("w_r_sb", [P, KD, R])
        b_r = sb("b_r_sb", [P, R])
        g_ffn = sb("m_g_ffn", [P, KD])
        minus_half, eps = sb("m_minus_half", [P, 1]), sb("m_eps", [P, 1])
        xb = [sb(f"m_x{j}", [P, D]) for j in range(2)]
        mix = [sb(f"m_mix{j}", [P, D]) for j in range(2)]
        yb = [sb(f"m_y{j}", [P, GW]) for j in range(2)]
        ysq, yin, yth, gy = sb("ysq", [P, GW]), sb("yin", [P, GW]), sb("yth", [P, GW]), sb("gy", [P, GW])
        gyT = sb("gyT", [P, 2, P])
        gate, gate_th = sb("gate", [P, GW]), sb("gate_th", [P, GW])
        mixT = sb("mixT", [P, KD, P])
        x2 = [sb(f"m_x2{j}", [P, D]) for j in range(2)]
        xn = [sb(f"m_xn{j}", [P, D]) for j in range(2)]
        sq = sb("m_sq", [P, D])
        ss, rs = sb("m_ss", [P, 1]), sb("m_rs", [P, 1])
        xnT = sb("xnT", [P, KD, P])

        b = [ctx.enter_context(nc.psum_tensor(f"m_bank{n}", [P, 512], F32)) for n in range(8)]
        uses = [1, 1, 1, 1, 2, 1, 1, 1]
        bank = [Bank(sem(f"m_full{n}"), sem(f"m_free{n}"), uses[n]) for n in range(8)]
        MIXT, PROD, GLU, LOGIT, XNT = 0, 2, 4, 5, 6

        consts_in, w_scaled, half_set = sem("m_consts_in"), sem("m_w_scaled"), sem("m_half_set")
        x_in = [sem(f"m_x_in{j}") for j in range(2)]
        mix_in = [sem(f"m_mix_in{j}") for j in range(2)]
        y_in = [sem(f"m_y_in{j}") for j in range(2)]
        x2_out = [sem(f"m_x2_out{j}") for j in range(2)]
        xn_out = [sem(f"m_xn_out{j}") for j in range(2)]
        ysq_ready, yin_ready, yth_ready, gy_ready = sem("ysq_ready"), sem("yin_ready"), sem("yth_ready"), sem("gy_ready")
        gate_ready, gate_th_ready, yb_ready = sem("gate_ready"), sem("gate_th_ready"), sem("yb_ready")
        x2_ready, sq_ready, rs_ready, xn_ready = sem("m_x2_ready"), sem("m_sq_ready"), sem("m_rs_ready"), sem("m_xn_ready")
        norm_chain = sem("m_norm_chain")

        LOADS = [(ident, io["ident"]), (w_out, io["w_out"]), (glu_w, io["glu_w"]), (glu_b, io["glu_b"]),
                 (w_r, io["w_r"]), (b_r, io["b_r"]), (g_ffn, io["g_ffn"])]
        ALL_IN = 16 * len(LOADS)
        tiled = lambda dram: dram.rearrange("(t p) d -> t p d", p=P)
        x_t, mix_t, y_t, x2_t, xn_t = map(tiled, (io["x"], mix_dram, y_dram, x2_dram, xn_dram))
        at = lambda dram, t: dram[bass.ds(t, 1)].rearrange("a p d -> (a p) d")

        def run_slots(engine, prologue, slot, epilogue):
            prologue()
            slot(0, 0, 0, False, True)
            with engine.Fori(0, TILES // 2 - 1) as i:
                slot(i * 2 + 1, 1, i, True, True)
                slot(i * 2 + 2, 0, i + 1, True, True)
            slot(TILES - 1, 1, TILES // 2 - 1, True, False)
            epilogue()

        nothing = lambda: None
        block = ctx.enter_context(nc.Block())

        @block.sync
        def _(sp):
            for dst, src in LOADS:
                sp.dma_start(dst[:], src).then_inc(consts_in, 16)

            def load(t, j):
                sp.wait_ge(x2_ready, t + 1)
                sp.dma_start(yb[j][:], at(y_t, t)).then_inc(y_in[j], 16)
                sp.dma_start(mix[j][:, 0:3 * GW], at(mix_t, t)).then_inc(mix_in[j], 16)
                sp.dma_start(xb[j][:], at(x_t, t)).then_inc(x_in[j], 16)

            def prologue():
                load(0, 0)
                load(1, 1)

            def slot(t, j, i, before, after):
                sp.wait_ge(x2_ready, t + 3)
                sp.dma_start(at(x2_t, t), x2[j][:]).then_inc(x2_out[j], 16)
                if not (isinstance(t, int) and t + 2 >= TILES):
                    load(t + 2, j)
                sp.wait_ge(xn_ready, t + 1)
                sp.dma_start(at(xn_t, t), xn[j][:]).then_inc(xn_out[j], 16)

            prologue()
            slot(0, 0, 0, False, True)
            with sp.Fori(0, TILES // 2 - 2) as i:
                slot(i * 2 + 1, 1, i, True, True)
                slot(i * 2 + 2, 0, i + 1, True, True)
            for t in range(TILES - 3, TILES):
                slot(t, t % 2, t // 2, True, True)
            for j in range(2):
                sp.wait_ge(x2_out[j], 16 * (TILES // 2 + 1))
                sp.wait_ge(xn_out[j], 16 * (TILES // 2 + 1))

        @block.gpsimd
        def _(pool):
            nchain = Chain(pool, norm_chain, 1)
            pool.sem_inc(x2_ready, 2)
            for j in range(2):
                pool.sem_inc(x2_out[j], 16)
                pool.sem_inc(xn_out[j], 16)
            nc.gpsimd.memset(minus_half[:], -0.5).then_inc(half_set, 1)
            nc.gpsimd.memset(eps[:], EPS).then_inc(half_set, 1)
            pool.wait_ge(half_set, 2)

            def slot(t, j, i, before, after):
                nchain.tile(t)
                if before:
                    pool.wait_ge(xn_ready, t)
                pool.wait_ge(sq_ready, t + 1)
                nchain(nc.gpsimd.tensor_tensor(rs[:], ss[:], eps[:], ALU.add))
                nc.gpsimd.tensor_tensor(rs[:], rs[:], minus_half[:], ALU.pow).then_inc(rs_ready, 1)

            run_slots(pool, nothing, slot, nothing)

        @block.scalar
        def _(act):
            act.wait_ge(consts_in, ALL_IN)

            def square(t, j, i):
                act.wait_ge(y_in[j], (i + 1) * 16)
                if not (isinstance(t, int) and t == 0):
                    act.wait_ge(yin_ready, t)
                nc.scalar.activation(ysq[:], yb[j][:], ACT.Square, scale=GELU_A ** 0.5).then_inc(ysq_ready, 1)

            def glu(t):
                act.wait_ge(yin_ready, t + 1)
                nc.scalar.activation(yth[:], yin[:], ACT.Tanh, scale=GELU_B).then_inc(yth_ready, 1)
                bank[GLU].wait_full(act, t, 0)
                nc.scalar.activation(gyT[:], b[GLU][:, 0:2 * P].rearrange("p (k n) -> p k n", k=2), ACT.Copy)\
                    .then_inc(bank[GLU].free, 1)
                act.wait_ge(gate_ready, t + 1)
                nc.scalar.activation(gate_th[:], gate[:], ACT.Tanh, scale=0.5).then_inc(gate_th_ready, 1)

            def route(t):
                bank[XNT].wait_full(act, t, 0)
                nc.scalar.activation(xnT[:, 0:4, :], b[XNT][:].rearrange("p (k n) -> p k n", k=4), ACT.Copy)\
                    .then_inc(bank[XNT].free, 1)

            def slot(t, j, i, before, after):
                if after:
                    square(t + 1, 1 - j, i + j)
                bank[MIXT].wait_full(act, t, 0)
                nc.scalar.activation(mixT[:, 0:4, :], b[MIXT][:].rearrange("p (k n) -> p k n", k=4), ACT.Copy)\
                    .then_inc(bank[MIXT].free, 1)
                if before:
                    route(t - 1)
                if after:
                    glu(t + 1)
                act.wait_ge(x2_ready, t + 3)
                nc.scalar.activation(sq[:], x2[j][:], ACT.Square, scale=D ** -0.5, accum_out=ss[:]).then_inc(sq_ready, 1)
                act.wait_ge(xn_out[j], (i + 1) * 16)
                act.wait_ge(rs_ready, t + 1)
                nc.scalar.activation(xn[j][:], x2[j][:], ACT.Copy, scale=rs[:, 0:1]).then_inc(xn_ready, 1)

            def prologue():
                square(0, 0, 0)
                glu(0)

            run_slots(act, prologue, slot, lambda: route(TILES - 1))

        @block.vector
        def _(dve):
            V = nc.vector
            for k in bank:
                dve.sem_inc(k.free, 1)
            dve.wait_ge(consts_in, ALL_IN)
            for k, factor in ((2, 0.5), (4, 0.5), (6, 0.25)):
                V.tensor_scalar(w_out[:, k:k + 2, :], w_out[:, k:k + 2, :], factor, None, ALU.mult).then_inc(w_scaled, 1)
            V.tensor_tensor(w_r[:], w_r[:], bc(g_ffn[:], R), ALU.mult).then_inc(w_scaled, 1)

            def glu(t, j):
                dve.wait_ge(ysq_ready, t + 1)
                V.scalar_tensor_tensor(yin[:], ysq[:], 1.0, yb[j][:], ALU.add, ALU.mult).then_inc(yin_ready, 1)
                dve.wait_ge(yth_ready, t + 1)
                V.scalar_tensor_tensor(gy[:], yth[:], 1.0, yb[j][:], ALU.add, ALU.mult).then_inc(gy_ready, 1)
                dve.wait_ge(gy_ready, t + 1)
                bank[GLU].wait_full(dve, t, 1)
                V.scalar_tensor_tensor(gate[:], b[GLU][:, 0:GW], 0.5, glu_b[:], ALU.mult, ALU.add)\
                    .then_inc(bank[GLU].free, 1)
                bank[GLU].wait_free(dve, t + 1, 0)
                dve.sem_inc(gate_ready, 1)
                dve.wait_ge(gate_th_ready, t + 1)
                V.scalar_tensor_tensor(mix[j][:, 3 * GW:D], gate_th[:], 1.0, gy[:], ALU.add, ALU.mult)\
                    .then_inc(yb_ready, 1)

            def route(t):
                bank[XNT + 1].wait_full(dve, t, 0)
                V.tensor_copy(xnT[:, 4:8, :], b[XNT + 1][:].rearrange("p (k n) -> p k n", k=4))\
                    .then_inc(bank[XNT + 1].free, 1)

            def logit(t):
                bank[LOGIT].wait_full(dve, t, 0)
                V.tensor_tensor(logits[:, bass.ds(t, 1), :].rearrange("p a r -> p (a r)"), b[LOGIT][:, 0:R], b_r[:],
                                ALU.add).then_inc(bank[LOGIT].free, 1)

            def slot(t, j, i, before, after):
                bank[MIXT + 1].wait_full(dve, t, 0)
                V.tensor_copy(mixT[:, 4:8, :], b[MIXT + 1][:].rearrange("p (k n) -> p k n", k=4))\
                    .then_inc(bank[MIXT + 1].free, 1)
                if before:
                    route(t - 1)
                if after:
                    glu(t + 1, 1 - j)
                dve.wait_ge(x_in[j], (i + 1) * 16)
                dve.wait_ge(x2_out[j], (i + 1) * 16)
                for n in range(2):
                    bank[PROD + n].wait_full(dve, t, 0)
                    V.tensor_tensor(x2[j][:, n * 512:(n + 1) * 512], b[PROD + n][:], xb[j][:, n * 512:(n + 1) * 512],
                                    ALU.add).then_inc(bank[PROD + n].free, 1)
                for n in range(2):
                    bank[PROD + n].wait_free(dve, t + 1, 0)
                dve.sem_inc(x2_ready, 1)
                if before:
                    logit(t - 1)

            def epilogue():
                route(TILES - 1)
                logit(TILES - 1)

            run_slots(dve, lambda: glu(0, 0), slot, epilogue)

        @block.tensor
        def _(pe):
            pe.wait_ge(consts_in, ALL_IN)
            pe.wait_ge(w_scaled, 4)

            def glu_transpose(t):
                pe.wait_ge(gy_ready, t + 1)
                bank[GLU].wait_free(pe, t, 0)
                for c in range(2):
                    ins = nc.tensor.transpose(b[GLU][:, c * P:(c + 1) * P], gy[:, c * P:(c + 1) * P], ident[:])
                ins.then_inc(bank[GLU].full, 1)

            def glu_product(t):
                bank[GLU].wait_free(pe, t, 1)
                for c in range(2):
                    ins = nc.tensor.matmul(b[GLU][:, 0:GW], gyT[:, c, :], glu_w[:, c, :], start=c == 0, stop=c == 1)
                ins.then_inc(bank[GLU].full, 1)

            def xn_transpose(t, j):
                pe.wait_ge(xn_ready, t + 1)
                for k in range(2):
                    bank[XNT + k].wait_free(pe, t, 0)
                    for c in range(4):
                        ins = nc.tensor.transpose(b[XNT + k][:, c * P:(c + 1) * P],
                                                  xn[j][:, (4 * k + c) * P:(4 * k + c + 1) * P], ident[:])
                    ins.then_inc(bank[XNT + k].full, 1)

            def route(t):
                bank[XNT].wait_free(pe, t + 1, 0)
                bank[XNT + 1].wait_free(pe, t + 1, 0)
                bank[LOGIT].wait_free(pe, t, 0)
                for k in range(KD):
                    ins = nc.tensor.matmul(b[LOGIT][:, 0:R], xnT[:, k, :], w_r[:, k, :], start=k == 0, stop=k == KD - 1)
                ins.then_inc(bank[LOGIT].full, 1)

            def product(t, n):
                bank[PROD + n].wait_free(pe, t, 0)
                for k in range(KD):
                    ins = nc.tensor.matmul(b[PROD + n][:], mixT[:, k, :], w_out[:, k, n * 512:(n + 1) * 512],
                                           start=k == 0, stop=k == KD - 1)
                ins.then_inc(bank[PROD + n].full, 1)

            def slot(t, j, i, before, after):
                pe.wait_ge(yb_ready, t + 1)
                pe.wait_ge(mix_in[j], (i + 1) * 16)
                for k in range(2):
                    bank[MIXT + k].wait_free(pe, t, 0)
                    for c in range(4):
                        ins = nc.tensor.transpose(b[MIXT + k][:, c * P:(c + 1) * P],
                                                  mix[j][:, (4 * k + c) * P:(4 * k + c + 1) * P], ident[:])
                    ins.then_inc(bank[MIXT + k].full, 1)
                if before:
                    xn_transpose(t - 1, 1 - j)
                if after:
                    glu_transpose(t + 1)
                bank[MIXT].wait_free(pe, t + 1, 0)
                bank[MIXT + 1].wait_free(pe, t + 1, 0)
                product(t, 0)
                if after:
                    glu_product(t + 1)
                product(t, 1)
                if before:
                    route(t - 1)

            def prologue():
                glu_transpose(0)
                glu_product(0)

            def epilogue():
                xn_transpose(TILES - 1, 1)
                route(TILES - 1)

            run_slots(pe, prologue, slot, epilogue)


def plan_experts(nc, io, logits, wts, dest, block_rows, block_expert, block_side, expert_end, table_dram):
    semaphores = []
    with ExitStack() as ctx:
        ctx.callback(end_phase, nc, semaphores)

        def sb(name, shape, dt=F32):
            return ctx.enter_context(nc.sbuf_tensor(name, shape, dt))

        def sem(name):
            semaphores.append(nc.alloc_semaphore(name=name))
            return semaphores[-1]

        T = TILES
        before = sb("p_before", [P, P])
        ones = sb("p_ones", [P, P])
        reset = sb("p_reset", [P, NE * T])
        rank4, rank8 = sb("rank4", [P, NG]), sb("rank8", [P, NE_G])
        block_no = sb("block_no", [1, BLOCKS])
        gm, mv, sh = sb("p_gm", [P, T]), sb("p_mv", [P, T]), sb("p_sh", [P, T, NG])
        ohg, vg = sb("ohg", [P, T, NG]), sb("vg", [P, T, NG])
        eg, pg = sb("eg", [P, T, NG]), sb("pg", [P, T])
        big = sb("p_big", [P, T, NG, NE_G])
        ein, v8 = sb("ein", [P, T, NE_G]), sb("v8", [P, T, NE_G])
        m1, m2 = sb("m1", [P, T]), sb("m2", [P, T])
        oh1, oh2 = sb("oh1", [P, T, NE_G]), sb("oh2", [P, T, NE_G])
        dl, el = sb("p_dl", [P, T]), sb("p_el", [P, T])
        pair = [sb(f"pair{k}", [P, T, NG, NE_G]) for k in range(2)]
        both = sb("p_both", [P, T * NE])
        tot, incl, base = sb("p_tot", [P, NE, T]), sb("p_incl", [P, NE, T]), sb("p_base", [P, NE, T])
        row = sb("p_row", [P, T, NE])
        nb, ni, endb, startr = sb("p_nb", [P, NE]), sb("p_ni", [P, NE], I32), sb("p_endb", [P, NE]), sb("p_startr", [P, NE])
        drow = sb("p_drow", [P, 2, T])
        dlow, dhigh = sb("p_dlow", [P, 2, T], I32), sb("p_dhigh", [P, 2, T], I32)
        flow, fhigh = sb("p_flow", [P, 2, T]), sb("p_fhigh", [P, 2, T])
        place = sb("p_place", [P, 2, T], I32)
        token = sb("p_token", [P, T], I32)
        zero = sb("p_zero", [P, BLOCKS], I32)
        cmp = sb("p_cmp", [1, BLOCKS, NE])
        bexp = sb("p_bexp", [1, BLOCKS])

        b = [ctx.enter_context(nc.psum_tensor(f"p_bank{n}", [P, 512], F32)) for n in range(4)]
        consts_in, shifted, e_done, d_ready, el_ready = (sem(n) for n in ("p_consts_in", "shifted", "e_done", "d_ready",
                                                                          "el_ready"))
        both_ready, counted, place_ready, ids_set, table_zero, table_set, rows_in, zero_set = (
            sem(n) for n in ("both_ready", "counted", "place_ready", "ids_set", "table_zero", "table_set", "rows_in",
                             "zero_set"))
        chain_sem = sem("p_dve_chain")
        LOADS = [(before, io["before"]), (ones, io["ones"]), (reset, io["reset"]), (rank4, io["rank4"]),
                 (rank8, io["rank8"]), (block_no, io["block_no"])]
        over = lambda ap, n: ap.unsqueeze(1).to_broadcast([P, T, n])

        block = ctx.enter_context(nc.Block())

        @block.sync
        def _(sp):
            for dst, src in LOADS:
                sp.dma_start(dst[:], src).then_inc(consts_in, 16)
            sp.wait_ge(zero_set, 1)
            sp.dma_start(table_dram.rearrange("(p s) a -> p (s a)", p=P), zero[:]).then_inc(table_zero, 16)
            sp.wait_ge(table_set, 16 * 2 * T)
            sp.dma_start(block_rows[:], table_dram.rearrange("(p s) a -> p (s a)", p=P)).then_inc(rows_in, 16)
            sp.wait_ge(rows_in, 16)

        @block.gpsimd
        def _(pool):
            nc.gpsimd.memset(zero[:], 0).then_inc(zero_set, 1)
            nc.gpsimd.iota(token[:], [[P, T]], base=0, channel_multiplier=1).then_inc(ids_set, 1)
            pool.wait_ge(ids_set, 1)
            pool.wait_ge(table_zero, 16)
            pool.wait_ge(place_ready, 1)
            for t in range(T):
                for k in range(2):
                    pool.indirect_dma_start(out=table_dram, out_offset=bass.IndirectOffsetOnAxis(ap=place[:, k, t:t + 1], axis=0),
                                            in_=token[:, t:t + 1], in_offset=None).then_inc(table_set, 16)
            pool.wait_ge(table_set, 16 * 2 * T)

        @block.scalar
        def _(act):
            act.wait_ge(shifted, 1)
            nc.scalar.activation(eg[:], sh[:], ACT.Exp).then_inc(e_done, 1)
            act.wait_ge(d_ready, 1)
            nc.scalar.activation(el[:], dl[:], ACT.Exp).then_inc(el_ready, 1)

        @block.tensor
        def _(pe):
            pe.wait_ge(consts_in, 16 * len(LOADS))
            pe.wait_ge(both_ready, 1)
            for n in range(2):
                nc.tensor.matmul(b[n][:], before[:], both[:, n * 512:(n + 1) * 512], start=True, stop=True)
            for n in range(2):
                ins = nc.tensor.matmul(b[2 + n][:], ones[:], both[:, n * 512:(n + 1) * 512], start=True, stop=True)
            ins.then_inc(counted, 1)

        @block.vector
        def _(dve):
            V = nc.vector
            chain = Chain(dve, chain_sem)
            lg = logits[:, :, 0:NG]
            le = logits[:, :, NG:NG + NE].rearrange("p t (g e) -> p t g e", g=NG)
            dve.wait_ge(consts_in, 16 * len(LOADS))

            def first_max(out, x, largest, ranks, scratch, n):
                chain(V.tensor_reduce(largest, x, AX.X, ALU.max))
                chain(V.tensor_tensor(scratch, x, bc(largest, n), ALU.is_equal))
                chain(V.tensor_tensor(scratch, scratch, over(ranks[:], n), ALU.mult))
                chain(V.tensor_reduce(mv[:], scratch, AX.X, ALU.max))
                chain(V.tensor_tensor(out, scratch, bc(mv[:], n), ALU.is_equal))

            first_max(ohg[:], lg, gm[:], rank4, vg[:], NG)
            V.tensor_tensor(sh[:], lg, bc(gm[:], NG), ALU.subtract).then_inc(shifted, 1)
            chosen = ohg[:].unsqueeze(3).to_broadcast([P, T, NG, NE_G])
            chain(V.tensor_tensor(big[:], le, chosen, ALU.mult))
            chain(V.tensor_reduce(ein[:], big[:].rearrange("p t g e -> p t e g"), AX.X, ALU.add))
            first_max(oh1[:], ein[:], m1[:], rank8, v8[:], NE_G)
            chain(V.scalar_tensor_tensor(ein[:], oh1[:], -1e30, ein[:], ALU.mult, ALU.add))
            first_max(oh2[:], ein[:], m2[:], rank8, v8[:], NE_G)
            V.tensor_tensor(dl[:], m2[:], m1[:], ALU.subtract).then_inc(d_ready, 1)
            for k, oh in enumerate((oh1, oh2)):
                chain(V.tensor_tensor(pair[k][:], chosen, oh[:].unsqueeze(2).to_broadcast([P, T, NG, NE_G]), ALU.mult))
            V.tensor_tensor(both[:], pair[0][:].rearrange("p t g e -> p (t g e)"),
                            pair[1][:].rearrange("p t g e -> p (t g e)"), ALU.add).then_inc(both_ready, 1)
            dve.wait_ge(e_done, 1)
            chain(V.tensor_reduce(pg[:], eg[:], AX.X, ALU.add))
            chain(V.reciprocal(pg[:], pg[:]))
            dve.wait_ge(el_ready, 1)
            chain(V.tensor_scalar(dl[:], el[:], 1.0, None, ALU.add))
            chain(V.reciprocal(dl[:], dl[:]))
            chain(V.tensor_tensor(wts[:, 0, :], dl[:], pg[:], ALU.mult))
            chain(V.tensor_tensor(wts[:, 1, :], wts[:, 0, :], el[:], ALU.mult))
            dve.wait_ge(counted, 1)
            for n in range(2):
                chain(V.tensor_copy(tot[:, :, n * 16:(n + 1) * 16], b[2 + n][:].rearrange("p (t e) -> p e t", e=NE)))
            flat = lambda ap: ap.rearrange("p e t -> p (e t)")
            chain(V.tensor_tensor_scan(flat(incl[:]), reset[:], flat(tot[:]), 0.0, ALU.mult, ALU.add))
            chain(V.tensor_scalar(nb[:], incl[:, :, T - 1], float(P - 1), None, ALU.add))
            chain(V.tensor_copy(ni[:], nb[:]))
            chain(V.tensor_scalar(ni[:], ni[:], 7, None, ALU.arith_shift_right))
            chain(V.tensor_copy(nb[:], ni[:]))
            chain(V.tensor_tensor_scan(endb[:], ones[:, 0:NE], nb[:], 0.0, ALU.mult, ALU.add))
            chain(V.tensor_tensor(startr[:], endb[:], nb[:], ALU.subtract))
            chain(V.tensor_tensor(base[:], incl[:], tot[:], ALU.subtract))
            chain(V.tensor_scalar(startr[:], startr[:], float(P), None, ALU.mult))
            chain(V.tensor_tensor(base[:], base[:], bc(startr[:], T), ALU.add))
            for n in range(2):
                tiles = slice(n * 16, (n + 1) * 16)
                chain(V.tensor_tensor(row[:, tiles, :], b[n][:].rearrange("p (t e) -> p t e", e=NE),
                                      base[:, :, tiles].rearrange("p e t -> p t e"), ALU.add))
            for k in range(2):
                chain(V.tensor_tensor(pair[k][:].rearrange("p t g e -> p t (g e)"),
                                      pair[k][:].rearrange("p t g e -> p t (g e)"), row[:], ALU.mult))
                chain(V.tensor_reduce(drow[:, k, :], pair[k][:].rearrange("p t g e -> p t (g e)"), AX.X, ALU.add))
            chain(V.tensor_copy(dest[:], drow[:]))
            chain(V.tensor_scalar(dlow[:], dest[:], P - 1, None, ALU.bitwise_and))
            chain(V.tensor_scalar(dhigh[:], dest[:], 7, None, ALU.arith_shift_right))
            chain(V.tensor_copy(flow[:], dlow[:]))
            chain(V.tensor_copy(fhigh[:], dhigh[:]))
            chain(V.scalar_tensor_tensor(flow[:], flow[:], float(BLOCKS), fhigh[:], ALU.mult, ALU.add))
            V.tensor_copy(place[:], flow[:]).then_inc(place_ready, 1)
            wide = [1, BLOCKS, NE]
            chain(V.tensor_tensor(cmp[:], block_no[:].unsqueeze(2).to_broadcast(wide),
                                  endb[0:1, :].unsqueeze(1).to_broadcast(wide), ALU.is_ge))
            chain(V.tensor_reduce(bexp[:], cmp[:], AX.X, ALU.add))
            chain(V.tensor_scalar(bexp[:], bexp[:], float(NE - 1), None, ALU.min))
            chain(V.tensor_copy(block_expert[:], bexp[:]))
            chain(V.tensor_scalar(block_side[:], block_expert[:], 1, None, ALU.bitwise_and))
            chain(V.tensor_scalar(nb[:], endb[:], 1.0, None, ALU.add))
            chain(V.tensor_copy(expert_end[:], nb[0:1, :]))


def run_experts(nc, io, block_rows, block_expert, block_side, expert_end, xn_dram, out_dram):
    semaphores = []
    with ExitStack() as ctx:
        ctx.callback(end_phase, nc, semaphores)

        def sb(name, shape, dt=F32):
            return ctx.enter_context(nc.sbuf_tensor(name, shape, dt))

        def sem(name):
            semaphores.append(nc.alloc_semaphore(name=name))
            return semaphores[-1]

        ident = sb("e_ident", [P, P])
        g_ffn = sb("e_g_ffn", [P, KD])
        wg = sb("wg", [P, 2 * KD, FE])
        wu = sb("wu", [P, 2 * KD, FE])
        wd = sb("wd", [P, 2 * KF, D])
        icol = [sb(f"icol{j}", [P, 1], I32) for j in range(2)]
        xg = [sb(f"xg{j}", [P, D]) for j in range(2)]
        xT = [sb(f"e_xT{j}", [P, KD, P]) for j in range(2)]
        sg = sb("sg", [P, FE])
        hh = [sb(f"hh{j}", [P, FE]) for j in range(2)]
        hT = sb("hT", [P, KF, P])
        ys = [sb(f"ys{j}", [P, D]) for j in range(2)]

        b = [ctx.enter_context(nc.psum_tensor(f"e_bank{n}", [P, 512], F32)) for n in range(7)]
        GATE, UP, HT, XT, DOWN = 0, 1, 2, 3, 5
        bank = [Bank(sem(f"e_full{n}"), sem(f"e_free{n}"), 1) for n in range(7)]
        consts_in = sem("e_consts_in")
        w_in = [sem(f"e_w_in{j}") for j in range(2)]
        experts_in = sem("experts_in")
        blocks_done = sem("blocks_done")
        icol_ready, pool_passed = sem("icol_ready"), sem("e_pool_passed")
        x_in = [sem(f"e_x_in{j}") for j in range(2)]
        sg_ready, hh_ready = sem("sg_ready"), sem("hh_ready")
        y_out = [sem(f"e_y_out{j}") for j in range(2)]
        out_b = out_dram.rearrange("(s p) d -> s p d", p=P)

        def run_slots(engine, prologue, slot, epilogue):
            prologue()
            slot(0, 0, 0, False, True, True)
            with engine.Fori(0, (BLOCKS - 3) // 2) as i:
                slot(i * 2 + 1, 1, i, True, True, True)
                slot(i * 2 + 2, 0, i + 1, True, True, True)
            slot(BLOCKS - 2, (BLOCKS - 2) % 2, (BLOCKS - 2) // 2, True, True, False)
            slot(BLOCKS - 1, (BLOCKS - 1) % 2, (BLOCKS - 1) // 2, True, False, False)
            epilogue()

        assert BLOCKS % 2 == 1
        nothing = lambda: None
        block = ctx.enter_context(nc.Block())

        @block.sync
        def _(sp):
            sp.dma_start(ident[:], io["ident"]).then_inc(consts_in, 16)
            sp.dma_start(g_ffn[:], io["g_ffn"]).then_inc(consts_in, 16)

            def load(e, j):
                gate = io["w_gate"][bass.ds(e, 1)].rearrange("a (k p) f -> p (a k) f", p=P)
                up = io["w_up"][bass.ds(e, 1)].rearrange("a (k p) f -> p (a k) f", p=P)
                down = io["w_down"][bass.ds(e, 1)].rearrange("a (k p) f -> p (a k) f", p=P)
                sp.dma_start(wg[:, j * KD:(j + 1) * KD, :], gate).then_inc(w_in[j], 16)
                sp.dma_start(wu[:, j * KD:(j + 1) * KD, :], up).then_inc(w_in[j], 16)
                sp.dma_start(wd[:, j * KF:(j + 1) * KF, :], down).then_inc(w_in[j], 16)

            def announce(j, i):
                sp.wait_ge(w_in[j], (i + 1) * 48)
                sp.sem_inc(experts_in, 1)

            load(0, 0)
            load(1, 1)
            announce(0, 0)
            with sp.Fori(1, NE // 2) as i:
                for j in range(2):
                    announce(1 - j, i - 1 + j)
                    end = sp.value_load(expert_end[0:1, bass.ds(i * 2 + j - 2, 1)], min_val=1, max_val=BLOCKS + 1)
                    sp.wait_ge(blocks_done, end)
                    load(i * 2 + j, j)
            announce(1, NE // 2 - 1)

        @block.gpsimd
        def _(pool):
            for j in range(2):
                pool.sem_inc(y_out[j], 16)

            def gather(s, j):
                if not (isinstance(s, int) and s < 2):
                    bank[XT + 1].wait_full(pool, s - 2, 0)
                    pass_wait(pool, pool_passed)
                nc.gpsimd.tensor_copy(icol[j][:], block_rows[:, bass.ds(s, 1)]).then_inc(icol_ready, 1)
                pool.wait_ge(icol_ready, s + 1)
                pass_wait(pool, pool_passed)
                pool.indirect_dma_start(out=xg[j][:], out_offset=None, in_=xn_dram,
                                        in_offset=bass.IndirectOffsetOnAxis(ap=icol[j][:, 0:1], axis=0))\
                    .then_inc(x_in[j], 16)

            def slot(s, j, i, before, after, after2):
                if after2:
                    gather(s + 2, j)

            def prologue():
                gather(0, 0)
                gather(1, 1)

            run_slots(pool, prologue, slot, nothing)

        @block.scalar
        def _(act):
            def slot(s, j, i, before, after, after2):
                bank[GATE].wait_full(act, s, 0)
                if not (isinstance(s, int) and s == 0):
                    act.wait_ge(hh_ready, s)
                nc.scalar.activation(sg[:], b[GATE][:], ACT.Silu).then_inc(bank[GATE].free, 1)
                bank[GATE].wait_free(act, s + 1, 0)
                act.sem_inc(sg_ready, 1)
                if before:
                    down_h(s - 1)
                    down_y(s - 1, 1 - j, i - 1 + j)

            def down_h(s):
                bank[HT].wait_full(act, s, 0)
                nc.scalar.activation(hT[:], b[HT][:].rearrange("p (k n) -> p k n", k=KF), ACT.Copy)\
                    .then_inc(bank[HT].free, 1)

            def down_y(s, j, i):
                act.wait_ge(y_out[j], (i + 1) * 16)
                for n in range(2):
                    bank[DOWN + n].wait_full(act, s, 0)
                    nc.scalar.activation(ys[j][:, n * 512:(n + 1) * 512], b[DOWN + n][:], ACT.Copy)\
                        .then_inc(bank[DOWN + n].free, 1)
                for n in range(2):
                    bank[DOWN + n].wait_free(act, s + 1, 0)
                act.dma_start(out_b[bass.ds(s, 1)].rearrange("a p d -> (a p) d"), ys[j][:]).then_inc(y_out[j], 16)

            def epilogue():
                s = BLOCKS - 1
                down_h(s)
                down_y(s, s % 2, s // 2)

            run_slots(act, nothing, slot, epilogue)
            act.wait_ge(y_out[0], 16 * ((BLOCKS + 1) // 2 + 1))
            act.wait_ge(y_out[1], 16 * (BLOCKS // 2 + 1))

        @block.vector
        def _(dve):
            V = nc.vector
            for k in bank:
                dve.sem_inc(k.free, 1)
            dve.sem_inc(blocks_done, 1)
            dve.wait_ge(consts_in, 32)

            def evac_xT(s, j):
                for k in range(2):
                    bank[XT + k].wait_full(dve, s, 0)
                    V.tensor_tensor(xT[j][:, 4 * k:4 * k + 4, :], b[XT + k][:].rearrange("p (k n) -> p k n", k=4),
                                    bc(g_ffn[:, 4 * k:4 * k + 4], P), ALU.mult).then_inc(bank[XT + k].free, 1)

            def slot(s, j, i, before, after, after2):
                dve.wait_ge(sg_ready, s + 1)
                bank[UP].wait_full(dve, s, 0)
                V.tensor_tensor(hh[j][:], b[UP][:], sg[:], ALU.mult).then_inc(bank[UP].free, 1)
                bank[UP].wait_free(dve, s + 1, 0)
                dve.sem_inc(hh_ready, 1)
                if after:
                    evac_xT(s + 1, 1 - j)

            run_slots(dve, lambda: evac_xT(0, 0), slot, nothing)

        @block.tensor
        def _(pe):
            pe.wait_ge(consts_in, 32)

            def transpose_x(s, j, i):
                pe.wait_ge(x_in[j], (i + 1) * 16)
                for k in range(2):
                    bank[XT + k].wait_free(pe, s, 0)
                    for c in range(4):
                        ins = nc.tensor.transpose(b[XT + k][:, c * P:(c + 1) * P],
                                                  xg[j][:, (4 * k + c) * P:(4 * k + c + 1) * P], ident[:])
                    ins.then_inc(bank[XT + k].full, 1)

            def first(s, j, w, which, side):
                bank[which].wait_free(pe, s, 0)
                for k in range(KD):
                    ins = nc.tensor.matmul(b[which][:], xT[j][:, k, :],
                                           w[:, bass.ds(side * KD + k, 1), :].rearrange("p a f -> p (a f)"),
                                           start=k == 0, stop=k == KD - 1)
                ins.then_inc(bank[which].full, 1)

            def transpose_h(s, j):
                pe.wait_ge(hh_ready, s + 1)
                bank[HT].wait_free(pe, s, 0)
                for k in range(KF):
                    ins = nc.tensor.transpose(b[HT][:, k * P:(k + 1) * P], hh[j][:, k * P:(k + 1) * P], ident[:])
                ins.then_inc(bank[HT].full, 1)

            def down(s):
                side = pe.value_load(block_side[0:1, bass.ds(s, 1)], min_val=0, max_val=1)
                bank[HT].wait_free(pe, s + 1, 0)
                for n in range(2):
                    bank[DOWN + n].wait_free(pe, s, 0)
                    for k in range(KF):
                        ins = nc.tensor.matmul(b[DOWN + n][:], hT[:, k, :],
                                               wd[:, bass.ds(side * KF + k, 1), n * 512:(n + 1) * 512]
                                               .rearrange("p a f -> p (a f)"), start=k == 0, stop=k == KF - 1)
                    ins.then_inc(bank[DOWN + n].full, 1)
                bank[DOWN + 1].wait_full(pe, s, 0)
                pe.sem_inc(blocks_done, 1)

            def slot(s, j, i, before, after, after2):
                expert = pe.value_load(block_expert[0:1, bass.ds(s, 1)], min_val=0, max_val=NE - 1)
                side = pe.value_load(block_side[0:1, bass.ds(s, 1)], min_val=0, max_val=1)
                pe.wait_ge(experts_in, expert + 1)
                for k in range(2):
                    bank[XT + k].wait_free(pe, s + 1, 0)
                first(s, j, wg, GATE, side)
                if before:
                    transpose_h(s - 1, 1 - j)
                first(s, j, wu, UP, side)
                if after:
                    transpose_x(s + 1, 1 - j, i + j)
                if before:
                    down(s - 1)

            def epilogue():
                s = BLOCKS - 1
                transpose_h(s, s % 2)
                down(s)

            run_slots(pe, lambda: transpose_x(0, 0, 0), slot, epilogue)


def combine(nc, io, wts, dest, x2_dram, experts_dram, out_dram):
    semaphores = []
    with ExitStack() as ctx:
        ctx.callback(end_phase, nc, semaphores)

        def sb(name, shape, dt=F32):
            return ctx.enter_context(nc.sbuf_tensor(name, shape, dt))

        def sem(name):
            semaphores.append(nc.alloc_semaphore(name=name))
            return semaphores[-1]

        g_fin = sb("g_fin_sb", [P, D])
        minus_half, eps = sb("f_minus_half", [P, 1]), sb("f_eps", [P, 1])
        icol = [[sb(f"f_icol{j}{k}", [P, 1], I32) for k in range(2)] for j in range(2)]
        ye = [[sb(f"f_y{j}{k}", [P, D]) for k in range(2)] for j in range(2)]
        xb = [sb(f"f_x{j}", [P, D]) for j in range(2)]
        acc = [sb(f"f_acc{j}", [P, D]) for j in range(2)]
        sq = sb("f_sq", [P, D])
        ss, rs = [sb(f"f_ss{j}", [P, 1]) for j in range(2)], [sb(f"f_rs{j}", [P, 1]) for j in range(2)]
        ot = [sb(f"f_out{j}", [P, D]) for j in range(2)]
        consts_in, half_set, icol_ready = sem("f_consts_in"), sem("f_half_set"), sem("f_icol_ready")
        pool_passed = sem("f_pool_passed")
        y_in = [[sem(f"f_y_in{j}{k}") for k in range(2)] for j in range(2)]
        x_in = [sem(f"f_x_in{j}") for j in range(2)]
        acc_ready, sq_ready, rs_ready, out_ready = (sem(n) for n in ("acc_ready", "f_sq_ready", "f_rs_ready", "out_ready"))
        stored = [sem(f"f_stored{j}") for j in range(2)]
        acc_chain, rs_chain = sem("acc_chain"), sem("rs_chain")
        x_t = x2_dram.rearrange("(t p) d -> t p d", p=P)
        o_t = out_dram.rearrange("(t p) d -> t p d", p=P)
        at = lambda dram, t: dram[bass.ds(t, 1)].rearrange("a p d -> (a p) d")
        block = ctx.enter_context(nc.Block())

        @block.sync
        def _(sp):
            sp.dma_start(g_fin[:], io["g_fin"]).then_inc(consts_in, 16)
            for j in range(2):
                sp.sem_inc(stored[j], 16)
            with sp.Fori(0, TILES // 2) as i:
                for j in range(2):
                    t = i * 2 + j
                    sp.wait_ge(acc_ready, t + 1)
                    sp.dma_start(xb[j][:], at(x_t, t)).then_inc(x_in[j], 16)

        @block.gpsimd
        def _(pool):
            pool.sem_inc(acc_ready, 2)
            nc.gpsimd.memset(minus_half[:], -0.5).then_inc(half_set, 1)
            nc.gpsimd.memset(eps[:], EPS).then_inc(half_set, 1)
            pool.wait_ge(half_set, 2)
            chain = Chain(pool, rs_chain, 1)

            def gather(t, j):
                pool.wait_ge(acc_ready, t + 1)
                pass_wait(pool, pool_passed)
                for k in range(2):
                    nc.gpsimd.tensor_copy(icol[j][k][:], dest[:, k, bass.ds(t, 1)]).then_inc(icol_ready, 1)
                pool.wait_ge(icol_ready, (t + 1) * 2)
                pass_wait(pool, pool_passed)
                for k in range(2):
                    pool.indirect_dma_start(out=ye[j][k][:], out_offset=None, in_=experts_dram,
                                            in_offset=bass.IndirectOffsetOnAxis(ap=icol[j][k][:, 0:1], axis=0))\
                        .then_inc(y_in[j][k], 16)

            def root(t, j):
                chain.tile(t)
                pool.wait_ge(sq_ready, t + 1)
                chain(nc.gpsimd.tensor_tensor(rs[j][:], ss[j][:], eps[:], ALU.add))
                nc.gpsimd.tensor_tensor(rs[j][:], rs[j][:], minus_half[:], ALU.pow).then_inc(rs_ready, 1)

            gather(0, 0)
            gather(1, 1)
            with pool.Fori(0, TILES // 2 - 1) as i:
                for j in range(2):
                    gather(i * 2 + j + 2, j)
                    root(i * 2 + j, j)
            for t in range(TILES - 2, TILES):
                root(t, t % 2)

        @block.scalar
        def _(act):
            with act.Fori(0, TILES // 2) as i:
                for j in range(2):
                    t = i * 2 + j
                    act.wait_ge(acc_ready, t + 3)
                    nc.scalar.activation(sq[:], acc[j][:], ACT.Square, scale=D ** -0.5, accum_out=ss[j][:])\
                        .then_inc(sq_ready, 1)
                    act.wait_ge(out_ready, t + 3)
                    act.dma_start(at(o_t, t), ot[j][:]).then_inc(stored[j], 16)
            for j in range(2):
                act.wait_ge(stored[j], 16 * (TILES // 2 + 1))

        @block.vector
        def _(dve):
            V = nc.vector
            dve.sem_inc(out_ready, 2)
            dve.wait_ge(consts_in, 16)
            chain = Chain(dve, acc_chain, 1)

            def add(t, j, i):
                chain.tile(t)
                dve.wait_ge(out_ready, t + 1)
                dve.wait_ge(x_in[j], (i + 1) * 16)
                dve.wait_ge(y_in[j][0], (i + 1) * 16)
                chain(V.scalar_tensor_tensor(acc[j][:], ye[j][0][:], wts[:, 0, bass.ds(t, 1)], xb[j][:], ALU.mult, ALU.add))
                dve.wait_ge(y_in[j][1], (i + 1) * 16)
                V.scalar_tensor_tensor(acc[j][:], ye[j][1][:], wts[:, 1, bass.ds(t, 1)], acc[j][:], ALU.mult, ALU.add)\
                    .then_inc(acc_ready, 1)

            def norm(t, j, i):
                dve.wait_ge(rs_ready, t + 1)
                dve.wait_ge(acc_ready, t + 3)
                dve.wait_ge(stored[j], (i + 1) * 16)
                V.scalar_tensor_tensor(ot[j][:], acc[j][:], rs[j][:, 0:1], g_fin[:], ALU.mult, ALU.mult)\
                    .then_inc(out_ready, 1)

            add(0, 0, 0)
            with dve.Fori(0, TILES // 2 - 1) as i:
                add(i * 2 + 1, 1, i)
                norm(i * 2, 0, i)
                add(i * 2 + 2, 0, i + 1)
                norm(i * 2 + 1, 1, i)
            add(TILES - 1, 1, TILES // 2 - 1)
            norm(TILES - 2, 0, TILES // 2 - 1)
            norm(TILES - 1, 1, TILES // 2 - 1)


def layer_program(nc, io, out):
    dram = lambda name, shape, dt=F32: nc.dram_tensor(name, shape, dt, kind="Internal").ap()
    u_dram = dram("u_dram", [SEQ, GW])
    y_dram = dram("y_dram", [SEQ, GW])
    mix_dram = dram("mix_dram", [SEQ, 3 * GW])
    x2_dram = dram("x2_dram", [SEQ, D])
    xn_dram = dram("xn_dram", [SEQ, D])
    experts_dram = dram("experts_dram", [BLOCKS * P, D])
    table_dram = dram("table_dram", [BLOCKS * P, 1], I32)
    project_and_mix(nc, io, u_dram, mix_dram)
    state_space(nc, io, u_dram, y_dram)
    with ExitStack() as ctx:
        keep = lambda name, shape, dt=F32: ctx.enter_context(nc.sbuf_tensor(name, shape, dt))
        logits = keep("logits", [P, TILES, NG + NE])
        wts = keep("pair_weights", [P, 2, TILES])
        dest = keep("pair_rows", [P, 2, TILES], I32)
        block_rows = keep("block_rows", [P, BLOCKS], I32)
        block_expert = keep("block_expert", [1, BLOCKS], I32)
        block_side = keep("block_side", [1, BLOCKS], I32)
        expert_end = keep("expert_end", [1, NE], I32)
        merge_and_route(nc, io, mix_dram, y_dram, x2_dram, xn_dram, logits)
        plan_experts(nc, io, logits, wts, dest, block_rows, block_expert, block_side, expert_end, table_dram)
        run_experts(nc, io, block_rows, block_expert, block_side, expert_end, xn_dram, experts_dram)
        combine(nc, io, wts, dest, x2_dram, experts_dram, out)


def host_layout(inputs):
    import numpy as np

    a = {k: np.asarray(v) for k, v in inputs.items()}
    rows = lambda v: np.ascontiguousarray(np.broadcast_to(v.reshape(1, -1), (P, v.size)))
    kblocks = lambda w: np.ascontiguousarray(w.reshape(-1, P, w.shape[-1]).transpose(1, 0, 2))
    kcol = lambda v: np.ascontiguousarray(v.reshape(-1, P).T)
    w = a["w_in"][0]
    aq, ak, av, su, cq, ck, cv, ci, cf, co, gu, gv = np.split(
        w, np.cumsum([256, 128, 128, 256, 256, 256, 256, 4, 4, 256, 256])[:], axis=1)
    q = aq.reshape(D, 4, DH)[:, [0, 2, 1, 3]].reshape(D, GW)
    w = np.concatenate([q, ak, cq, ck, av, cv, co, gu, gv, su, ci, cf], axis=1)
    step = np.arange(P)
    neg = np.float32(-1e30)
    current = np.where(step[None] <= step[:, None], np.float32(0), neg)
    before = np.where(step[None] > step[:, None], np.float32(0), neg)
    head = np.arange(HEADS)
    out = {
        "x": np.ascontiguousarray(a["x"][0]),
        "ident": np.eye(P, dtype=np.float32),
        "w_in": kblocks(w),
        "g_mix": kcol(a["norm_mix_g"][0]),
        "gate_b": rows(a["mlstm_gate_b"][0]),
        "sinks": rows(a["attn_sinks"][0]),
        "conv_w": np.ascontiguousarray(a["mlstm_conv_w"][0].reshape(4, 4, P).transpose(2, 1, 0)),
        "norm_c": rows(a["mlstm_norm_g"][0]),
        "ln_g": rows(a["sgu_ln_g"][0]),
        "ln_b": rows(a["sgu_ln_b"][0]),
        "sgu_w": np.ascontiguousarray(a["sgu_w"][0].transpose(2, 0, 1)),
        "sgu_b": np.ascontiguousarray(a["sgu_b"][0].T),
        "tri": (step[:, None] <= step[None]).astype(np.float32),
        "causal": np.where(step[:, None] <= step[None], np.float32(0), neg),
        "mask_first": np.stack([current, np.full((P, P), neg)], 1),
        "mask_even": np.stack([current, before], 1),
        "mask_odd": np.stack([before, current], 1),
        "sel": np.ascontiguousarray(np.broadcast_to(np.eye(HEADS, dtype=np.float32)[:, :, None], (HEADS, HEADS, P))),
        "half": (head[:, None] % 2 == step[None] // 64).astype(np.float32),
        "slotmask": (head[:, None] // 2 == np.arange(2)[None]).astype(np.float32),
    }
    return out


def s5_layout(a):
    import numpy as np

    both = lambda v: np.ascontiguousarray(np.concatenate([v.T, v.T]))
    stack = lambda top, low: np.ascontiguousarray(np.concatenate([top, low]))
    b_re, b_im = (a[k][0].transpose(1, 0, 2) for k in ("ssm_b_re", "ssm_b_im"))
    c_re, c_im = (a[k][0].transpose(2, 0, 1) for k in ("ssm_c_re", "ssm_c_im"))
    eye = np.eye(P, dtype=np.float32)
    return {
        "swap": np.roll(eye, 64, 0),
        "sign": np.repeat(np.array([-1, 1], np.float32), 64)[:, None],
        "idt": np.concatenate([eye, np.zeros((P, P), np.float32), eye], 1),
        "dskip": np.ascontiguousarray(np.tile(a["ssm_d"][0].reshape(GROUPS, GH).T, (P // GH, 1))),
        "are": both(a["ssm_a_re"][0]),
        "aim": both(a["ssm_a_im"][0]),
        "ldt": np.ascontiguousarray(np.broadcast_to(a["ssm_log_dt"][0][None], (P, GROUPS))),
        "b1": stack(b_re, b_im),
        "b2": stack(b_im, b_re),
        "c1": stack(c_re, c_im),
        "c2": stack(c_im, c_re),
    }


def ffn_layout(a):
    import numpy as np

    rows = lambda v: np.ascontiguousarray(np.broadcast_to(v.reshape(1, -1), (P, v.size)))
    kblocks = lambda w: np.ascontiguousarray(w.reshape(-1, P, w.shape[-1]).transpose(1, 0, 2))
    w_out = a["w_out"][0].reshape(4, GW, D)[[0, 2, 3, 1]].reshape(D, D)
    step = np.arange(P)
    down = lambda n: rows(np.arange(n, 0, -1).astype(np.float32))
    return {
        "w_out": kblocks(w_out),
        "glu_w": kblocks(a["ssm_glu_w"][0]),
        "glu_b": rows(a["ssm_glu_b"][0]),
        "w_r": kblocks(np.concatenate([a["router_group_w"][0], a["router_expert_w"][0]], 1)),
        "b_r": rows(np.concatenate([a["router_group_b"][0], a["router_expert_b"][0]])),
        "g_ffn": np.ascontiguousarray(a["norm_ffn_g"][0].reshape(-1, P).T),
        "g_fin": rows(a["norm_final_g"]),
        "before": (step[:, None] < step[None]).astype(np.float32),
        "ones": np.ones((P, P), np.float32),
        "reset": rows((np.arange(NE * TILES) % TILES > 0).astype(np.float32)),
        "rank4": down(NG),
        "rank8": down(NE_G),
        "block_no": np.arange(BLOCKS, dtype=np.float32)[None],
        "w_gate": np.ascontiguousarray(a["expert_w_gate"][0]),
        "w_up": np.ascontiguousarray(a["expert_w_up"][0]),
        "w_down": np.ascontiguousarray(a["expert_w_down"][0]),
    }


def kernel(**inputs):
    import numpy as np
    import concourse.bacc as bacc
    from concourse.bass_utils import run_bass_kernel_spmd

    a = {k: np.asarray(v) for k, v in inputs.items()}
    arrays = {**host_layout(a), **s5_layout(a), **ffn_layout(a)}
    nc = bacc.Bacc("TRN2", target_bir_lowering=False, num_devices=1)
    io = {k: nc.dram_tensor(f"in_{k}", v.shape, mybir.dt.from_np(v.dtype), kind="ExternalInput").ap()
          for k, v in arrays.items()}
    out = nc.dram_tensor("out", (SEQ, D), F32, kind="ExternalOutput").ap()
    layer_program(nc, io, out)
    r = run_bass_kernel_spmd(nc, [{f"in_{k}": v for k, v in arrays.items()}], core_ids=[0])
    return r.results[0]["out"].reshape(1, SEQ, D)
```

```python
from contextlib import ExitStack

import concourse.bass as bass
from concourse import mybir

F32 = mybir.dt.float32
I32 = mybir.dt.int32
F32R = mybir.dt.float32r
ALU = mybir.AluOpType
ACT = mybir.ActivationFunctionType
AX = mybir.AxisListType

P = 128
SEQ = 4096
D = 1024
TILES = SEQ // P
KD = D // P
GW = 256
HEADS = 4
DH = 64
EPS = 1e-6
GELU_A = 0.044715
GELU_B = 0.7978845608028654

AQ, AK, CQK, AV, CV, CO, GU, GV, SU, GATES = 0, 256, 384, 896, 1024, 1280, 1536, 1792, 2048, 2304
ZW = 2312
ZCHUNK = 512
ZCHUNKS = [(c, min(ZCHUNK, ZW - c)) for c in range(0, ZW, ZCHUNK)]

GROUPS, GH, STATE = 16, 16, 64
L = 16
CH = SEQ // L
CT = CH // P
LEVELS = 8

NG, NE_G = 4, 8
NE = NG * NE_G
FE = 512
KF = FE // P
BLOCKS = SEQ * 2 // P + NE - 1


class Chain:

    def __init__(self, engine, sem, per_tile=0):
        self.engine, self.sem, self.per_tile, self.base, self.n = engine, sem, per_tile, 0, 0

    def tile(self, t):
        if self.n and self.per_tile:
            assert self.n == self.per_tile, (self.n, self.per_tile)
        self.base, self.n = t * self.per_tile, 0

    def __call__(self, instruction):
        self.n += 1
        instruction.then_inc(self.sem, 1)
        self.engine.wait_ge(self.sem, self.base + self.n)


class Bank:

    def __init__(self, full, free, uses):
        self.full, self.free, self.uses = full, free, uses

    def wait_free(self, pe, t, use):
        pe.wait_ge(self.free, t * self.uses + use + 1)

    def wait_full(self, engine, t, use):
        engine.wait_ge(self.full, t * self.uses + use + 1)


def end_phase(nc, semaphores):
    nc.clear_and_free_semaphores(semaphores)
    nc.all_engine_barrier()


def pass_wait(engine, passed):
    engine.sem_inc(passed, 1)


def bc(ap, n):
    return ap.unsqueeze(2).to_broadcast([ap.shape[0], ap.shape[1], n])


def project_and_mix(nc, io, u_dram, mix_dram):
    semaphores = []
    with ExitStack() as ctx:
        ctx.callback(end_phase, nc, semaphores)

        def sb(name, shape, dt=F32):
            return ctx.enter_context(nc.sbuf_tensor(name, shape, dt))

        def sem(name):
            semaphores.append(nc.alloc_semaphore(name=name))
            return semaphores[-1]

        ident = sb("a_ident", [P, P])
        w_in = sb("w_in_sb", [P, KD, ZW])
        g_mix = sb("g_mix_sb", [P, KD])
        gate_b = sb("gate_b_sb", [P, 8])
        sinks = sb("sinks_sb", [P, HEADS])
        conv_w = sb("conv_w_sb", [P, 4, 4])
        norm_c = sb("norm_c_sb", [P, GW])
        ln_g = sb("ln_g_sb", [P, GW])
        ln_b = sb("ln_b_sb", [P, GW])
        sgu_w = sb("sgu_w_sb", [P, HEADS, P])
        sgu_b = sb("sgu_b_sb", [P, HEADS])
        tri = sb("tri_sb", [P, P])
        causal = sb("causal_sb", [P, P])
        mask_even = sb("mask_even", [P, 2, P])
        mask_even_std = sb("mask_even_std", [P, 2, P])
        mask_odd = sb("mask_odd", [P, 2, P])
        sel = sb("sel_sb", [HEADS, HEADS, P])
        half = sb("half_sb", [HEADS, P])
        slotmask = sb("slotmask_sb", [HEADS, 2])
        xb = [sb(f"a_x{j}", [P, D]) for j in range(2)]
        xn = sb("a_xn", [P, D])
        xsq = sb("xsq", [P, D])
        xT = sb("a_xT", [P, KD, P])
        ss = sb("a_ss", [P, 1])
        rs = sb("a_rs", [P, 1])
        minus_half = sb("a_minus_half", [P, HEADS])
        eps, eps_twice = sb("a_eps", [P, 1]), sb("eps_twice", [P, 1])
        z = [sb(f"z{j}", [P, ZW]) for j in range(2)]
        qT = sb("qT", [P, 2, P])
        kT = sb("kT", [P, 2, P])
        va = sb("va", [P, 2, P])
        scores = sb("scores", [P, HEADS, 2 * P])
        smax = sb("smax", [P, HEADS])
        snmax = sb("snmax", [P, HEADS])
        ssink = sb("ssink", [P, HEADS])
        esink = sb("esink", [P, HEADS])
        den = sb("den", [P, HEADS])
        rden = sb("rden", [P, HEADS])
        probs = sb("probs", [P, HEADS, 2 * P])
        pT = sb("pT", [P, HEADS, 2, P])
        cx = sb("cx", [P, 4, P + 3])
        cv = sb("cv", [P, 4, P])
        cth = sb("cth", [P, 4, P])
        qk = sb("qk", [P, 4, P])
        k_tok = sb("k_tok", [P, HEADS, DH])
        kw = sb("kw", [P, HEADS, DH])
        v1 = sb("v1", [P, HEADS, DH + 1])
        gates = sb("gates", [P, 8])
        fa = sb("fa", [P, 4])
        fy = sb("fy", [P, 4])
        fq = sb("fq", [P, 4])
        fq2 = sb("fq2", [P, 4])
        fp = sb("fp", [P, 4])
        nlogf = sb("nlogf", [P, 4])
        zero_row = sb("zero_row", [HEADS, P])
        m_row = sb("m_row", [HEADS, P])
        mt_row = sb("mt_row", [HEADS, P])
        m_prev = sb("m_prev", [HEADS, 1])
        wi_row = sb("wi_row", [HEADS, P])
        em_row = sb("em_row", [HEADS, P])
        wi_last = sb("wi_last", [HEADS, 2])
        gcol = sb("gcol", [P, 4])
        cols = sb("cols", [P, 10])
        earg = sb("earg", [P, HEADS, P])
        et = sb("et", [P, HEADS, P])
        wT = sb("wT", [P, HEADS, P])
        cn = sb("cn", [P, 2, DH + 1])
        inter = sb("inter", [P, HEADS, DH + 1])
        num = sb("num", [P, HEADS, DH + 1])
        dena = sb("dena", [P, HEADS])
        rdc = sb("rdc", [P, HEADS])
        hc = sb("hc", [P, HEADS, DH])
        hsq = sb("hsq", [P, HEADS, DH])
        hss = sb("hss", [P, HEADS])
        hrs = sb("hrs", [P, HEADS])
        coth = sb("coth", [P, GW])
        gco = sb("gco", [P, GW])
        gsq = sb("gsq", [P, 2 * GW])
        gin = sb("gin", [P, 2 * GW])
        gth = sb("gth", [P, 2 * GW])
        ge = sb("ge", [P, 2 * GW])
        bst = sb("bst", [P, 6])
        mv = sb("mv", [P, 2])
        lrs = sb("lrs", [P, 1])
        vn = sb("vn", [P, GW])
        mix = [sb(f"mix{j}", [P, 3 * GW]) for j in range(2)]

        b = [ctx.enter_context(nc.psum_tensor(f"a_bank{n}", [P, 512], F32)) for n in range(8)]
        uses = [4, 3, 3, 3, 4, 1, 1, 3]
        bank = [Bank(sem(f"a_full{n}"), sem(f"a_free{n}"), uses[n]) for n in range(8)]

        weights_in = sem("weights_in")
        consts_set = sem("consts_set")
        w_scaled = sem("w_scaled")
        x_in = [sem(f"a_x_in{j}") for j in range(2)]
        sq_done = sem("sq_done")
        xn_ready = sem("xn_ready")
        z_ready = sem("z_ready")
        su_out = [sem(f"su_out{j}") for j in range(2)]
        mix_out = [sem(f"mix_out{j}") for j in range(2)]
        mix_ready = sem("mix_ready")
        qkT_ready = sem("qkT_ready")
        cx_ready = sem("cx_ready")
        conv_ready = sem("conv_ready")
        cth_ready = sem("cth_ready")
        qk_ready = sem("qk_ready")
        gates_ready = sem("gates_ready")
        fa_ready = sem("fa_ready")
        fy_ready = sem("fy_ready")
        nlogf_ready = sem("nlogf_ready")
        m_ready = sem("m_ready")
        rows_ready = sem("rows_ready")
        wi_last_ready = sem("wi_last_ready")
        k_tok_ready = sem("k_tok_ready")
        v1_ready = sem("v1_ready")
        va_ready = sem("va_ready")
        earg_ready = sem("earg_ready")
        et_ready = sem("et_ready")
        wT_ready = sem("wT_ready")
        cn_ready = sem("cn_ready")
        snmax_ready = sem("snmax_ready")
        probs_ready = sem("probs_ready")
        esink_ready = sem("esink_ready")
        pT_ready = sem("pT_ready")
        gin_ready = sem("gin_ready")
        gth_ready = sem("gth_ready")
        ge_ready = sem("ge_ready")
        var_ready = sem("var_ready")
        lrs_ready = sem("lrs_ready")
        vn_ready = sem("vn_ready")
        vnb_ready = sem("vnb_ready")
        coth_ready = sem("coth_ready")
        hc_ready = sem("hc_ready")
        rs_ready = sem("rs_ready")
        conv_tail = sem("conv_tail")
        mask_kept = sem("mask_kept")
        hsq_ready = sem("hsq_ready")
        hss_ready = sem("hss_ready")
        hrs_ready = sem("hrs_ready")
        pool_passed, dve_passed = sem("a_pool_passed"), sem("a_dve_passed")
        dve_chain = sem("a_dve_chain")
        act_chain = sem("a_act_chain")
        pool_norm_chain = sem("a_pool_norm_chain")
        pool_mix_chain = sem("a_pool_mix_chain")

        LOADS = [(ident, io["ident"]), (w_in, io["w_in"]), (g_mix, io["g_mix"]), (gate_b, io["gate_b"]),
                 (sinks, io["sinks"]), (conv_w, io["conv_w"]), (norm_c, io["norm_c"]), (ln_g, io["ln_g"]),
                 (ln_b, io["ln_b"]), (sgu_w, io["sgu_w"]), (sgu_b, io["sgu_b"]), (tri, io["tri"]),
                 (causal, io["causal"]), (mask_even, io["mask_first"]), (mask_even_std, io["mask_even"]),
                 (mask_odd, io["mask_odd"]), (sel, io["sel"]), (half, io["half"]), (slotmask, io["slotmask"])]
        ALL_IN = 16 * len(LOADS)
        x_tiles = io["x"].rearrange("(t p) d -> t p d", p=P)
        u_tiles = u_dram.rearrange("(t p) d -> t p d", p=P)
        mix_tiles = mix_dram.rearrange("(t p) d -> t p d", p=P)
        heads_of = lambda ap, e: ap.rearrange("p (s e) l -> p e s l", e=2)[:, e]

        def run_slots(engine, slot, prologue):
            prologue()
            with engine.Fori(0, TILES // 2 - 1) as i:
                slot(i * 2, 0, i, True, True)
                slot(i * 2 + 1, 1, i, True, True)
            slot(TILES - 2, 0, TILES // 2 - 1, True, False)
            slot(TILES - 1, 1, TILES // 2 - 1, False, False)

        block = ctx.enter_context(nc.Block())

        @block.sync
        def _(sp):
            for dst, src in LOADS:
                sp.dma_start(dst[:], src).then_inc(weights_in, 16)

            def load_x(t, j):
                sp.wait_ge(xn_ready, t + 1)
                sp.dma_start(xb[j][:], x_tiles[bass.ds(t, 1)].rearrange("a p d -> (a p) d")).then_inc(x_in[j], 16)

            def slot(t, j, i):
                if not (isinstance(t, int) and t + 3 >= TILES):
                    load_x(t + 3, 1 - j)
                sp.wait_ge(z_ready, (t + 1) * len(ZCHUNKS))
                sp.dma_start(u_tiles[bass.ds(t, 1)].rearrange("a p d -> (a p) d"),
                             z[j][:, SU:SU + GW]).then_inc(su_out[j], 16)
                sp.wait_ge(mix_ready, t + 2)
                sp.dma_start(mix_tiles[bass.ds(t, 1)].rearrange("a p d -> (a p) d"), mix[j][:]).then_inc(mix_out[j], 16)

            for t in range(3):
                load_x(t, t % 2)
            with sp.Fori(0, TILES // 2 - 2) as i:
                slot(i * 2, 0, i)
                slot(i * 2 + 1, 1, i)
            for t in range(TILES - 4, TILES):
                slot(t, t % 2, t // 2)
            for j in range(2):
                sp.wait_ge(su_out[j], 16 * (TILES // 2 + 1))
                sp.wait_ge(mix_out[j], 16 * (TILES // 2 + 1))

        @block.gpsimd
        def _(pool):
            norm_chain = Chain(pool, pool_norm_chain, 1)
            chain = Chain(pool, pool_mix_chain, 5)
            pool.sem_inc(xn_ready, 2)
            for j in range(2):
                pool.sem_inc(su_out[j], 16)
                pool.sem_inc(mix_out[j], 16)
            nc.gpsimd.memset(minus_half[:], -0.5).then_inc(consts_set, 1)
            nc.gpsimd.memset(eps[:], EPS).then_inc(consts_set, 1)
            nc.gpsimd.memset(eps_twice[:], 4 * EPS).then_inc(consts_set, 1)
            nc.gpsimd.memset(v1[:, :, DH:DH + 1], 1.0).then_inc(consts_set, 1)
            nc.gpsimd.memset(va[:, 1, :], 0.0).then_inc(consts_set, 1)
            nc.gpsimd.memset(zero_row[:], 0.0).then_inc(consts_set, 1)
            nc.gpsimd.memset(mt_row[:], 0.0).then_inc(consts_set, 1)
            nc.gpsimd.memset(cx[:, :, 0:3], 0.0).then_inc(consts_set, 1)
            nc.gpsimd.memset(kT[:, 1, :], 0.0).then_inc(consts_set, 1)
            nc.gpsimd.memset(cn[:], 0.0).then_inc(cn_ready, 1)
            pool.wait_ge(consts_set, 9)
            pool.wait_ge(weights_in, ALL_IN)

            def normalise(t, j):
                norm_chain.tile(t)
                pool.wait_ge(sq_done, t + 1)
                norm_chain(nc.gpsimd.tensor_tensor(rs[:], ss[:], eps[:], ALU.add))
                nc.gpsimd.tensor_tensor(rs[:], rs[:], minus_half[:, 0:1], ALU.pow).then_inc(rs_ready, 1)
                pool.wait_ge(rs_ready, t + 1)
                if not (isinstance(t, int) and t == 0):
                    bank[0].wait_full(pool, t - 1, 0)
                    bank[1].wait_full(pool, t - 1, 0)
                pass_wait(pool, pool_passed)
                nc.gpsimd.tensor_scalar(xn[:], xb[j][:], rs[:, 0:1], None, ALU.mult).then_inc(xn_ready, 1)

            def slot(t, j, i, projecting, norming):
                chain.tile(t)
                zt = z[j]
                pool.wait_ge(z_ready, (t + 1) * len(ZCHUNKS))
                pool.wait_ge(mix_ready, t + 1)
                pass_wait(pool, pool_passed)
                nc.gpsimd.tensor_copy(va[:, j, :], zt[:, AV:AV + P]).then_inc(va_ready, 1)
                nc.gpsimd.tensor_copy(v1[:, :, 0:DH], zt[:, CV:CV + GW].rearrange("p (h d) -> p h d", h=HEADS))\
                    .then_inc(v1_ready, 1)
                guv = zt[:, GU:GU + 2 * GW]
                chain(nc.gpsimd.tensor_tensor(gsq[:], guv, guv, ALU.mult))
                pass_wait(pool, pool_passed)
                chain(nc.gpsimd.tensor_scalar(gsq[:], gsq[:], GELU_A, 1.0, ALU.mult, ALU.add))
                nc.gpsimd.tensor_tensor(gin[:], gsq[:], guv, ALU.mult).then_inc(gin_ready, 1)
                if norming:
                    normalise(t + 2, j)
                pool.wait_ge(var_ready, t + 1)
                chain(nc.gpsimd.tensor_tensor(lrs[:], mv[:, 1:2], eps_twice[:], ALU.add))
                nc.gpsimd.tensor_tensor(lrs[:], lrs[:], minus_half[:, 0:1], ALU.pow).then_inc(lrs_ready, 1)
                pool.wait_ge(vn_ready, t + 1)
                chain(nc.gpsimd.tensor_tensor(vn[:], vn[:], ln_g[:], ALU.mult))
                nc.gpsimd.tensor_tensor(vn[:], vn[:], ln_b[:], ALU.add).then_inc(vnb_ready, 1)
                pool.wait_ge(hc_ready, t + 1)
                nc.gpsimd.tensor_tensor(hsq[:], hc[:], hc[:], ALU.mult).then_inc(hsq_ready, 1)
                pool.wait_ge(hss_ready, t + 1)
                pass_wait(pool, pool_passed)
                chain(nc.gpsimd.tensor_scalar(hrs[:], hss[:], 1.0 / DH, EPS, ALU.mult, ALU.add))
                nc.gpsimd.tensor_tensor(hrs[:], hrs[:], minus_half[:], ALU.pow).then_inc(hrs_ready, 1)

            def prologue():
                normalise(0, 0)
                normalise(1, 1)

            run_slots(pool, slot, prologue)

        @block.scalar
        def _(act):
            chain = Chain(act, act_chain)
            act.wait_ge(consts_set, 9)
            act.wait_ge(weights_in, ALL_IN)

            def square(t, j, i):
                act.wait_ge(x_in[j], (i + 1) * 16)
                nc.scalar.activation(xsq[:], xb[j][:], ACT.Square, scale=D ** -0.5, accum_out=ss[:]).then_inc(sq_done, 1)

            def evac_xT(t):
                bank[0].wait_full(act, t, 0)
                nc.scalar.activation(xT[:, 0:4, :], b[0][:].rearrange("p (k n) -> p k n", k=4), ACT.Copy)\
                    .then_inc(bank[0].free, 1)

            def evac_z(t, j, n):
                c, w = ZCHUNKS[n]
                k, use = (0, 1 + n // 2) if n % 2 == 0 else (1, 1 + n // 2)
                bank[k].wait_full(act, t, use)
                nc.scalar.activation(z[j][:, c:c + w], b[k][:, 0:w], ACT.Copy).then_inc(bank[k].free, 1)
                bank[k].wait_free(act, t, use + 1)
                act.sem_inc(z_ready, 1)

            def slot(t, j, i, projecting, norming):
                tp, jp = t + 1, 1 - j
                ip = i if j == 0 else i + 1
                zt = z[j]
                if projecting:
                    evac_xT(tp)
                bank[2].wait_full(act, t, 0)
                nc.scalar.activation(qT[:], b[2][:, 0:2 * P].rearrange("p (c n) -> p c n", c=2), ACT.Copy)\
                    .then_inc(qkT_ready, 1)
                nc.scalar.activation(kT[:, j, :], b[2][:, 2 * P:3 * P], ACT.Copy).then_inc(bank[2].free, 1)
                bank[3].wait_full(act, t, 0)
                act.wait_ge(conv_tail, t + 1)
                nc.scalar.activation(cx[:, :, 3:P + 3], b[3][:].rearrange("p (c n) -> p c n", c=4), ACT.Copy)\
                    .then_inc(bank[3].free, 1)
                act.wait_ge(gates_ready, t + 1)
                nc.scalar.activation(fa[:], gates[:, 4:8], ACT.Abs).then_inc(fa_ready, 1)
                act.wait_ge(fa_ready, t + 1)
                nc.scalar.activation(fy[:], fa[:], ACT.Exp, scale=-1.0).then_inc(fy_ready, 1)
                if norming:
                    act.wait_ge(xn_ready, t + 4)
                    square(t + 2, j, i + 1)
                nc.scalar.activation(coth[:], zt[:, CO:CO + GW], ACT.Tanh, scale=0.5).then_inc(coth_ready, 1)
                act.wait_ge(gin_ready, t + 1)
                nc.scalar.activation(gth[:], gin[:], ACT.Tanh, scale=GELU_B).then_inc(gth_ready, 1)
                if projecting:
                    act.wait_ge(mix_ready, t + 1)
                    act.wait_ge(su_out[jp], (ip + 1) * 16)
                    evac_z(tp, jp, 0)
                act.wait_ge(conv_ready, t + 1)
                nc.scalar.activation(cth[:], cv[:], ACT.Tanh, scale=0.5).then_inc(cth_ready, 1)
                act.wait_ge(m_ready, 2 * (t + 1))
                nc.scalar.activation(wi_row[:], m_row[:], ACT.Exp, bias=m_prev[:, 0:1], scale=-1.0).then_inc(rows_ready, 1)
                nc.scalar.activation(em_row[:], mt_row[:], ACT.Exp, scale=-1.0).then_inc(rows_ready, 1)
                if projecting:
                    evac_z(tp, jp, 1)
                act.wait_ge(snmax_ready, t + 1)
                for h in range(HEADS):
                    nc.scalar.activation(probs[:, h, :], scores[:, h, :], ACT.Exp, bias=snmax[:, h:h + 1],
                                         scale=DH ** -0.5, accum_out=den[:, h:h + 1]).then_inc(probs_ready, 1)
                nc.scalar.activation(esink[:], ssink[:], ACT.Exp).then_inc(esink_ready, 1)
                bank[7].wait_full(act, t, 0)
                nc.scalar.activation(k_tok[:], b[7][:, 0:GW].rearrange("p (h d) -> p h d", h=HEADS), ACT.Copy)\
                    .then_inc(bank[7].free, 1)
                act.wait_ge(earg_ready, t + 1)
                for h in range(HEADS):
                    nc.scalar.activation(et[:, h, :], earg[:, h, :], ACT.Exp, bias=gcol[:, h:h + 1])\
                        .then_inc(et_ready, 1)
                if projecting:
                    evac_z(tp, jp, 2)
                    evac_z(tp, jp, 3)
                bank[2].wait_full(act, t, 2)
                nc.scalar.activation(pT[:, 0:2].rearrange("p h s n -> p (h s n)"), b[2][:], ACT.Copy)\
                    .then_inc(bank[2].free, 1)
                bank[3].wait_full(act, t, 2)
                nc.scalar.activation(pT[:, 2:4].rearrange("p h s n -> p (h s n)"), b[3][:], ACT.Copy)\
                    .then_inc(bank[3].free, 1)
                if projecting:
                    evac_z(tp, jp, 4)

            def prologue():
                square(0, 0, 0)
                act.wait_ge(xn_ready, 3)
                square(1, 1, 0)
                evac_xT(0)
                for n in range(len(ZCHUNKS)):
                    evac_z(0, 0, n)

            run_slots(act, slot, prologue)

        @block.vector
        def _(dve):
            chain = Chain(dve, dve_chain, 50)
            for k in bank:
                dve.sem_inc(k.free, 1)
            dve.sem_inc(mix_ready, 1)
            dve.sem_inc(conv_tail, 1)
            dve.sem_inc(mask_kept, 1)
            dve.wait_ge(consts_set, 9)
            dve.wait_ge(weights_in, ALL_IN)
            for k in range(KD):
                nc.vector.tensor_scalar(w_in[:, k, :], w_in[:, k, :], g_mix[:, k:k + 1], None, ALU.mult)\
                    .then_inc(w_scaled, 1)
            nc.vector.tensor_tensor(sgu_w[:], sgu_w[:], tri[:].unsqueeze(1).to_broadcast([P, HEADS, P]), ALU.mult)\
                .then_inc(w_scaled, 1)

            def evac_xT(t):
                bank[1].wait_full(dve, t, 0)
                nc.vector.tensor_copy(xT[:, 4:8, :], b[1][:].rearrange("p (k n) -> p k n", k=4))\
                    .then_inc(bank[1].free, 1)

            def slot(t, j, i, projecting, norming):
                chain.tile(t)
                zt, mx = z[j], mix[j]
                if projecting:
                    evac_xT(t + 1)
                dve.wait_ge(z_ready, (t + 1) * len(ZCHUNKS))
                nc.vector.tensor_tensor(gates[:], zt[:, GATES:GATES + 8], gate_b[:], ALU.add).then_inc(gates_ready, 1)
                dve.wait_ge(gates_ready, t + 1)
                dve.wait_ge(fy_ready, t + 1)
                chain(nc.vector.tensor_scalar(fp[:], fy[:], 2.0, None, ALU.add))
                chain(nc.vector.reciprocal(fp[:], fp[:]))
                chain(nc.vector.tensor_tensor(fq[:], fy[:], fp[:], ALU.mult))
                chain(nc.vector.tensor_tensor(fq2[:], fq[:], fq[:], ALU.mult))
                chain(nc.vector.tensor_scalar(fp[:], fq2[:], 1.0 / 17, None, ALU.mult))
                for c in (15, 13, 11, 9, 7, 5, 3):
                    chain(nc.vector.scalar_tensor_tensor(fp[:], fp[:], 1.0 / c, fq2[:], ALU.add, ALU.mult))
                chain(nc.vector.scalar_tensor_tensor(fp[:], fp[:], 1.0, fq[:], ALU.add, ALU.mult))
                chain(nc.vector.tensor_scalar(fq[:], gates[:, 4:8], -1.0, 0.0, ALU.mult, ALU.max))
                nc.vector.scalar_tensor_tensor(nlogf[:], fp[:], 2.0, fq[:], ALU.mult, ALU.add).then_inc(nlogf_ready, 1)
                bank[4].wait_full(dve, t, 0)
                nc.vector.tensor_copy(m_prev[:], mt_row[:, P - 1:P]).then_inc(m_ready, 1)
                chain(nc.vector.tensor_tensor_scan(m_row[:], zero_row[:], b[4][0:HEADS, P:2 * P],
                                                   mt_row[:, P - 1:P], ALU.add, ALU.max))
                chain(nc.vector.tensor_copy(gcol[:], b[4][:, 2 * P:2 * P + 4]))
                nc.vector.tensor_tensor(mt_row[:], m_row[:], b[4][0:HEADS, 0:P], ALU.subtract)\
                    .then_inc(bank[4].free, 1)
                bank[4].wait_free(dve, t, 1)
                dve.sem_inc(m_ready, 1)
                mask = mask_even if j == 0 else mask_odd
                dve.wait_ge(mask_kept, i + 1)
                for e in range(2):
                    bank[2 + e].wait_full(dve, t, 1)
                    nc.vector.tensor_tensor(scores[:, 2 * e:2 * e + 2, :],
                                            b[2 + e][:].rearrange("p (h n) -> p h n", h=2),
                                            mask[:].rearrange("p s n -> p (s n)").unsqueeze(1)
                                            .to_broadcast([P, 2, 2 * P]), ALU.add).then_inc(bank[2 + e].free, 1)
                bank[2].wait_free(dve, t, 2)
                bank[3].wait_free(dve, t, 2)
                chain(nc.vector.tensor_reduce(smax[:], scores[:], AX.X, ALU.max))
                chain(nc.vector.scalar_tensor_tensor(smax[:], smax[:], DH ** -0.5, sinks[:], ALU.mult, ALU.max))
                chain(nc.vector.tensor_tensor(ssink[:], sinks[:], smax[:], ALU.subtract))
                if j == 0:
                    nc.vector.tensor_copy(mask_even[:], mask_even_std[:]).then_inc(mask_kept, 1)
                nc.vector.tensor_scalar(snmax[:], smax[:], -1.0, None, ALU.mult).then_inc(snmax_ready, 1)
                bank[3].wait_free(dve, t, 1)
                for c in range(4):
                    chain(nc.vector.tensor_scalar(cv[:, c, :], cx[:, c, 0:P], conv_w[:, c, 0:1], None, ALU.mult))
                for tap in range(1, 4):
                    for c in range(4):
                        ins = nc.vector.scalar_tensor_tensor(cv[:, c, :], cx[:, c, tap:tap + P],
                                                             conv_w[:, c, tap:tap + 1], cv[:, c, :], ALU.mult, ALU.add)
                        if tap == 3 and c == 3:
                            ins.then_inc(conv_ready, 1)
                        else:
                            chain(ins)
                dve.wait_ge(conv_ready, t + 1)
                nc.vector.tensor_copy(cx[:, :, 0:3], cx[:, :, P:P + 3]).then_inc(conv_tail, 1)
                dve.wait_ge(cth_ready, t + 1)
                nc.vector.scalar_tensor_tensor(qk[:], cth[:], 1.0, cv[:], ALU.add, ALU.mult).then_inc(qk_ready, 1)
                dve.wait_ge(gth_ready, t + 1)
                nc.vector.scalar_tensor_tensor(ge[:], gth[:], 1.0, zt[:, GU:GU + 2 * GW], ALU.add, ALU.mult)\
                    .then_inc(ge_ready, 1)
                dve.wait_ge(ge_ready, t + 1)
                chain(nc.vector.bn_stats(bst[:], ge[:, GW:2 * GW]))
                pass_wait(dve, dve_passed)
                nc.vector.bn_aggr(mv[:], bst[:]).then_inc(var_ready, 1)
                dve.wait_ge(rows_ready, 2 * (t + 1))
                nc.vector.tensor_scalar(wi_last[:], slotmask[:], wi_row[:, P - 1:P], None, ALU.mult)\
                    .then_inc(wi_last_ready, 1)
                bank[4].wait_full(dve, t, 1)
                nc.vector.tensor_tensor(earg[:], causal[:].unsqueeze(1).to_broadcast([P, HEADS, P]),
                                        b[4][:].rearrange("p (h n) -> p h n", h=HEADS), ALU.subtract)\
                    .then_inc(bank[4].free, 1)
                bank[4].wait_free(dve, t, 2)
                dve.sem_inc(earg_ready, 1)
                dve.wait_ge(lrs_ready, t + 1)
                dve.wait_ge(var_ready, t + 1)
                nc.vector.tensor_scalar(vn[:], ge[:, GW:2 * GW], mv[:, 0:1], lrs[:, 0:1], ALU.subtract, ALU.mult)\
                    .then_inc(vn_ready, 1)
                bank[7].wait_full(dve, t, 1)
                nc.vector.tensor_copy(cols[:], b[7][:, 0:10]).then_inc(bank[7].free, 1)
                bank[7].wait_free(dve, t, 2)
                dve.wait_ge(et_ready, 4 * (t + 1))
                for e in range(2):
                    bank[5 + e].wait_full(dve, t, 0)
                    chain(nc.vector.tensor_tensor(heads_of(wT[:], e), heads_of(et[:], e),
                                                  b[5 + e][:, 0:2 * P].rearrange("p (s n) -> p s n", s=2), ALU.mult))
                    nc.vector.tensor_tensor(heads_of(inter[:], e),
                                            b[5 + e][:, 2 * P:2 * P + 130].rearrange("p (s n) -> p s n", s=2),
                                            bc(cols[:, e:4:2], DH + 1), ALU.mult).then_inc(bank[5 + e].free, 1)
                bank[6].wait_free(dve, t + 1, 0)
                bank[7].wait_free(dve, t, 1)
                nc.vector.tensor_tensor(kw[:], k_tok[:], et[:, :, P - 1:P].to_broadcast([P, HEADS, DH]), ALU.mult)\
                    .then_inc(wT_ready, 1)
                dve.wait_ge(coth_ready, t + 1)
                chain(nc.vector.scalar_tensor_tensor(gco[:], coth[:], 1.0, norm_c[:], ALU.add, ALU.mult))
                bank[7].wait_full(dve, t, 2)
                bank[5].wait_free(dve, t + 1, 0)
                chain(nc.vector.tensor_tensor(num[:], b[7][:, 0:260].rearrange("p (h n) -> p h n", h=HEADS), inter[:],
                                              ALU.add))
                for s in range(2):
                    ins = nc.vector.scalar_tensor_tensor(cn[:, s, :], cn[:, s, :], cols[:, 8 + s:9 + s],
                                                         b[7][:, 260 + 65 * s:325 + 65 * s], ALU.mult, ALU.add)
                    if s == 0:
                        chain(ins)
                    else:
                        ins.then_inc(bank[7].free, 1)
                bank[7].wait_free(dve, t + 1, 0)
                dve.sem_inc(cn_ready, 1)
                den_c = num[:, :, DH]
                chain(nc.vector.tensor_scalar(dena[:], cols[:, 4:8], 32.0, None, ALU.mult))
                chain(nc.vector.tensor_tensor(dena[:], dena[:], den_c, ALU.max))
                chain(nc.vector.scalar_tensor_tensor(dena[:], den_c, -1.0, dena[:], ALU.mult, ALU.max))
                chain(nc.vector.reciprocal(rdc[:], dena[:]))
                nc.vector.tensor_tensor(hc[:], num[:, :, 0:DH], bc(rdc[:], DH), ALU.mult).then_inc(hc_ready, 1)
                dve.wait_ge(esink_ready, t + 1)
                dve.wait_ge(probs_ready, 4 * (t + 1))
                chain(nc.vector.tensor_tensor(den[:], den[:], esink[:], ALU.add))
                chain(nc.vector.reciprocal(rden[:], den[:]))
                dve.wait_ge(mix_out[j], (i + 1) * 16)
                bank[4].wait_full(dve, t, 2)
                for g in range(HEADS):
                    ins = nc.vector.scalar_tensor_tensor(mx[:, 2 * GW + 64 * g:2 * GW + 64 * g + 64],
                                                         b[4][:, 64 * g:64 * g + 64], sgu_b[:, g:g + 1],
                                                         ge[:, 64 * g:64 * g + 64], ALU.add, ALU.mult)
                    if g < 3:
                        chain(ins)
                    else:
                        ins.then_inc(bank[4].free, 1)
                bank[4].wait_free(dve, t, 3)
                dve.wait_ge(hsq_ready, t + 1)
                nc.vector.tensor_reduce(hss[:], hsq[:], AX.X, ALU.add).then_inc(hss_ready, 1)
                chain(nc.vector.tensor_tensor(hc[:], hc[:], gco[:].rearrange("p (h d) -> p h d", h=HEADS), ALU.mult))
                bank[4].wait_full(dve, t, 3)
                nc.vector.tensor_tensor(mx[:, 0:GW].rearrange("p (h d) -> p h d", h=HEADS),
                                        b[4][:, 0:GW].rearrange("p (h d) -> p h d", h=HEADS), bc(rden[:], DH),
                                        ALU.mult).then_inc(bank[4].free, 1)
                bank[4].wait_free(dve, t + 1, 0)
                dve.wait_ge(hrs_ready, t + 1)
                nc.vector.tensor_tensor(mx[:, GW:2 * GW].rearrange("p (h d) -> p h d", h=HEADS), hc[:],
                                        bc(hrs[:], DH), ALU.mult).then_inc(mix_ready, 1)

            run_slots(dve, slot, lambda: evac_xT(0))

        @block.tensor
        def _(pe):
            pe.wait_ge(weights_in, ALL_IN)
            pe.wait_ge(w_scaled, KD + 1)

            def transpose_x(t):
                pe.wait_ge(xn_ready, t + 3)
                for k in range(2):
                    bank[k].wait_free(pe, t, 0)
                    for c in range(4):
                        ins = nc.tensor.transpose(b[k][:, c * P:(c + 1) * P], xn[:, (4 * k + c) * P:(4 * k + c + 1) * P],
                                                  ident[:])
                    ins.then_inc(bank[k].full, 1)

            def project(t, n):
                c, w = ZCHUNKS[n]
                k, use = n % 2, 1 + n // 2
                if n == 0:
                    bank[1].wait_free(pe, t, 1)
                bank[k].wait_free(pe, t, use)
                for d in range(KD):
                    ins = nc.tensor.matmul(b[k][:, 0:w], xT[:, d, :], w_in[:, d, c:c + w], start=d == 0, stop=d == KD - 1)
                ins.then_inc(bank[k].full, 1)

            def slot(t, j, i, projecting, norming):
                tp = t + 1
                zt = z[j]
                pe.wait_ge(z_ready, (t + 1) * len(ZCHUNKS))
                bank[2].wait_free(pe, t, 0)
                for c in range(3):
                    ins = nc.tensor.transpose(b[2][:, c * P:(c + 1) * P], zt[:, AQ + c * P:AQ + (c + 1) * P], ident[:])
                ins.then_inc(bank[2].full, 1)
                bank[3].wait_free(pe, t, 0)
                for c in range(4):
                    ins = nc.tensor.transpose(b[3][:, c * P:(c + 1) * P], zt[:, CQK + c * P:CQK + (c + 1) * P], ident[:])
                ins.then_inc(bank[3].full, 1)
                if projecting:
                    project(tp, 0)
                bank[4].wait_free(pe, t, 0)
                pe.wait_ge(nlogf_ready, t + 1)
                nc.tensor.matmul(b[4][0:HEADS, 0:P], nlogf[:], tri[:], start=True, stop=True)
                nc.tensor.matmul(b[4][0:HEADS, P:2 * P], nlogf[:], tri[:], start=True, stop=False)
                nc.tensor.matmul(b[4][0:HEADS, P:2 * P], gates[:, 0:4], ident[:], start=False, stop=True)
                nc.tensor.matmul(b[4][:, 2 * P:2 * P + 4], tri[:], nlogf[:], start=True, stop=False)
                nc.tensor.matmul(b[4][:, 2 * P:2 * P + 4], ident[:], gates[:, 0:4], start=False, stop=True)\
                    .then_inc(bank[4].full, 1)
                for e in range(2):
                    bank[2 + e].wait_free(pe, t, 1)
                    for c in range(2):
                        ins = nc.tensor.matmul(b[2 + e][:, c * 2 * P:(c + 1) * 2 * P], qT[64 * e:64 * e + 64, c, :],
                                               kT[64 * e:64 * e + 64].rearrange("p s n -> p (s n)"),
                                               start=True, stop=True)
                    ins.then_inc(bank[2 + e].full, 1)
                if projecting:
                    project(tp, 1)
                bank[4].wait_free(pe, t, 1)
                for h in range(HEADS):
                    ins = nc.tensor.matmul(b[4][:, h * P:(h + 1) * P], sel[:, h, :], m_row[:], start=True, stop=True)
                ins.then_inc(bank[4].full, 1)
                pe.wait_ge(qk_ready, t + 1)
                pe.wait_ge(cn_ready, t + 1)
                for e in range(2):
                    bank[5 + e].wait_free(pe, t, 0)
                    rows = slice(64 * e, 64 * e + 64)
                    for s in range(2):
                        nc.tensor.matmul(b[5 + e][:, s * P:(s + 1) * P], qk[rows, 2 + s, :], qk[rows, s, :],
                                         start=True, stop=True)
                    for s in range(2):
                        ins = nc.tensor.matmul(b[5 + e][:, 2 * P + 65 * s:2 * P + 65 * s + 65], qk[rows, s, :],
                                               cn[rows, s, :], start=True, stop=True)
                    ins.then_inc(bank[5 + e].full, 1)
                bank[7].wait_free(pe, t, 0)
                for s in range(2):
                    ins = nc.tensor.transpose(b[7][:, s * P:(s + 1) * P], qk[:, 2 + s, :], ident[:])
                ins.then_inc(bank[7].full, 1)
                if projecting:
                    project(tp, 2)
                bank[7].wait_free(pe, t, 1)
                pe.wait_ge(rows_ready, 2 * (t + 1))
                pe.wait_ge(wi_last_ready, t + 1)
                nc.tensor.matmul(b[7][:, 0:4], wi_row[:], ident[0:4, 0:4], start=True, stop=True)
                nc.tensor.matmul(b[7][:, 4:8], em_row[:], ident[0:4, 0:4], start=True, stop=True)
                nc.tensor.matmul(b[7][:, 8:10], half[:], wi_last[:], start=True, stop=True).then_inc(bank[7].full, 1)
                if projecting:
                    project(tp, 3)
                pe.wait_ge(vnb_ready, t + 1)
                bank[4].wait_free(pe, t, 2)
                for g in range(HEADS):
                    ins = nc.tensor.matmul(b[4][:, 64 * g:64 * g + 64], sgu_w[:, g, :], vn[:, 64 * g:64 * g + 64],
                                           start=True, stop=True)
                ins.then_inc(bank[4].full, 1)
                pe.wait_ge(wT_ready, t + 1)
                pe.wait_ge(v1_ready, t + 1)
                bank[7].wait_free(pe, t, 2)
                for h in range(HEADS):
                    nc.tensor.matmul(b[7][:, 65 * h:65 * h + 65], wT[:, h, :], v1[:, h, :], start=True, stop=True)
                for h in range(HEADS):
                    lo, s = 64 * (h % 2), h // 2
                    ins = nc.tensor.matmul(b[7][lo:lo + 64, 260 + 65 * s:325 + 65 * s], kw[:, h, :], v1[:, h, :],
                                           start=True, stop=True)
                ins.then_inc(bank[7].full, 1)
                pe.wait_ge(probs_ready, 4 * (t + 1))
                for e in range(2):
                    bank[2 + e].wait_free(pe, t, 2)
                    for n in range(4):
                        ins = nc.tensor.transpose(b[2 + e][:, n * P:(n + 1) * P],
                                                  probs[:, 2 * e + n // 2, (n % 2) * P:(n % 2 + 1) * P], ident[:])
                    ins.then_inc(bank[2 + e].full, 1)
                if projecting:
                    project(tp, 4)
                pe.wait_ge(va_ready, t + 1)
                bank[3].wait_free(pe, t + 1, 0)
                bank[4].wait_free(pe, t, 3)
                for h in range(HEADS):
                    for s in range(2):
                        ins = nc.tensor.matmul(b[4][:, 64 * h:64 * h + 64], pT[:, h, s, :],
                                               va[:, s, 64 * (h // 2):64 * (h // 2) + 64], start=s == 0, stop=s == 1)
                ins.then_inc(bank[4].full, 1)
                if norming:
                    transpose_x(t + 2)

            def prologue():
                transpose_x(0)
                for n in range(len(ZCHUNKS)):
                    project(0, n)
                transpose_x(1)

            run_slots(pe, slot, prologue)


def state_space(nc, io, u_dram, y_dram):
    semaphores = []
    with ExitStack() as ctx:
        ctx.callback(end_phase, nc, semaphores)

        def sb(name, shape, dt=F32):
            return ctx.enter_context(nc.sbuf_tensor(name, shape, dt))

        def sem(name):
            semaphores.append(nc.alloc_semaphore(name=name))
            return semaphores[-1]

        G = GROUPS
        QUAD = 4
        ZM = 2 * L - 9
        PAD = P
        ident = sb("s_ident", [P, P])
        swap = sb("swap_sb", [P, P])
        sign = sb("sign_sb", [P, 1])
        idt = sb("idt_sb", [P, 2 * P])
        dskip = sb("dskip_sb", [P, G])
        are, aim, ldt = sb("are", [P, G]), sb("aim", [P, G]), sb("ldt", [P, G])
        b1, b2 = sb("b1", [P, G, GH]), sb("b2", [P, G, GH])
        c1, c2 = sb("c1", [P, G, GH]), sb("c2", [P, G, GH])
        dt = sb("dt", [P, G])
        ex, en, en2, ei = sb("ex", [P, G]), sb("en", [P, G]), sb("en2", [P, G]), sb("ei", [P, G], I32)
        ep, es = sb("ep", [P, G]), sb("es", [P, G])
        mag, th, sn, cs = sb("mag", [P, G]), sb("th", [P, G]), sb("sn", [P, G]), sb("cs", [P, G])
        pr, pi = sb("pr", [P, L + 1, G]), sb("pi", [P, L + 1, G])
        t1, t2 = sb("t1", [P, 8 * G]), sb("t2", [P, 8 * G])
        qr, qi = sb("qr", [P, LEVELS, G]), sb("qi", [P, LEVELS, G])
        cr, ci = sb("cr", [P, G]), sb("ci", [P, G])
        bb1, bb2 = sb("bb1", [P, G, GH]), sb("bb2", [P, G, GH])
        tb = sb("tb", [P, G, GH])
        zz = sb("zz", [P, G, ZM, GH])
        oo = sb("oo", [P, G, L, GH])
        u = sb("u_sb", [P, CT, L, GW])
        y = sb("y_sb", [P, CT, L, GW])
        zg = [sb(f"zg{e}", [P, ZM, GH]) for e in range(QUAD)]
        ug = [sb(f"ug{e}", [P, CT, L, GH]) for e in range(QUAD)]
        uT = [sb(f"uT{e}", [P, 2, CT * P]) for e in range(QUAD)]
        rg = [sb(f"rg{e}", [P, 2, P]) for e in range(QUAD)]
        tg = [sb(f"tg{e}", [P, 2 * P]) for e in range(QUAD)]
        st = [[sb(f"st{e}{n}", [P, PAD + CH]) for n in range(2)] for e in range(QUAD)]
        rr, ri = sb("rr", [P, L, G]), sb("ri", [P, L, G])
        tz, to = sb("tz", [P, G, L, GH]), sb("to", [P, G, L, GH])

        b = [ctx.enter_context(nc.psum_tensor(f"s_bank{n}", [P, 512], F32)) for n in range(8)]
        uses = [4, 4, 1 + LEVELS, 1 + LEVELS]
        bank = [[Bank(sem(f"s_full{e}{n}"), sem(f"s_free{e}{n}"), uses[n]) for n in range(4)] for e in range(2)]

        def banks_of(e):
            x, second = e % 2, e // 2
            return [(b[4 * x + n], bank[x][n]) for n in (0, 1, 2 + second)] + [second]

        consts_in = sem("s_consts_in")
        u_in = sem("s_u_in")
        y_out = sem("s_y_out")
        pads_set = sem("pads_set")
        sin_arg = sem("sin_arg")
        sin_done = sem("sin_done")
        coeffs = sem("coeffs")
        group_copied = [sem(f"group_copied{e}") for e in range(QUAD)]
        powers_ready, reversed_ready, terms_ready, inputs_ready = (
            sem(n) for n in ("powers_ready", "reversed_ready", "terms_ready", "inputs_ready"))
        chain_sem = sem("s_dve_chain")
        pool_passed = sem("s_pool_passed")
        half_sem = [sem(f"half_level{e}") for e in range(QUAD)]

        LOADS = [(ident, io["ident"]), (swap, io["swap"]), (sign, io["sign"]), (idt, io["idt"]),
                 (dskip, io["dskip"]), (are, io["are"]), (aim, io["aim"]), (ldt, io["ldt"]),
                 (b1, io["b1"]), (b2, io["b2"]), (c1, io["c1"]), (c2, io["c2"])]
        ALL_IN = 16 * len(LOADS)
        u_v = u_dram.rearrange("(t c l) w -> t c l w", c=P, l=L)
        y_v = y_dram.rearrange("(t c l) w -> t c l w", c=P, l=L)
        QUADS = G // QUAD
        per_step = [P, G, L, GH]
        over_steps = lambda v: v[:].unsqueeze(2).to_broadcast(per_step)
        over_channels = lambda v: v.rearrange("p n g -> p g n").unsqueeze(3).to_broadcast(per_step)

        block = ctx.enter_context(nc.Block())

        @block.sync
        def _(sp):
            for dst, src in LOADS:
                sp.dma_start(dst[:], src).then_inc(consts_in, 16)
            for t in range(CT):
                sp.dma_start(u[:, t], u_v[t]).then_inc(u_in, 16)
            for e in range(2):
                bank[e][0].wait_free(sp, QUADS, 0)
            for t in range(CT):
                sp.dma_start(y_v[t], y[:, t]).then_inc(y_out, 16)
            sp.wait_ge(y_out, 16 * CT)

        @block.gpsimd
        def _(pool):
            for e in range(QUAD):
                for n in range(2):
                    nc.gpsimd.memset(st[e][n][:, 0:PAD], 0.0).then_inc(pads_set, 1)
            nc.gpsimd.memset(zz[:, :, L:ZM, :], 0.0).then_inc(pads_set, 1)
            pool.wait_ge(powers_ready, 1)
            nc.gpsimd.tensor_tensor(to[:], over_steps(c2), over_channels(pi[:, 1:L + 1, :]), ALU.mult).then_inc(terms_ready, 1)
            pool.wait_ge(reversed_ready, 2 * L)
            pool.wait_ge(inputs_ready, 1)
            nc.gpsimd.tensor_tensor(tz[:], over_steps(bb2), over_channels(ri[:]), ALU.mult).then_inc(terms_ready, 1)
            pool.wait_ge(u_in, 16 * CT)
            pool.wait_ge(coeffs, 1)
            pool.wait_ge(pads_set, 2 * QUAD + 1)
            with pool.Fori(0, QUADS) as i:
                for e in range(QUAD):
                    banks_of(e)[1][1].wait_free(pool, i, 0)
                    pass_wait(pool, pool_passed)
                    nc.gpsimd.tensor_copy(zg[e][:], zz[:, bass.ds(i * QUAD + e, 1), :, :].rearrange("p a m h -> p (a m) h"))\
                        .then_inc(group_copied[e], 1)
                    nc.gpsimd.tensor_copy(ug[e][:].rearrange("p t l h -> p (t l) h"),
                                          u[:, :, :, bass.ds((i * QUAD + e) * GH, GH)].rearrange("p t l h -> p (t l) h"))\
                        .then_inc(group_copied[e], 1)

        @block.scalar
        def _(act):
            act.wait_ge(sin_arg, 1)
            nc.scalar.activation(sn[:], th[:], ACT.Sin).then_inc(sin_done, 1)
            nc.scalar.activation(cs[:], th[:], ACT.Sin, scale=0.5).then_inc(sin_done, 1)
            act.wait_ge(powers_ready, 1)
            for n in range(L):
                nc.scalar.activation(rr[:, n, :], pr[:, L - 1 - n, :], ACT.Copy).then_inc(reversed_ready, 1)
                nc.scalar.activation(ri[:, n, :], pi[:, L - 1 - n, :], ACT.Copy).then_inc(reversed_ready, 1)
            with act.Fori(0, QUADS) as i:
                for second in range(2):
                    pair = range(2 * second, 2 * second + 2)
                    for e in pair:
                        (B0, bank0), (B1, bank1), (B2, bank2), _ = banks_of(e)
                        bank0.wait_full(act, i, second)
                        nc.scalar.activation(uT[e][:], B0[:].rearrange("p (k n) -> p k n", k=2), ACT.Copy)\
                            .then_inc(bank0.free, 1)
                        bank1.wait_full(act, i, 2 * second)
                        nc.scalar.activation(rg[e][:], B1[:, 0:2 * P].rearrange("p (k n) -> p k n", k=2), ACT.Copy)\
                            .then_inc(bank1.free, 1)
                    for e in pair:
                        (B0, bank0), (B1, bank1), (B2, bank2), _ = banks_of(e)
                        bank2.wait_full(act, i, 0)
                        nc.scalar.activation(st[e][0][:, PAD:PAD + CH], B2[:, 0:CH], ACT.Copy).then_inc(bank2.free, 1)
                for e in range(QUAD):
                    (B0, bank0), (B1, bank1), (B2, bank2), second = banks_of(e)
                    bank0.wait_full(act, i, 2 + second)
                    nc.scalar.activation(y[:, :, :, bass.ds((i * QUAD + e) * GH, GH)].rearrange("p t l h -> p (t l) h"),
                                         B0[:].rearrange("p (a h) -> p a h", h=GH), ACT.Copy).then_inc(bank0.free, 1)

        @block.vector
        def _(dve):
            chain = Chain(dve, chain_sem)
            for e in range(2):
                for k in bank[e]:
                    dve.sem_inc(k.free, 1)
            dve.wait_ge(consts_in, ALL_IN)
            V = nc.vector

            def rint(out, x):
                chain(V.tensor_scalar(out, x, 12582912.0, None, ALU.add))
                chain(V.tensor_scalar(out, out, 12582912.0, None, ALU.subtract))

            def exp(out, x):
                chain(V.tensor_scalar(ex[:], x, -104.0, 89.0, ALU.max, ALU.min))
                chain(V.tensor_scalar(en[:], ex[:], 1.4426950408889634, None, ALU.mult))
                rint(en[:], en[:])
                chain(V.scalar_tensor_tensor(ex[:], en[:], -0.693359375, ex[:], ALU.mult, ALU.add))
                chain(V.scalar_tensor_tensor(ex[:], en[:], 2.12194440e-4, ex[:], ALU.mult, ALU.add))
                chain(V.tensor_scalar(ep[:], ex[:], 1.0 / 40320, None, ALU.mult))
                for c in (5040, 720, 120, 24, 6, 2, 1):
                    chain(V.scalar_tensor_tensor(ep[:], ep[:], 1.0 / c, ex[:], ALU.add, ALU.mult))
                chain(V.tensor_scalar(ep[:], ep[:], 1.0, None, ALU.add))
                chain(V.tensor_scalar(en2[:], en[:], 0.5, None, ALU.mult))
                rint(en2[:], en2[:])
                chain(V.tensor_tensor(en[:], en[:], en2[:], ALU.subtract))
                for n in (en, en2):
                    chain(V.tensor_scalar(es[:], n[:], 127.0, 8388608.0, ALU.add, ALU.mult))
                    chain(V.tensor_copy(ei[:], es[:]))
                    chain(V.tensor_tensor(ep[:], ep[:], ei[:].bitcast(F32), ALU.mult))
                chain(V.tensor_copy(out, ep[:]))

            def cmul(outr, outi, ar, ai, br, bi, sr, si):
                chain(V.tensor_tensor(sr, ai, bi, ALU.mult))
                chain(V.tensor_tensor(si, ar, bi, ALU.mult))
                chain(V.tensor_tensor(outr, ar, br, ALU.mult))
                chain(V.tensor_tensor(outi, ai, br, ALU.mult))
                chain(V.tensor_tensor(outr, outr, sr, ALU.subtract))
                chain(V.tensor_tensor(outi, outi, si, ALU.add))

            flat = lambda a: a[:].rearrange("p g h -> p (g h)")
            chain(V.tensor_scalar(flat(b2), flat(b2), sign[:, 0:1], None, ALU.mult))
            chain(V.tensor_scalar(flat(c1), flat(c1), sign[:, 0:1], -1.0, ALU.mult, ALU.mult))
            chain(V.tensor_scalar(flat(c2), flat(c2), -1.0, None, ALU.mult))
            exp(dt[:], ldt[:])
            chain(V.tensor_tensor(mag[:], are[:], dt[:], ALU.mult))
            exp(mag[:], mag[:])
            chain(V.tensor_tensor(th[:], aim[:], dt[:], ALU.mult))
            chain(V.tensor_scalar(en[:], th[:], 0.15915494309189535, None, ALU.mult))
            rint(en[:], en[:])
            chain(V.scalar_tensor_tensor(th[:], en[:], -6.28125, th[:], ALU.mult, ALU.add))
            chain(V.scalar_tensor_tensor(th[:], en[:], -0.0019340515136718750, th[:], ALU.mult, ALU.add))
            chain(V.scalar_tensor_tensor(th[:], en[:], -1.2556659146e-06, th[:], ALU.mult, ALU.add))
            V.tensor_scalar(th[:], th[:], 3.1415925, -3.1415925, ALU.min, ALU.max).then_inc(sin_arg, 1)
            dve.wait_ge(sin_done, 2)
            chain(V.tensor_tensor(cs[:], cs[:], cs[:], ALU.mult))
            chain(V.tensor_scalar(cs[:], cs[:], -2.0, 1.0, ALU.mult, ALU.add))
            chain(V.memset(pr[:, 0, :], 1.0))
            chain(V.memset(pi[:, 0, :], 0.0))
            chain(V.tensor_tensor(pr[:, 1, :], mag[:], cs[:], ALU.mult))
            chain(V.tensor_tensor(pi[:, 1, :], mag[:], sn[:], ALU.mult))
            n = 1
            while n < L:
                shape = [P, n, G]
                s1 = t1[:, 0:n * G].rearrange("p (n g) -> p n g", g=G)
                s2 = t2[:, 0:n * G].rearrange("p (n g) -> p n g", g=G)
                cmul(pr[:, n + 1:2 * n + 1, :], pi[:, n + 1:2 * n + 1, :], pr[:, 1:n + 1, :], pi[:, 1:n + 1, :],
                     pr[:, n:n + 1, :].to_broadcast(shape), pi[:, n:n + 1, :].to_broadcast(shape), s1, s2)
                n *= 2
            dve.sem_inc(powers_ready, 1)
            chain(V.tensor_copy(qr[:, 0, :], pr[:, L, :]))
            chain(V.tensor_copy(qi[:, 0, :], pi[:, L, :]))
            for n in range(1, LEVELS):
                cmul(qr[:, n, :], qi[:, n, :], qr[:, n - 1, :], qi[:, n - 1, :], qr[:, n - 1, :], qi[:, n - 1, :],
                     t1[:, 0:G], t2[:, 0:G])
            chain(V.tensor_scalar(qi[:].rearrange("p n g -> p (n g)"), qi[:].rearrange("p n g -> p (n g)"),
                                  sign[:, 0:1], None, ALU.mult))
            chain(V.tensor_tensor(t1[:, 0:G], are[:], are[:], ALU.mult))
            chain(V.tensor_tensor(t2[:, 0:G], aim[:], aim[:], ALU.mult))
            chain(V.tensor_tensor(t1[:, 0:G], t1[:, 0:G], t2[:, 0:G], ALU.add))
            chain(V.reciprocal(t1[:, 0:G], t1[:, 0:G]))
            chain(V.tensor_tensor(t2[:, 0:G], are[:], t1[:, 0:G], ALU.mult))
            chain(V.scalar_tensor_tensor(t1[:, 0:G], aim[:], -1.0, t1[:, 0:G], ALU.mult, ALU.mult))
            chain(V.tensor_scalar(ex[:], pr[:, 1, :], 1.0, None, ALU.subtract))
            cmul(cr[:], ci[:], ex[:], pi[:, 1, :], t2[:, 0:G], t1[:, 0:G], en[:], en2[:])
            wide = [P, G, GH]
            crb, cib = cr[:].unsqueeze(2).to_broadcast(wide), ci[:].unsqueeze(2).to_broadcast(wide)
            chain(V.tensor_tensor(bb1[:], b1[:], crb, ALU.mult))
            chain(V.tensor_tensor(tb[:], b2[:], cib, ALU.mult))
            chain(V.tensor_tensor(bb1[:], bb1[:], tb[:], ALU.add))
            chain(V.tensor_tensor(bb2[:], b2[:], crb, ALU.mult))
            chain(V.tensor_tensor(tb[:], b1[:], cib, ALU.mult))
            chain(V.tensor_tensor(bb2[:], bb2[:], tb[:], ALU.subtract))
            dve.sem_inc(inputs_ready, 1)
            chain(V.tensor_tensor(oo[:], over_steps(c1), over_channels(pr[:, 1:L + 1, :]), ALU.mult))
            dve.wait_ge(reversed_ready, 2 * L)
            chain(V.tensor_tensor(zz[:, :, 0:L, :], over_steps(bb1), over_channels(rr[:]), ALU.mult))
            dve.wait_ge(terms_ready, 1)
            chain(V.tensor_tensor(oo[:], oo[:], to[:], ALU.add))
            dve.wait_ge(terms_ready, 2)
            chain(V.tensor_tensor(zz[:, :, 0:L, :], zz[:, :, 0:L, :], tz[:], ALU.add))
            dve.sem_inc(coeffs, 1)
            dve.wait_ge(pads_set, 2 * QUAD + 1)
            with dve.Fori(0, QUADS) as i:
                for e in range(QUAD):
                    (B0, bank0), (B1, bank1), (B2, bank2), second = banks_of(e)
                    bank1.wait_full(dve, i, 2 * second + 1)
                    V.scalar_tensor_tensor(tg[e][:], idt[:], dskip[:, bass.ds(i * QUAD + e, 1)], B1[:, 0:2 * P],
                                           ALU.mult, ALU.add).then_inc(bank1.free, 1)
                for n in range(LEVELS):
                    d = 1 << n
                    now, before = slice(PAD, PAD + CH), slice(PAD - d, PAD + CH - d)
                    for e in range(QUAD):
                        banks_of(e)[2][1].wait_free(dve, i, 1 + n)
                        x, out = st[e][n % 2], st[e][(n + 1) % 2]
                        V.scalar_tensor_tensor(out[:, now], x[:, before], qr[:, n, bass.ds(i * QUAD + e, 1)], x[:, now],
                                               ALU.mult, ALU.add).then_inc(half_sem[e], 1)
                    for e in range(QUAD):
                        B2, bank2 = banks_of(e)[2]
                        out = st[e][(n + 1) % 2]
                        bank2.wait_full(dve, i, 1 + n)
                        dve.wait_ge(half_sem[e], i * LEVELS + n + 1)
                        V.scalar_tensor_tensor(out[:, now], B2[:, 0:CH], qi[:, n, bass.ds(i * QUAD + e, 1)],
                                               out[:, now], ALU.mult, ALU.add).then_inc(bank2.free, 1)

        @block.tensor
        def _(pe):
            pe.wait_ge(coeffs, 1)

            def transposes(e, i):
                (B0, bank0), (B1, bank1), (B2, bank2), second = banks_of(e)
                pe.wait_ge(group_copied[e], 2 * (i + 1))
                bank0.wait_free(pe, i, second)
                for k in range(2):
                    for t in range(CT):
                        ins = nc.tensor.transpose(B0[:, (k * CT + t) * P:(k * CT + t + 1) * P],
                                                  ug[e][:, t, 8 * k:8 * k + 8, :], ident[:])
                ins.then_inc(bank0.full, 1)
                bank1.wait_free(pe, i, 2 * second)
                for k in range(2):
                    ins = nc.tensor.transpose(B1[:, k * P:(k + 1) * P], zg[e][:, 8 * k:8 * k + 8, :], ident[:])
                ins.then_inc(bank1.full, 1)

            def states_and_toeplitz(e, i):
                (B0, bank0), (B1, bank1), (B2, bank2), second = banks_of(e)
                bank0.wait_free(pe, i, second + 1)
                bank1.wait_free(pe, i, 2 * second + 1)
                bank2.wait_free(pe, i, 0)
                for k in range(2):
                    ins = nc.tensor.matmul(B2[:, 0:CH], rg[e][:, k, :], uT[e][:, k, :], start=k == 0, stop=k == 1)
                ins.then_inc(bank2.full, 1)
                for n in range(L // 2):
                    m = L - 1 - n
                    nc.tensor.matmul(B1[:, n * GH:(n + 1) * GH], zg[e][:, m:m + 8, :],
                                     c1[:, bass.ds(i * QUAD + e, 1), :].rearrange("p a h -> p (a h)"),
                                     start=True, stop=True)
                nc.tensor.matmul(B1[:, P:2 * P], zg[e][:, L // 2:L, :],
                                 oo[:, bass.ds(i * QUAD + e, 1), 0:L // 2, :].rearrange("p a l h -> p (a l h)"),
                                 start=True, stop=True).then_inc(bank1.full, 1)

            def outputs(e, i):
                (out, bank0), (B1, bank1), (B2, bank2), second = banks_of(e)
                bank0.wait_free(pe, i, 2 + second)
                bank1.wait_free(pe, i + 1, 0)
                bank2.wait_free(pe, i + 1, 0)
                last = LEVELS % 2
                for t in range(CT):
                    c = slice(t * P, (t + 1) * P)
                    nc.tensor.matmul(out[:, t * 2 * P:(t + 1) * 2 * P], uT[e][:, 0, c], tg[e][:, 0:2 * P],
                                     start=True, stop=False)
                    nc.tensor.matmul(out[:, t * 2 * P + P:(t + 1) * 2 * P], uT[e][:, 1, c], tg[e][:, 0:P],
                                     start=False, stop=False)
                    ins = nc.tensor.matmul(out[:, t * 2 * P:(t + 1) * 2 * P],
                                           st[e][last][:, PAD - 1 + t * P:PAD - 1 + (t + 1) * P],
                                           oo[:, bass.ds(i * QUAD + e, 1), :, :].rearrange("p a l h -> p (a l h)"),
                                           start=False, stop=True)
                ins.then_inc(bank0.full, 1)

            with pe.Fori(0, QUADS) as i:
                for second in range(2):
                    pair = range(2 * second, 2 * second + 2)
                    for e in pair:
                        transposes(e, i)
                    for e in pair:
                        states_and_toeplitz(e, i)
                for n in range(LEVELS):
                    for e in range(QUAD):
                        B2, bank2 = banks_of(e)[2]
                        bank2.wait_free(pe, i, 1 + n)
                        nc.tensor.matmul(B2[:, 0:CH], swap[:], st[e][n % 2][:, PAD - (1 << n):PAD - (1 << n) + CH],
                                         start=True, stop=True).then_inc(bank2.full, 1)
                for e in range(QUAD):
                    outputs(e, i)


def merge_and_route(nc, io, mix_dram, y_dram, x2_dram, xn_dram, logits):
    semaphores = []
    with ExitStack() as ctx:
        ctx.callback(end_phase, nc, semaphores)

        def sb(name, shape, dt=F32):
            return ctx.enter_context(nc.sbuf_tensor(name, shape, dt))

        def sem(name):
            semaphores.append(nc.alloc_semaphore(name=name))
            return semaphores[-1]

        R = NG + NE
        ident = sb("m_ident", [P, P])
        w_out = sb("w_out_sb", [P, KD, D])
        w_hi, w_lo = sb("m_w_hi", [P, KD, D], F32R), sb("m_w_lo", [P, KD, D], F32R)
        glu_w = sb("glu_w_sb", [P, 2, GW])
        glu_b = sb("glu_b_sb", [P, GW])
        w_r = sb("w_r_sb", [P, KD, R])
        b_r = sb("b_r_sb", [P, R])
        g_ffn = sb("m_g_ffn", [P, D])
        minus_half, eps = sb("m_minus_half", [P, 1]), sb("m_eps", [P, 1])
        xb = [sb(f"m_x{j}", [P, D]) for j in range(2)]
        mix = [sb(f"m_mix{j}", [P, D]) for j in range(2)]
        yb = [sb(f"m_y{j}", [P, GW]) for j in range(2)]
        ysq, yin, yth = sb("ysq", [P, GW]), sb("yin", [P, GW]), sb("yth", [P, GW])
        gy = [sb(f"gy{j}", [P, GW]) for j in range(2)]
        gyT = sb("gyT", [P, 2, P])
        gate, gate_th = sb("gate", [P, GW]), sb("gate_th", [P, GW])
        mT_hi, mT_lo = sb("mT_hi", [P, KD, P], F32R), sb("mT_lo", [P, KD, P], F32R)
        x2 = [sb(f"m_x2{j}", [P, D]) for j in range(2)]
        xn = [sb(f"m_xn{j}", [P, D]) for j in range(2)]
        sq = sb("m_sq", [P, D])
        ss, rs = sb("m_ss", [P, 1]), sb("m_rs", [P, 1])
        xnT = sb("xnT", [P, KD, P])

        b = [ctx.enter_context(nc.psum_tensor(f"m_bank{n}", [P, 512], F32)) for n in range(8)]
        uses = [1, 1, 1, 1, 2, 1, 1, 1]
        bank = [Bank(sem(f"m_full{n}"), sem(f"m_free{n}"), uses[n]) for n in range(8)]
        MIXT, PROD, GLU, LOGIT, XNT = 0, 2, 4, 5, 6

        small_in, w_in, w_hi_ready, w_lo_ready = (sem(n) for n in ("m_small_in", "m_w_in", "m_w_hi_ready", "m_w_lo_ready"))
        half_set = sem("m_half_set")
        x_in = [sem(f"m_x_in{j}") for j in range(2)]
        mix_in = [sem(f"m_mix_in{j}") for j in range(2)]
        y_in = [sem(f"m_y_in{j}") for j in range(2)]
        x2_out = [sem(f"m_x2_out{j}") for j in range(2)]
        xn_out = [sem(f"m_xn_out{j}") for j in range(2)]
        ysq_ready, yin_ready, yth_ready, gy_ready = sem("ysq_ready"), sem("yin_ready"), sem("yth_ready"), sem("gy_ready")
        gate_ready, gate_th_ready, gated_ready = sem("gate_ready"), sem("gate_th_ready"), sem("gated_ready")
        mT_hi_ready = sem("mT_hi_ready")
        x2_ready, sq_ready, rs_ready, xn_ready = sem("m_x2_ready"), sem("m_sq_ready"), sem("m_rs_ready"), sem("m_xn_ready")
        norm_chain = sem("m_norm_chain")

        SMALL = [(ident, io["ident"]), (glu_w, io["glu_w"]), (glu_b, io["glu_b"]), (w_r, io["w_r"]), (b_r, io["b_r"]),
                 (g_ffn, io["g_ffn"])]
        factor = lambda k: (1.0, 0.5, 0.5, 0.25)[k // 2]
        tiled = lambda dram: dram.rearrange("(t p) d -> t p d", p=P)
        x_t, mix_t, y_t, x2_t, xn_t = map(tiled, (io["x"], mix_dram, y_dram, x2_dram, xn_dram))
        at = lambda dram, t: dram[bass.ds(t, 1)].rearrange("a p d -> (a p) d")
        fixed = lambda t: isinstance(t, int)
        has = lambda t: not fixed(t) or 0 <= t < TILES

        def run_slots(engine, prologue, slot, epilogue, last=2):
            prologue()
            for t in range(2):
                slot(t, t, 0)
            with engine.Fori(0, (TILES - 2 - last) // 2) as i:
                slot(i * 2 + 2, 0, i + 1)
                slot(i * 2 + 3, 1, i + 1)
            for t in range(TILES - last, TILES):
                slot(t, t % 2, t // 2)
            epilogue()

        nothing = lambda: None
        block = ctx.enter_context(nc.Block())

        @block.sync
        def _(sp):
            def load_y(t, j):
                sp.wait_ge(gy_ready, t + 1)
                sp.dma_start(yb[j][:], at(y_t, t)).then_inc(y_in[j], 16)

            def load_mix(t, j):
                if not (fixed(t) and t < 2):
                    for k in range(2):
                        bank[MIXT + k].wait_full(sp, t - 2, 0)
                sp.dma_start(mix[j][:, 0:3 * GW], at(mix_t, t)).then_inc(mix_in[j], 16)

            def load_x(t, j):
                sp.wait_ge(x2_ready, t + 1)
                sp.dma_start(xb[j][:], at(x_t, t)).then_inc(x_in[j], 16)

            def prologue():
                load_y(0, 0)
                load_y(1, 1)
                for dst, src in SMALL:
                    sp.dma_start(dst[:], src).then_inc(small_in, 16)
                for k in range(KD):
                    sp.dma_start(w_out[:, k, :], io["w_out"][:, k, :]).then_inc(w_in, 16)
                load_mix(0, 0)
                load_mix(1, 1)
                load_x(0, 0)
                load_y(2, 0)

            def slot(t, j, i):
                if not fixed(t) or t + 3 < TILES:
                    load_y(t + 3, 1 - j)
                if has(t + 2):
                    load_mix(t + 2, j)
                if has(t + 1):
                    load_x(t + 1, 1 - j)
                sp.wait_ge(x2_ready, t + 3)
                sp.dma_start(at(x2_t, t), x2[j][:]).then_inc(x2_out[j], 16)
                sp.wait_ge(xn_ready, t + 1)
                sp.dma_start(at(xn_t, t), xn[j][:]).then_inc(xn_out[j], 16)

            def epilogue():
                for j in range(2):
                    sp.wait_ge(x2_out[j], 16 * (TILES // 2 + 1))
                    sp.wait_ge(xn_out[j], 16 * (TILES // 2 + 1))

            run_slots(sp, prologue, slot, epilogue, last=4)

        @block.gpsimd
        def _(pool):
            nchain = Chain(pool, norm_chain, 1)
            pool.sem_inc(x2_ready, 2)
            pool.sem_inc(gy_ready, 2)
            for j in range(2):
                pool.sem_inc(x2_out[j], 16)
                pool.sem_inc(xn_out[j], 16)
            nc.gpsimd.memset(minus_half[:], -0.5).then_inc(half_set, 1)
            nc.gpsimd.memset(eps[:], EPS).then_inc(half_set, 1)
            pool.wait_ge(half_set, 2)

            def slot(t, j, i):
                nchain.tile(t)
                if not (fixed(t) and t == 0):
                    pool.wait_ge(xn_ready, t)
                pool.wait_ge(sq_ready, t + 1)
                nchain(nc.gpsimd.tensor_tensor(rs[:], ss[:], eps[:], ALU.add))
                nc.gpsimd.tensor_tensor(rs[:], rs[:], minus_half[:], ALU.pow).then_inc(rs_ready, 1)

            run_slots(pool, nothing, slot, nothing)

        @block.scalar
        def _(act):
            def square_y(t, j, i):
                act.wait_ge(y_in[j], (i + 1) * 16)
                if not (fixed(t) and t == 0):
                    act.wait_ge(yin_ready, t)
                nc.scalar.activation(ysq[:], yb[j][:], ACT.Square, scale=GELU_A ** 0.5).then_inc(ysq_ready, 1)

            def gelu(t):
                act.wait_ge(yin_ready, t + 1)
                act.wait_ge(gy_ready, t + 2)
                nc.scalar.activation(yth[:], yin[:], ACT.Tanh, scale=GELU_B).then_inc(yth_ready, 1)

            def evac_gyT(t):
                bank[GLU].wait_full(act, t, 0)
                nc.scalar.activation(gyT[:], b[GLU][:, 0:2 * P].rearrange("p (k n) -> p k n", k=2), ACT.Copy)\
                    .then_inc(bank[GLU].free, 1)

            def gate_tanh(t):
                act.wait_ge(gate_ready, t + 1)
                nc.scalar.activation(gate_th[:], gate[:], ACT.Tanh, scale=0.5).then_inc(gate_th_ready, 1)

            def evac_mT(t):
                for k in range(2):
                    bank[MIXT + k].wait_full(act, t, 0)
                    nc.scalar.activation(mT_hi[:, 4 * k:4 * k + 4, :], b[MIXT + k][:].rearrange("p (k n) -> p k n", k=4),
                                         ACT.Copy).then_inc(mT_hi_ready, 1)

            def evac_xnT(t):
                bank[XNT].wait_full(act, t, 0)
                nc.scalar.activation(xnT[:, 0:4, :], b[XNT][:].rearrange("p (k n) -> p k n", k=4), ACT.Copy)\
                    .then_inc(bank[XNT].free, 1)

            def slot(t, j, i):
                if has(t - 2):
                    evac_xnT(t - 2)
                if has(t + 2):
                    square_y(t + 2, j, i + 1)
                if has(t + 1):
                    gate_tanh(t + 1)
                if has(t + 2):
                    gelu(t + 2)
                    evac_gyT(t + 2)
                act.wait_ge(x2_ready, t + 3)
                nc.scalar.activation(sq[:], x2[j][:], ACT.Square, scale=D ** -0.5, accum_out=ss[:]).then_inc(sq_ready, 1)
                if has(t + 1):
                    evac_mT(t + 1)

            def prologue():
                for t in range(2):
                    square_y(t, t, 0)
                    gelu(t)
                    evac_gyT(t)
                    if t == 0:
                        for k in range(KD):
                            act.wait_ge(w_in, 16 * KD)
                            nc.scalar.activation(w_hi[:, k, :], w_out[:, k, :], ACT.Copy, scale=factor(k))\
                                .then_inc(w_hi_ready, 1)
                        gate_tanh(0)
                        evac_mT(0)

            def epilogue():
                for t in range(TILES - 2, TILES):
                    evac_xnT(t)

            run_slots(act, prologue, slot, epilogue)

        @block.vector
        def _(dve):
            V = nc.vector
            for k in bank:
                dve.sem_inc(k.free, 1)

            def gelu_arg(t, j):
                dve.wait_ge(ysq_ready, t + 1)
                V.scalar_tensor_tensor(yin[:], ysq[:], 1.0, yb[j][:], ALU.add, ALU.mult).then_inc(yin_ready, 1)

            def gelu(t, j):
                dve.wait_ge(yth_ready, t + 1)
                V.scalar_tensor_tensor(gy[j][:], yth[:], 1.0, yb[j][:], ALU.add, ALU.mult).then_inc(gy_ready, 1)

            def gate_arg(t):
                bank[GLU].wait_full(dve, t, 1)
                V.scalar_tensor_tensor(gate[:], b[GLU][:, 0:GW], 0.5, glu_b[:], ALU.mult, ALU.add)\
                    .then_inc(bank[GLU].free, 1)
                bank[GLU].wait_free(dve, t + 1, 0)
                dve.sem_inc(gate_ready, 1)

            def gated(t, j):
                dve.wait_ge(gate_th_ready, t + 1)
                V.scalar_tensor_tensor(mix[j][:, 3 * GW:D], gate_th[:], 1.0, gy[j][:], ALU.add, ALU.mult)\
                    .then_inc(gated_ready, 1)

            def evac_mT(t):
                for k in range(2):
                    part = slice(4 * k, 4 * k + 4)
                    bank[MIXT + k].wait_full(dve, t, 0)
                    dve.wait_ge(mT_hi_ready, t * 2 + (k + 1))
                    V.tensor_tensor(mT_lo[:, part, :], b[MIXT + k][:].rearrange("p (k n) -> p k n", k=4),
                                    mT_hi[:, part, :], ALU.subtract).then_inc(bank[MIXT + k].free, 1)

            def evac_xnT(t):
                bank[XNT + 1].wait_full(dve, t, 0)
                V.tensor_copy(xnT[:, 4:8, :], b[XNT + 1][:].rearrange("p (k n) -> p k n", k=4))\
                    .then_inc(bank[XNT + 1].free, 1)

            def logit(t):
                bank[LOGIT].wait_full(dve, t, 0)
                V.tensor_tensor(logits[:, bass.ds(t, 1), :].rearrange("p a r -> p (a r)"), b[LOGIT][:, 0:R], b_r[:],
                                ALU.add).then_inc(bank[LOGIT].free, 1)

            def slot(t, j, i):
                if has(t - 2):
                    evac_xnT(t - 2)
                if has(t + 1):
                    gate_arg(t + 1)
                if has(t + 2):
                    gelu_arg(t + 2, j)
                if has(t + 1):
                    gated(t + 1, 1 - j)
                if has(t + 2):
                    gelu(t + 2, j)
                dve.wait_ge(x_in[j], (i + 1) * 16)
                dve.wait_ge(x2_out[j], (i + 1) * 16)
                for n in range(2):
                    bank[PROD + n].wait_full(dve, t, 0)
                    V.tensor_tensor(x2[j][:, n * 512:(n + 1) * 512], b[PROD + n][:], xb[j][:, n * 512:(n + 1) * 512],
                                    ALU.add).then_inc(bank[PROD + n].free, 1)
                for n in range(2):
                    bank[PROD + n].wait_free(dve, t + 1, 0)
                dve.sem_inc(x2_ready, 1)
                if has(t - 2):
                    logit(t - 2)
                if has(t + 1):
                    evac_mT(t + 1)
                dve.wait_ge(xn_out[j], (i + 1) * 16)
                dve.wait_ge(rs_ready, t + 1)
                V.scalar_tensor_tensor(xn[j][:], x2[j][:], rs[:, 0:1], g_ffn[:], ALU.mult, ALU.mult)\
                    .then_inc(xn_ready, 1)

            def prologue():
                for t in range(2):
                    gelu_arg(t, t)
                    gelu(t, t)
                    if t == 0:
                        for k in range(KD):
                            dve.wait_ge(w_hi_ready, k + 1)
                            V.scalar_tensor_tensor(w_lo[:, k, :], w_out[:, k, :], factor(k), w_hi[:, k, :], ALU.mult,
                                                   ALU.subtract).then_inc(w_lo_ready, 1)
                        dve.wait_ge(small_in, 16 * len(SMALL))
                        gate_arg(0)
                        gated(0, 0)
                        evac_mT(0)

            def epilogue():
                for t in range(TILES - 2, TILES):
                    evac_xnT(t)
                    logit(t)

            run_slots(dve, prologue, slot, epilogue)

        @block.tensor
        def _(pe):
            def glu_transpose(t, j):
                pe.wait_ge(gy_ready, t + 3)
                bank[GLU].wait_free(pe, t, 0)
                for c in range(2):
                    ins = nc.tensor.transpose(b[GLU][:, c * P:(c + 1) * P], gy[j][:, c * P:(c + 1) * P], ident[:])
                ins.then_inc(bank[GLU].full, 1)

            def glu_product(t):
                bank[GLU].wait_free(pe, t, 1)
                for c in range(2):
                    ins = nc.tensor.matmul(b[GLU][:, 0:GW], gyT[:, c, :], glu_w[:, c, :], start=c == 0, stop=c == 1)
                ins.then_inc(bank[GLU].full, 1)

            def mix_transpose(t, j, i):
                pe.wait_ge(gated_ready, t + 1)
                pe.wait_ge(mix_in[j], (i + 1) * 16)
                for k in range(2):
                    bank[MIXT + k].wait_free(pe, t, 0)
                    for c in range(4):
                        ins = nc.tensor.transpose(b[MIXT + k][:, c * P:(c + 1) * P],
                                                  mix[j][:, (4 * k + c) * P:(4 * k + c + 1) * P], ident[:])
                    ins.then_inc(bank[MIXT + k].full, 1)

            def xn_transpose(t, j):
                pe.wait_ge(xn_ready, t + 1)
                for k in range(2):
                    bank[XNT + k].wait_free(pe, t, 0)
                    for c in range(4):
                        ins = nc.tensor.transpose(b[XNT + k][:, c * P:(c + 1) * P],
                                                  xn[j][:, (4 * k + c) * P:(4 * k + c + 1) * P], ident[:])
                    ins.then_inc(bank[XNT + k].full, 1)

            def route(t):
                bank[XNT].wait_free(pe, t + 1, 0)
                bank[XNT + 1].wait_free(pe, t + 1, 0)
                bank[LOGIT].wait_free(pe, t, 0)
                for k in range(KD):
                    ins = nc.tensor.matmul(b[LOGIT][:, 0:R], xnT[:, k, :], w_r[:, k, :], start=k == 0, stop=k == KD - 1)
                ins.then_inc(bank[LOGIT].full, 1)

            def product(t, n):
                if n == 0:
                    for k in range(2):
                        bank[MIXT + k].wait_free(pe, t + 1, 0)
                bank[PROD + n].wait_free(pe, t, 0)
                cols = slice(n * 512, (n + 1) * 512)
                for k in range(KD):
                    nc.tensor.matmul(b[PROD + n][:], mT_hi[:, k, :], w_hi[:, k, cols], start=k == 0, stop=False)
                    nc.tensor.matmul(b[PROD + n][:], mT_hi[:, k, :], w_lo[:, k, cols], start=False, stop=False)
                    ins = nc.tensor.matmul(b[PROD + n][:], mT_lo[:, k, :], w_hi[:, k, cols], start=False,
                                           stop=k == KD - 1)
                ins.then_inc(bank[PROD + n].full, 1)

            def slot(t, j, i):
                product(t, 0)
                if has(t + 2):
                    glu_transpose(t + 2, j)
                product(t, 1)
                if has(t - 2):
                    route(t - 2)
                if has(t + 1):
                    mix_transpose(t + 1, 1 - j, i + j)
                if has(t + 2):
                    glu_product(t + 2)
                if has(t - 1):
                    xn_transpose(t - 1, 1 - j)

            def prologue():
                pe.wait_ge(small_in, 16 * len(SMALL))
                glu_transpose(0, 0)
                glu_product(0)
                mix_transpose(0, 0, 0)
                glu_transpose(1, 1)
                glu_product(1)
                pe.wait_ge(w_lo_ready, KD)

            def epilogue():
                route(TILES - 2)
                xn_transpose(TILES - 1, 1)
                route(TILES - 1)

            run_slots(pe, prologue, slot, epilogue)


def plan_experts(nc, io, logits, wts, dest, block_rows, block_expert, block_slot, expert_end, table_dram):
    semaphores = []
    with ExitStack() as ctx:
        ctx.callback(end_phase, nc, semaphores)

        def sb(name, shape, dt=F32):
            return ctx.enter_context(nc.sbuf_tensor(name, shape, dt))

        def sem(name):
            semaphores.append(nc.alloc_semaphore(name=name))
            return semaphores[-1]

        T = TILES
        before = sb("p_before", [P, P])
        ones = sb("p_ones", [P, P])
        reset = sb("p_reset", [P, NE * T])
        rank4, rank8 = sb("rank4", [P, NG]), sb("rank8", [P, NE_G])
        block_no = sb("block_no", [1, BLOCKS])
        gm, mv, sh = sb("p_gm", [P, T]), sb("p_mv", [P, T]), sb("p_sh", [P, T, NG])
        ohg, vg = sb("ohg", [P, T, NG]), sb("vg", [P, T, NG])
        eg, pg = sb("eg", [P, T, NG]), sb("pg", [P, T])
        big = sb("p_big", [P, T, NG, NE_G])
        ein, v8 = sb("ein", [P, T, NE_G]), sb("v8", [P, T, NE_G])
        m1, m2 = sb("m1", [P, T]), sb("m2", [P, T])
        oh1, oh2 = sb("oh1", [P, T, NE_G]), sb("oh2", [P, T, NE_G])
        dl, el = sb("p_dl", [P, T]), sb("p_el", [P, T])
        pair = [sb(f"pair{k}", [P, T, NG, NE_G]) for k in range(2)]
        both = sb("p_both", [P, T * NE])
        tot, incl, base = sb("p_tot", [P, NE, T]), sb("p_incl", [P, NE, T]), sb("p_base", [P, NE, T])
        row = sb("p_row", [P, T, NE])
        nb, ni, endb, startr = sb("p_nb", [P, NE]), sb("p_ni", [P, NE], I32), sb("p_endb", [P, NE]), sb("p_startr", [P, NE])
        drow = sb("p_drow", [P, 2, T])
        dlow, dhigh = sb("p_dlow", [P, 2, T], I32), sb("p_dhigh", [P, 2, T], I32)
        flow, fhigh = sb("p_flow", [P, 2, T]), sb("p_fhigh", [P, 2, T])
        place = sb("p_place", [P, 2, T], I32)
        token = sb("p_token", [P, T], I32)
        zero = sb("p_zero", [P, BLOCKS], I32)
        cmp = sb("p_cmp", [1, BLOCKS, NE])
        bexp, ringpos = sb("p_bexp", [1, BLOCKS]), sb("p_ringpos", [1, BLOCKS])

        b = [ctx.enter_context(nc.psum_tensor(f"p_bank{n}", [P, 512], F32)) for n in range(4)]
        consts_in, shifted, e_done, d_ready, el_ready = (sem(n) for n in ("p_consts_in", "shifted", "e_done", "d_ready",
                                                                          "el_ready"))
        both_ready, counted, place_ready, ids_set, table_zero, table_set, rows_in, zero_set = (
            sem(n) for n in ("both_ready", "counted", "place_ready", "ids_set", "table_zero", "table_set", "rows_in",
                             "zero_set"))
        chain_sem = sem("p_dve_chain")
        LOADS = [(before, io["before"]), (ones, io["ones"]), (reset, io["reset"]), (rank4, io["rank4"]),
                 (rank8, io["rank8"]), (block_no, io["block_no"])]
        over = lambda ap, n: ap.unsqueeze(1).to_broadcast([P, T, n])

        block = ctx.enter_context(nc.Block())

        @block.sync
        def _(sp):
            for dst, src in LOADS:
                sp.dma_start(dst[:], src).then_inc(consts_in, 16)
            sp.wait_ge(zero_set, 1)
            sp.dma_start(table_dram.rearrange("(p s) a -> p (s a)", p=P), zero[:]).then_inc(table_zero, 16)
            sp.wait_ge(table_set, 16 * 2 * T)
            sp.dma_start(block_rows[:], table_dram.rearrange("(p s) a -> p (s a)", p=P)).then_inc(rows_in, 16)
            sp.wait_ge(rows_in, 16)

        @block.gpsimd
        def _(pool):
            nc.gpsimd.memset(zero[:], 0).then_inc(zero_set, 1)
            nc.gpsimd.iota(token[:], [[P, T]], base=0, channel_multiplier=1).then_inc(ids_set, 1)
            pool.wait_ge(ids_set, 1)
            pool.wait_ge(table_zero, 16)
            pool.wait_ge(place_ready, 1)
            for t in range(T):
                for k in range(2):
                    pool.indirect_dma_start(out=table_dram, out_offset=bass.IndirectOffsetOnAxis(ap=place[:, k, t:t + 1], axis=0),
                                            in_=token[:, t:t + 1], in_offset=None).then_inc(table_set, 16)
            pool.wait_ge(table_set, 16 * 2 * T)

        @block.scalar
        def _(act):
            act.wait_ge(shifted, 1)
            nc.scalar.activation(eg[:], sh[:], ACT.Exp).then_inc(e_done, 1)
            act.wait_ge(d_ready, 1)
            nc.scalar.activation(el[:], dl[:], ACT.Exp).then_inc(el_ready, 1)

        @block.tensor
        def _(pe):
            pe.wait_ge(consts_in, 16 * len(LOADS))
            pe.wait_ge(both_ready, 1)
            for n in range(2):
                nc.tensor.matmul(b[n][:], before[:], both[:, n * 512:(n + 1) * 512], start=True, stop=True)
            for n in range(2):
                ins = nc.tensor.matmul(b[2 + n][:], ones[:], both[:, n * 512:(n + 1) * 512], start=True, stop=True)
            ins.then_inc(counted, 1)

        @block.vector
        def _(dve):
            V = nc.vector
            chain = Chain(dve, chain_sem)
            lg = logits[:, :, 0:NG]
            le = logits[:, :, NG:NG + NE].rearrange("p t (g e) -> p t g e", g=NG)
            dve.wait_ge(consts_in, 16 * len(LOADS))

            def first_max(out, x, largest, ranks, scratch, n):
                chain(V.tensor_reduce(largest, x, AX.X, ALU.max))
                chain(V.tensor_tensor(scratch, x, bc(largest, n), ALU.is_equal))
                chain(V.tensor_tensor(scratch, scratch, over(ranks[:], n), ALU.mult))
                chain(V.tensor_reduce(mv[:], scratch, AX.X, ALU.max))
                chain(V.tensor_tensor(out, scratch, bc(mv[:], n), ALU.is_equal))

            first_max(ohg[:], lg, gm[:], rank4, vg[:], NG)
            V.tensor_tensor(sh[:], lg, bc(gm[:], NG), ALU.subtract).then_inc(shifted, 1)
            chosen = ohg[:].unsqueeze(3).to_broadcast([P, T, NG, NE_G])
            chain(V.tensor_tensor(big[:], le, chosen, ALU.mult))
            chain(V.tensor_reduce(ein[:], big[:].rearrange("p t g e -> p t e g"), AX.X, ALU.add))
            first_max(oh1[:], ein[:], m1[:], rank8, v8[:], NE_G)
            chain(V.scalar_tensor_tensor(ein[:], oh1[:], -1e30, ein[:], ALU.mult, ALU.add))
            first_max(oh2[:], ein[:], m2[:], rank8, v8[:], NE_G)
            V.tensor_tensor(dl[:], m2[:], m1[:], ALU.subtract).then_inc(d_ready, 1)
            for k, oh in enumerate((oh1, oh2)):
                chain(V.tensor_tensor(pair[k][:], chosen, oh[:].unsqueeze(2).to_broadcast([P, T, NG, NE_G]), ALU.mult))
            V.tensor_tensor(both[:], pair[0][:].rearrange("p t g e -> p (t g e)"),
                            pair[1][:].rearrange("p t g e -> p (t g e)"), ALU.add).then_inc(both_ready, 1)
            dve.wait_ge(e_done, 1)
            chain(V.tensor_reduce(pg[:], eg[:], AX.X, ALU.add))
            chain(V.reciprocal(pg[:], pg[:]))
            dve.wait_ge(el_ready, 1)
            chain(V.tensor_scalar(dl[:], el[:], 1.0, None, ALU.add))
            chain(V.reciprocal(dl[:], dl[:]))
            chain(V.tensor_tensor(wts[:, 0, :], dl[:], pg[:], ALU.mult))
            chain(V.tensor_tensor(wts[:, 1, :], wts[:, 0, :], el[:], ALU.mult))
            dve.wait_ge(counted, 1)
            for n in range(2):
                chain(V.tensor_copy(tot[:, :, n * 16:(n + 1) * 16], b[2 + n][:].rearrange("p (t e) -> p e t", e=NE)))
            flat = lambda ap: ap.rearrange("p e t -> p (e t)")
            chain(V.tensor_tensor_scan(flat(incl[:]), reset[:], flat(tot[:]), 0.0, ALU.mult, ALU.add))
            chain(V.tensor_scalar(nb[:], incl[:, :, T - 1], float(P - 1), None, ALU.add))
            chain(V.tensor_copy(ni[:], nb[:]))
            chain(V.tensor_scalar(ni[:], ni[:], 7, None, ALU.arith_shift_right))
            chain(V.tensor_copy(nb[:], ni[:]))
            chain(V.tensor_scalar(nb[:], nb[:], 1.0, None, ALU.max))
            chain(V.tensor_tensor_scan(endb[:], ones[:, 0:NE], nb[:], 0.0, ALU.mult, ALU.add))
            chain(V.tensor_tensor(startr[:], endb[:], nb[:], ALU.subtract))
            chain(V.tensor_tensor(base[:], incl[:], tot[:], ALU.subtract))
            chain(V.tensor_scalar(startr[:], startr[:], float(P), None, ALU.mult))
            chain(V.tensor_tensor(base[:], base[:], bc(startr[:], T), ALU.add))
            for n in range(2):
                tiles = slice(n * 16, (n + 1) * 16)
                chain(V.tensor_tensor(row[:, tiles, :], b[n][:].rearrange("p (t e) -> p t e", e=NE),
                                      base[:, :, tiles].rearrange("p e t -> p t e"), ALU.add))
            for k in range(2):
                chain(V.tensor_tensor(pair[k][:].rearrange("p t g e -> p t (g e)"),
                                      pair[k][:].rearrange("p t g e -> p t (g e)"), row[:], ALU.mult))
                chain(V.tensor_reduce(drow[:, k, :], pair[k][:].rearrange("p t g e -> p t (g e)"), AX.X, ALU.add))
            chain(V.tensor_copy(dest[:], drow[:]))
            chain(V.tensor_scalar(dlow[:], dest[:], P - 1, None, ALU.bitwise_and))
            chain(V.tensor_scalar(dhigh[:], dest[:], 7, None, ALU.arith_shift_right))
            chain(V.tensor_copy(flow[:], dlow[:]))
            chain(V.tensor_copy(fhigh[:], dhigh[:]))
            chain(V.scalar_tensor_tensor(flow[:], flow[:], float(BLOCKS), fhigh[:], ALU.mult, ALU.add))
            V.tensor_copy(place[:], flow[:]).then_inc(place_ready, 1)
            wide = [1, BLOCKS, NE]
            chain(V.tensor_tensor(cmp[:], block_no[:].unsqueeze(2).to_broadcast(wide),
                                  endb[0:1, :].unsqueeze(1).to_broadcast(wide), ALU.is_ge))
            chain(V.tensor_reduce(bexp[:], cmp[:], AX.X, ALU.add))
            chain(V.tensor_scalar(bexp[:], bexp[:], float(NE - 1), None, ALU.min))
            chain(V.tensor_copy(block_expert[:], bexp[:]))
            for m in range(3):
                chain(V.tensor_scalar(ringpos[:], bexp[:], 3.0, float(m), ALU.mult, ALU.add))
                chain(V.tensor_copy(block_slot[:, m, :], ringpos[:]))
            chain(V.tensor_scalar(block_slot[:], block_slot[:], 3, None, ALU.bitwise_and))
            chain(V.tensor_scalar(nb[:], endb[:], 1.0, None, ALU.add))
            chain(V.tensor_copy(expert_end[:, 2:2 + NE], nb[0:1, :]))
            chain(V.tensor_copy(expert_end[:, 0:2], ones[0:1, 0:2]))


def run_experts(nc, io, block_rows, block_expert, block_slot, expert_end, xn_dram, out_dram):
    semaphores = []
    with ExitStack() as ctx:
        ctx.callback(end_phase, nc, semaphores)

        def sb(name, shape, dt=F32):
            return ctx.enter_context(nc.sbuf_tensor(name, shape, dt))

        def sem(name):
            semaphores.append(nc.alloc_semaphore(name=name))
            return semaphores[-1]

        RING, RAW = 4, 3
        W_PARTS = 8
        ident, ident_r = sb("e_ident", [P, P]), sb("e_ident_r", [P, P], F32R)
        w_hi = sb("w_hi", [P, RING * W_PARTS, 512], F32R)
        w_lo = sb("w_lo", [P, RING * W_PARTS, 512], F32R)
        raw = [sb(f"w_raw{r}", [P, W_PARTS // 2, 512]) for r in range(RAW)]
        icol = sb("icol", [P, 1], I32)
        xg = sb("xg", [P, D])
        x_hi, x_lo = sb("x_hi", [P, D], F32R), sb("x_lo", [P, D], F32R)
        xT_hi, xT_lo = sb("e_xT_hi", [P, KD, P], F32R), sb("e_xT_lo", [P, KD, P], F32R)
        sg, up, hh = sb("sg", [P, FE]), sb("up", [P, FE]), sb("hh", [P, FE])
        h_hi, h_lo = sb("h_hi", [P, FE], F32R), sb("h_lo", [P, FE], F32R)
        hT_hi, hT_lo = sb("hT_hi", [P, KF, P], F32R), sb("hT_lo", [P, KF, P], F32R)
        ys = [sb(f"ys{j}", [P, D]) for j in range(2)]

        GATE, UP, HT, XT, DOWN = 0, 1, 2, 4, 6
        b = [ctx.enter_context(nc.psum_tensor(f"e_bank{n}", [P, 512], F32)) for n in range(8)]
        uses = [1, 1, 1, 1, 2, 2, 1, 1]
        bank = [Bank(sem(f"e_full{n}"), sem(f"e_free{n}"), uses[n]) for n in range(8)]
        consts_in, ident_set = sem("e_consts_in"), sem("e_ident_set")
        raw_in = [sem(f"raw_in{r}") for r in range(RAW)]
        w_hi_ready = sem("w_hi_ready")
        w_split = sem("w_split")
        blocks_through = [sem(f"blocks_through{m}") for m in range(3)]
        icol_ready, pool_passed = sem("icol_ready"), sem("e_pool_passed")
        x_in = sem("e_x_in")
        x_hi_ready, x_lo_ready = sem("x_hi_ready"), sem("x_lo_ready")
        hh_ready, h_hi_ready, h_lo_ready = sem("hh_ready"), sem("h_hi_ready"), sem("h_lo_ready")
        y_out = [sem(f"e_y_out{j}") for j in range(2)]
        out_b = out_dram.rearrange("(s p) d -> s p d", p=P)

        def run_slots(engine, prologue, slot, epilogue):
            prologue()
            slot(0, 0, 0, False, True, True)
            with engine.Fori(0, (BLOCKS - 3) // 2) as i:
                slot(i * 2 + 1, 1, i, True, True, True)
                slot(i * 2 + 2, 0, i + 1, True, True, True)
            slot(BLOCKS - 2, (BLOCKS - 2) % 2, (BLOCKS - 2) // 2, True, True, False)
            slot(BLOCKS - 1, (BLOCKS - 1) % 2, (BLOCKS - 1) // 2, True, False, False)
            epilogue()

        assert BLOCKS % 2 == 1 and NE % RING == 0
        nothing = lambda: None
        block = ctx.enter_context(nc.Block())

        @block.sync
        def _(sp):
            sp.dma_start(ident[:], io["ident"]).then_inc(consts_in, 16)
            quarter = W_PARTS // 2
            with sp.Fori(0, NE) as e:
                for m, name in enumerate(("w_gate", "w_up", "w_down")):
                    w = io[name][bass.ds(e, 1)].rearrange("a (k p) f -> p (a k) f", p=P)
                    rows = w.shape[1] // 2
                    for half in range(2):
                        r = (2 * m + half) % RAW
                        sp.wait_ge(w_split, e * 6 + 2 * m + half + 1)
                        sp.dma_start(raw[r][:].rearrange("p (k c) f -> p k (c f)", k=rows),
                                     w[:, half * rows:(half + 1) * rows, :]).then_inc(raw_in[r], 16)

        @block.vector
        def _(dve):
            V = nc.vector
            for k in bank:
                dve.sem_inc(k.free, 1)
            dve.sem_inc(w_split, RAW)
            for m in range(3):
                dve.sem_inc(blocks_through[m], 1)
            with dve.Fori(0, NE // RING) as i:
                for n in range(RING):
                    for m in range(3):
                        slot = (3 * n + m) % RING
                        older, which = (2, 2) if m == 0 else (1, m - 1)
                        end = dve.value_load(expert_end[0:1, bass.ds(i * RING + n + 2 - older, 1)], min_val=1,
                                             max_val=BLOCKS + 1)
                        dve.wait_ge(blocks_through[which], end)
                        for half in range(2):
                            r = (2 * m + half) % RAW
                            at = slot * W_PARTS + half * W_PARTS // 2
                            part = slice(at, at + W_PARTS // 2)
                            count = i * 6 * RING + (6 * n + 2 * m + half)
                            dve.wait_ge(raw_in[r], i * 32 * RING + 16 * (2 * n + (2 * m + half) // RAW + 1))
                            V.tensor_copy(w_hi[:, part, :], raw[r][:]).then_inc(w_hi_ready, 1)
                            dve.wait_ge(w_hi_ready, count + 1)
                            V.tensor_tensor(w_lo[:, part, :], raw[r][:], w_hi[:, part, :], ALU.subtract)\
                                .then_inc(w_split, 1)

        @block.gpsimd
        def _(pool):
            for j in range(2):
                pool.sem_inc(y_out[j], 16)

            def gather(s):
                if not (isinstance(s, int) and s == 0):
                    pool.wait_ge(x_lo_ready, s)
                pass_wait(pool, pool_passed)
                nc.gpsimd.tensor_copy(icol[:], block_rows[:, bass.ds(s, 1)]).then_inc(icol_ready, 1)
                pool.wait_ge(icol_ready, s + 1)
                pass_wait(pool, pool_passed)
                pool.indirect_dma_start(out=xg[:], out_offset=None, in_=xn_dram,
                                        in_offset=bass.IndirectOffsetOnAxis(ap=icol[:, 0:1], axis=0))\
                    .then_inc(x_in, 16)

            def split_x(s):
                pool.wait_ge(x_in, s * 16 + 16)
                pool.wait_ge(x_hi_ready, s + 1)
                if not (isinstance(s, int) and s == 0):
                    bank[XT + 1].wait_full(pool, s - 1, 1)
                nc.gpsimd.tensor_tensor(x_lo[:], xg[:], x_hi[:], ALU.subtract).then_inc(x_lo_ready, 1)

            def split_h(s, first):
                bank[GATE].wait_free(pool, s + 1, 0)
                bank[UP].wait_free(pool, s + 1, 0)
                if not first:
                    pool.wait_ge(h_lo_ready, s)
                nc.gpsimd.tensor_tensor(hh[:], sg[:], up[:], ALU.mult).then_inc(hh_ready, 1)
                pool.wait_ge(hh_ready, s + 1)
                pool.wait_ge(h_hi_ready, s + 1)
                if not first:
                    bank[HT + 1].wait_full(pool, s - 1, 0)
                nc.gpsimd.tensor_tensor(h_lo[:], hh[:], h_hi[:], ALU.subtract).then_inc(h_lo_ready, 1)

            def slot(s, j, i, before, after, after2):
                if after2:
                    gather(s + 2)
                split_h(s, not before)
                if after2:
                    split_x(s + 2)

            def prologue():
                for s in range(2):
                    gather(s)
                    split_x(s)

            run_slots(pool, prologue, slot, nothing)

        @block.scalar
        def _(act):
            def split_x(s):
                act.wait_ge(x_in, s * 16 + 16)
                if not (isinstance(s, int) and s == 0):
                    act.wait_ge(x_lo_ready, s)
                nc.scalar.activation(x_hi[:], xg[:], ACT.Copy).then_inc(x_hi_ready, 1)

            def evac_xT(s, part):
                for k in range(2):
                    bank[XT + k].wait_full(act, s, part)
                    nc.scalar.activation((xT_hi, xT_lo)[part][:, 4 * k:4 * k + 4, :],
                                         b[XT + k][:].rearrange("p (k n) -> p k n", k=4), ACT.Copy)\
                        .then_inc(bank[XT + k].free, 1)

            def evac_hT(s):
                for k, part in enumerate((hT_hi, hT_lo)):
                    bank[HT + k].wait_full(act, s, 0)
                    nc.scalar.activation(part[:], b[HT + k][:].rearrange("p (k n) -> p k n", k=KF), ACT.Copy)\
                        .then_inc(bank[HT + k].free, 1)

            def evac_y(s, j, i, n):
                if n == 0:
                    act.wait_ge(y_out[j], (i + 1) * 16)
                bank[DOWN + n].wait_full(act, s, 0)
                nc.scalar.activation(ys[j][:, n * 512:(n + 1) * 512], b[DOWN + n][:], ACT.Copy)\
                    .then_inc(bank[DOWN + n].free, 1)
                if n == 1:
                    act.sem_inc(blocks_through[2], 1)
                    for k in range(2):
                        bank[DOWN + k].wait_free(act, s + 1, 0)
                    act.dma_start(out_b[bass.ds(s, 1)].rearrange("a p d -> (a p) d"), ys[j][:]).then_inc(y_out[j], 16)

            def slot(s, j, i, before, after, after2):
                bank[GATE].wait_full(act, s, 0)
                act.sem_inc(blocks_through[0], 1)
                if before:
                    act.wait_ge(hh_ready, s)
                nc.scalar.activation(sg[:], b[GATE][:], ACT.Silu).then_inc(bank[GATE].free, 1)
                if before:
                    evac_hT(s - 1)
                bank[UP].wait_full(act, s, 0)
                act.sem_inc(blocks_through[1], 1)
                nc.scalar.activation(up[:], b[UP][:], ACT.Copy).then_inc(bank[UP].free, 1)
                if after:
                    evac_xT(s + 1, 0)
                act.wait_ge(hh_ready, s + 1)
                if before:
                    bank[HT].wait_full(act, s - 1, 0)
                    act.wait_ge(h_lo_ready, s)
                nc.scalar.activation(h_hi[:], hh[:], ACT.Copy).then_inc(h_hi_ready, 1)
                if before:
                    evac_y(s - 1, 1 - j, i - 1 + j, 0)
                if after:
                    evac_xT(s + 1, 1)
                if after2:
                    split_x(s + 2)
                if before:
                    evac_y(s - 1, 1 - j, i - 1 + j, 1)

            def prologue():
                act.wait_ge(consts_in, 16)
                nc.scalar.activation(ident_r[:], ident[:], ACT.Copy).then_inc(ident_set, 1)
                split_x(0)
                evac_xT(0, 0)
                evac_xT(0, 1)
                split_x(1)

            def epilogue():
                s = BLOCKS - 1
                evac_hT(s)
                for n in range(2):
                    evac_y(s, s % 2, s // 2, n)

            run_slots(act, prologue, slot, epilogue)
            act.wait_ge(y_out[0], 16 * ((BLOCKS + 1) // 2 + 1))
            act.wait_ge(y_out[1], 16 * (BLOCKS // 2 + 1))

        @block.tensor
        def _(pe):
            pe.wait_ge(ident_set, 1)

            def transpose(bank_at, out, x, blocks):
                for c in blocks:
                    ins = nc.tensor.matmul(out[:, (c % 4) * P:(c % 4 + 1) * P], x[:, c * P:(c + 1) * P], ident_r[:],
                                           start=True, stop=True)
                ins.then_inc(bank_at.full, 1)

            def transpose_x(s, part):
                pe.wait_ge((x_hi_ready, x_lo_ready)[part], s + 1)
                for k in range(2):
                    bank[XT + k].wait_free(pe, s, part)
                    transpose(bank[XT + k], b[XT + k], (x_hi, x_lo)[part], range(4 * k, 4 * k + 4))

            def transpose_h(s):
                pe.wait_ge(h_lo_ready, s + 1)
                for k, part in enumerate((h_hi, h_lo)):
                    bank[HT + k].wait_free(pe, s, 0)
                    transpose(bank[HT + k], b[HT + k], part, range(KF))

            def product(out, lhs_hi, lhs_lo, rhs, blocks):
                for k in range(blocks):
                    hi, lo = rhs(w_hi, k), rhs(w_lo, k)
                    nc.tensor.matmul(out[:], lhs_hi[:, k, :], hi, start=k == 0, stop=False)
                    nc.tensor.matmul(out[:], lhs_hi[:, k, :], lo, start=False, stop=False)
                    ins = nc.tensor.matmul(out[:], lhs_lo[:, k, :], hi, start=False, stop=k == blocks - 1)
                return ins

            def load_slot(s, m):
                return pe.value_load(block_slot[0:1, m:m + 1, bass.ds(s, 1)].rearrange("p a b -> p (a b)"),
                                     min_val=0, max_val=RING - 1)

            def load_expert(s):
                return pe.value_load(block_expert[0:1, bass.ds(s, 1)], min_val=0, max_val=NE - 1)

            def first(s, which, expert):
                at = load_slot(s, which)
                pe.wait_ge(w_split, expert * 6 + (2 * which + 2 + RAW))
                bank[which].wait_free(pe, s, 0)
                product(b[which], xT_hi, xT_lo,
                        lambda w, k: w[:, bass.ds(at * W_PARTS + k, 1), :].rearrange("p a f -> p (a f)"), KD)\
                    .then_inc(bank[which].full, 1)

            def down(s, n, at):
                bank[DOWN + n].wait_free(pe, s, 0)
                product(b[DOWN + n], hT_hi, hT_lo,
                        lambda w, k: w[:, bass.ds(at * W_PARTS + (2 * k + n), 1), :].rearrange("p a f -> p (a f)"), KF)\
                    .then_inc(bank[DOWN + n].full, 1)

            def begin_down(s):
                expert = load_expert(s)
                at = load_slot(s, 2)
                pe.wait_ge(w_split, expert * 6 + (6 + RAW))
                for k in range(2):
                    bank[HT + k].wait_free(pe, s + 1, 0)
                return at

            def slot(s, j, i, before, after, after2):
                expert = load_expert(s)
                for k in range(2):
                    bank[XT + k].wait_free(pe, s + 1, 0)
                first(s, GATE, expert)
                if before:
                    transpose_h(s - 1)
                first(s, UP, expert)
                if after:
                    transpose_x(s + 1, 0)
                if before:
                    at = begin_down(s - 1)
                    down(s - 1, 0, at)
                if after:
                    transpose_x(s + 1, 1)
                if before:
                    down(s - 1, 1, at)

            def prologue():
                transpose_x(0, 0)
                transpose_x(0, 1)

            def epilogue():
                s = BLOCKS - 1
                transpose_h(s)
                at = begin_down(s)
                for n in range(2):
                    down(s, n, at)

            run_slots(pe, prologue, slot, epilogue)


def combine(nc, io, wts, dest, x2_dram, experts_dram, out_dram):
    semaphores = []
    with ExitStack() as ctx:
        ctx.callback(end_phase, nc, semaphores)

        def sb(name, shape, dt=F32):
            return ctx.enter_context(nc.sbuf_tensor(name, shape, dt))

        def sem(name):
            semaphores.append(nc.alloc_semaphore(name=name))
            return semaphores[-1]

        g_fin = sb("g_fin_sb", [P, D])
        minus_half, eps = sb("f_minus_half", [P, 1]), sb("f_eps", [P, 1])
        icol = [[sb(f"f_icol{j}{k}", [P, 1], I32) for k in range(2)] for j in range(2)]
        ye = [[sb(f"f_y{j}{k}", [P, D]) for k in range(2)] for j in range(2)]
        xb = [sb(f"f_x{j}", [P, D]) for j in range(2)]
        acc = [sb(f"f_acc{j}", [P, D]) for j in range(2)]
        sq = sb("f_sq", [P, D])
        ss, rs = [sb(f"f_ss{j}", [P, 1]) for j in range(2)], [sb(f"f_rs{j}", [P, 1]) for j in range(2)]
        ot = [sb(f"f_out{j}", [P, D]) for j in range(2)]
        consts_in, half_set, icol_ready = sem("f_consts_in"), sem("f_half_set"), sem("f_icol_ready")
        pool_passed = sem("f_pool_passed")
        y_in = [[sem(f"f_y_in{j}{k}") for k in range(2)] for j in range(2)]
        x_in = [sem(f"f_x_in{j}") for j in range(2)]
        acc_ready, sq_ready, rs_ready, out_ready = (sem(n) for n in ("acc_ready", "f_sq_ready", "f_rs_ready", "out_ready"))
        stored = [sem(f"f_stored{j}") for j in range(2)]
        acc_chain, rs_chain = sem("acc_chain"), sem("rs_chain")
        x_t = x2_dram.rearrange("(t p) d -> t p d", p=P)
        o_t = out_dram.rearrange("(t p) d -> t p d", p=P)
        at = lambda dram, t: dram[bass.ds(t, 1)].rearrange("a p d -> (a p) d")
        block = ctx.enter_context(nc.Block())

        @block.sync
        def _(sp):
            sp.dma_start(g_fin[:], io["g_fin"]).then_inc(consts_in, 16)
            for j in range(2):
                sp.sem_inc(stored[j], 16)
            with sp.Fori(0, TILES // 2) as i:
                for j in range(2):
                    t = i * 2 + j
                    sp.wait_ge(acc_ready, t + 1)
                    sp.dma_start(xb[j][:], at(x_t, t)).then_inc(x_in[j], 16)

        @block.gpsimd
        def _(pool):
            pool.sem_inc(acc_ready, 2)
            nc.gpsimd.memset(minus_half[:], -0.5).then_inc(half_set, 1)
            nc.gpsimd.memset(eps[:], EPS).then_inc(half_set, 1)
            pool.wait_ge(half_set, 2)
            chain = Chain(pool, rs_chain, 1)

            def gather(t, j):
                pool.wait_ge(acc_ready, t + 1)
                pass_wait(pool, pool_passed)
                for k in range(2):
                    nc.gpsimd.tensor_copy(icol[j][k][:], dest[:, k, bass.ds(t, 1)]).then_inc(icol_ready, 1)
                pool.wait_ge(icol_ready, (t + 1) * 2)
                pass_wait(pool, pool_passed)
                for k in range(2):
                    pool.indirect_dma_start(out=ye[j][k][:], out_offset=None, in_=experts_dram,
                                            in_offset=bass.IndirectOffsetOnAxis(ap=icol[j][k][:, 0:1], axis=0))\
                        .then_inc(y_in[j][k], 16)

            def root(t, j):
                chain.tile(t)
                pool.wait_ge(sq_ready, t + 1)
                chain(nc.gpsimd.tensor_tensor(rs[j][:], ss[j][:], eps[:], ALU.add))
                nc.gpsimd.tensor_tensor(rs[j][:], rs[j][:], minus_half[:], ALU.pow).then_inc(rs_ready, 1)

            gather(0, 0)
            gather(1, 1)
            with pool.Fori(0, TILES // 2 - 1) as i:
                for j in range(2):
                    gather(i * 2 + j + 2, j)
                    root(i * 2 + j, j)
            for t in range(TILES - 2, TILES):
                root(t, t % 2)

        @block.scalar
        def _(act):
            with act.Fori(0, TILES // 2) as i:
                for j in range(2):
                    t = i * 2 + j
                    act.wait_ge(acc_ready, t + 3)
                    nc.scalar.activation(sq[:], acc[j][:], ACT.Square, scale=D ** -0.5, accum_out=ss[j][:])\
                        .then_inc(sq_ready, 1)
                    act.wait_ge(out_ready, t + 3)
                    act.dma_start(at(o_t, t), ot[j][:]).then_inc(stored[j], 16)
            for j in range(2):
                act.wait_ge(stored[j], 16 * (TILES // 2 + 1))

        @block.vector
        def _(dve):
            V = nc.vector
            dve.sem_inc(out_ready, 2)
            dve.wait_ge(consts_in, 16)
            chain = Chain(dve, acc_chain, 1)

            def add(t, j, i):
                chain.tile(t)
                dve.wait_ge(out_ready, t + 1)
                dve.wait_ge(x_in[j], (i + 1) * 16)
                dve.wait_ge(y_in[j][0], (i + 1) * 16)
                chain(V.scalar_tensor_tensor(acc[j][:], ye[j][0][:], wts[:, 0, bass.ds(t, 1)], xb[j][:], ALU.mult, ALU.add))
                dve.wait_ge(y_in[j][1], (i + 1) * 16)
                V.scalar_tensor_tensor(acc[j][:], ye[j][1][:], wts[:, 1, bass.ds(t, 1)], acc[j][:], ALU.mult, ALU.add)\
                    .then_inc(acc_ready, 1)

            def norm(t, j, i):
                dve.wait_ge(rs_ready, t + 1)
                dve.wait_ge(acc_ready, t + 3)
                dve.wait_ge(stored[j], (i + 1) * 16)
                V.scalar_tensor_tensor(ot[j][:], acc[j][:], rs[j][:, 0:1], g_fin[:], ALU.mult, ALU.mult)\
                    .then_inc(out_ready, 1)

            add(0, 0, 0)
            with dve.Fori(0, TILES // 2 - 1) as i:
                add(i * 2 + 1, 1, i)
                norm(i * 2, 0, i)
                add(i * 2 + 2, 0, i + 1)
                norm(i * 2 + 1, 1, i)
            add(TILES - 1, 1, TILES // 2 - 1)
            norm(TILES - 2, 0, TILES // 2 - 1)
            norm(TILES - 1, 1, TILES // 2 - 1)


def layer_program(nc, io, out):
    dram = lambda name, shape, dt=F32: nc.dram_tensor(name, shape, dt, kind="Internal").ap()
    u_dram = dram("u_dram", [SEQ, GW])
    y_dram = dram("y_dram", [SEQ, GW])
    mix_dram = dram("mix_dram", [SEQ, 3 * GW])
    x2_dram = dram("x2_dram", [SEQ, D])
    xn_dram = dram("xn_dram", [SEQ, D])
    experts_dram = dram("experts_dram", [BLOCKS * P, D])
    table_dram = dram("table_dram", [BLOCKS * P, 1], I32)
    project_and_mix(nc, io, u_dram, mix_dram)
    state_space(nc, io, u_dram, y_dram)
    with ExitStack() as ctx:
        keep = lambda name, shape, dt=F32: ctx.enter_context(nc.sbuf_tensor(name, shape, dt))
        logits = keep("logits", [P, TILES, NG + NE])
        wts = keep("pair_weights", [P, 2, TILES])
        dest = keep("pair_rows", [P, 2, TILES], I32)
        block_rows = keep("block_rows", [P, BLOCKS], I32)
        block_expert = keep("block_expert", [1, BLOCKS], I32)
        block_slot = keep("block_slot", [1, 3, BLOCKS], I32)
        expert_end = keep("expert_end", [1, 2 + NE], I32)
        merge_and_route(nc, io, mix_dram, y_dram, x2_dram, xn_dram, logits)
        plan_experts(nc, io, logits, wts, dest, block_rows, block_expert, block_slot, expert_end, table_dram)
        run_experts(nc, io, block_rows, block_expert, block_slot, expert_end, xn_dram, experts_dram)
        combine(nc, io, wts, dest, x2_dram, experts_dram, out)


def host_layout(inputs):
    import numpy as np

    a = {k: np.asarray(v) for k, v in inputs.items()}
    rows = lambda v: np.ascontiguousarray(np.broadcast_to(v.reshape(1, -1), (P, v.size)))
    kblocks = lambda w: np.ascontiguousarray(w.reshape(-1, P, w.shape[-1]).transpose(1, 0, 2))
    kcol = lambda v: np.ascontiguousarray(v.reshape(-1, P).T)
    w = a["w_in"][0]
    aq, ak, av, su, cq, ck, cv, ci, cf, co, gu, gv = np.split(
        w, np.cumsum([256, 128, 128, 256, 256, 256, 256, 4, 4, 256, 256])[:], axis=1)
    q = aq.reshape(D, 4, DH)[:, [0, 2, 1, 3]].reshape(D, GW)
    w = np.concatenate([q, ak, cq, ck, av, cv, co, gu, gv, su, ci, cf], axis=1)
    step = np.arange(P)
    neg = np.float32(-1e30)
    current = np.where(step[None] <= step[:, None], np.float32(0), neg)
    before = np.where(step[None] > step[:, None], np.float32(0), neg)
    head = np.arange(HEADS)
    out = {
        "x": np.ascontiguousarray(a["x"][0]),
        "ident": np.eye(P, dtype=np.float32),
        "w_in": kblocks(w),
        "g_mix": kcol(a["norm_mix_g"][0]),
        "gate_b": rows(a["mlstm_gate_b"][0]),
        "sinks": rows(a["attn_sinks"][0]),
        "conv_w": np.ascontiguousarray(a["mlstm_conv_w"][0].reshape(4, 4, P).transpose(2, 1, 0)),
        "norm_c": rows(a["mlstm_norm_g"][0]),
        "ln_g": rows(a["sgu_ln_g"][0]),
        "ln_b": rows(a["sgu_ln_b"][0]),
        "sgu_w": np.ascontiguousarray(a["sgu_w"][0].transpose(2, 0, 1)),
        "sgu_b": np.ascontiguousarray(a["sgu_b"][0].T),
        "tri": (step[:, None] <= step[None]).astype(np.float32),
        "causal": np.where(step[:, None] <= step[None], np.float32(0), neg),
        "mask_first": np.stack([current, np.full((P, P), neg)], 1),
        "mask_even": np.stack([current, before], 1),
        "mask_odd": np.stack([before, current], 1),
        "sel": np.ascontiguousarray(np.broadcast_to(np.eye(HEADS, dtype=np.float32)[:, :, None], (HEADS, HEADS, P))),
        "half": (head[:, None] % 2 == step[None] // 64).astype(np.float32),
        "slotmask": (head[:, None] // 2 == np.arange(2)[None]).astype(np.float32),
    }
    return out


def s5_layout(a):
    import numpy as np

    both = lambda v: np.ascontiguousarray(np.concatenate([v.T, v.T]))
    stack = lambda top, low: np.ascontiguousarray(np.concatenate([top, low]))
    b_re, b_im = (a[k][0].transpose(1, 0, 2) for k in ("ssm_b_re", "ssm_b_im"))
    c_re, c_im = (a[k][0].transpose(2, 0, 1) for k in ("ssm_c_re", "ssm_c_im"))
    eye = np.eye(P, dtype=np.float32)
    return {
        "swap": np.roll(eye, 64, 0),
        "sign": np.repeat(np.array([-1, 1], np.float32), 64)[:, None],
        "idt": np.concatenate([eye, np.zeros((P, P), np.float32)], 1),
        "dskip": np.ascontiguousarray(np.tile(a["ssm_d"][0].reshape(GROUPS, GH).T, (P // GH, 1))),
        "are": both(a["ssm_a_re"][0]),
        "aim": both(a["ssm_a_im"][0]),
        "ldt": np.ascontiguousarray(np.broadcast_to(a["ssm_log_dt"][0][None], (P, GROUPS))),
        "b1": stack(b_re, b_im),
        "b2": stack(b_im, b_re),
        "c1": stack(c_re, c_im),
        "c2": stack(c_im, c_re),
    }


def ffn_layout(a):
    import numpy as np

    rows = lambda v: np.ascontiguousarray(np.broadcast_to(v.reshape(1, -1), (P, v.size)))
    kblocks = lambda w: np.ascontiguousarray(w.reshape(-1, P, w.shape[-1]).transpose(1, 0, 2))
    w_out = a["w_out"][0].reshape(4, GW, D)[[0, 2, 3, 1]].reshape(D, D)
    step = np.arange(P)
    down = lambda n: rows(np.arange(n, 0, -1).astype(np.float32))
    return {
        "w_out": kblocks(w_out),
        "glu_w": kblocks(a["ssm_glu_w"][0]),
        "glu_b": rows(a["ssm_glu_b"][0]),
        "w_r": kblocks(np.concatenate([a["router_group_w"][0], a["router_expert_w"][0]], 1)),
        "b_r": rows(np.concatenate([a["router_group_b"][0], a["router_expert_b"][0]])),
        "g_ffn": rows(a["norm_ffn_g"][0]),
        "g_fin": rows(a["norm_final_g"]),
        "before": (step[:, None] < step[None]).astype(np.float32),
        "ones": np.ones((P, P), np.float32),
        "reset": rows((np.arange(NE * TILES) % TILES > 0).astype(np.float32)),
        "rank4": down(NG),
        "rank8": down(NE_G),
        "block_no": np.arange(BLOCKS, dtype=np.float32)[None],
        "w_gate": np.ascontiguousarray(a["expert_w_gate"][0]),
        "w_up": np.ascontiguousarray(a["expert_w_up"][0]),
        "w_down": np.ascontiguousarray(a["expert_w_down"][0]),
    }


def kernel(**inputs):
    import numpy as np
    import concourse.bacc as bacc
    from concourse.bass_utils import run_bass_kernel_spmd

    a = {k: np.asarray(v) for k, v in inputs.items()}
    arrays = {**host_layout(a), **s5_layout(a), **ffn_layout(a)}
    nc = bacc.Bacc("TRN2", target_bir_lowering=False, num_devices=1)
    io = {k: nc.dram_tensor(f"in_{k}", v.shape, mybir.dt.from_np(v.dtype), kind="ExternalInput").ap()
          for k, v in arrays.items()}
    out = nc.dram_tensor("out", (SEQ, D), F32, kind="ExternalOutput").ap()
    layer_program(nc, io, out)
    r = run_bass_kernel_spmd(nc, [{f"in_{k}": v for k, v in arrays.items()}], core_ids=[0])
    return r.results[0]["out"].reshape(1, SEQ, D)
```

```python
from contextlib import ExitStack

import concourse.bass as bass
from concourse import mybir

F32 = mybir.dt.float32
I32 = mybir.dt.int32
F32R = mybir.dt.float32r
ALU = mybir.AluOpType
ACT = mybir.ActivationFunctionType
AX = mybir.AxisListType

P = 128
SEQ = 4096
D = 1024
TILES = SEQ // P
KD = D // P
GW = 256
HEADS = 4
DH = 64
EPS = 1e-6
GELU_A = 0.044715
GELU_B = 0.7978845608028654

AQ, AK, CQK, AV, CV, CO, GU, GV, SU, GATES = 0, 256, 384, 896, 1024, 1280, 1536, 1792, 2048, 2304
ZW = 2312
ZCHUNK = 512
ZCHUNKS = [(c, min(ZCHUNK, ZW - c)) for c in range(0, ZW, ZCHUNK)]

GROUPS, GH, STATE = 16, 16, 64
L = 16
CH = SEQ // L
CT = CH // P
LEVELS = 8

NG, NE_G = 4, 8
NE = NG * NE_G
FE = 512
KF = FE // P
BLOCKS = SEQ * 2 // P + NE - 1


class Chain:

    def __init__(self, engine, sem, per_tile=0):
        self.engine, self.sem, self.per_tile, self.base, self.n = engine, sem, per_tile, 0, 0

    def tile(self, t):
        if self.n and self.per_tile:
            assert self.n == self.per_tile, (self.n, self.per_tile)
        self.base, self.n = t * self.per_tile, 0

    def post(self, instruction):
        self.n += 1
        instruction.then_inc(self.sem, 1)
        return self.n

    def done(self, number):
        self.engine.wait_ge(self.sem, self.base + number)

    def __call__(self, instruction):
        self.done(self.post(instruction))


class Bank:

    def __init__(self, full, free, uses):
        self.full, self.free, self.uses = full, free, uses

    def wait_free(self, pe, t, use):
        pe.wait_ge(self.free, t * self.uses + use + 1)

    def wait_full(self, engine, t, use):
        engine.wait_ge(self.full, t * self.uses + use + 1)


def end_phase(nc, semaphores):
    nc.clear_and_free_semaphores(semaphores)
    nc.all_engine_barrier()


def pass_wait(engine, passed):
    engine.sem_inc(passed, 1)


def bc(ap, n):
    return ap.unsqueeze(2).to_broadcast([ap.shape[0], ap.shape[1], n])


def project_and_mix(nc, io, u_dram, mix_dram):
    semaphores = []
    with ExitStack() as ctx:
        ctx.callback(end_phase, nc, semaphores)

        def sb(name, shape, dt=F32):
            return ctx.enter_context(nc.sbuf_tensor(name, shape, dt))

        def sem(name):
            semaphores.append(nc.alloc_semaphore(name=name))
            return semaphores[-1]

        ident = sb("a_ident", [P, P])
        w_hi, w_lo = sb("a_w_hi", [P, KD, ZW], F32R), sb("a_w_lo", [P, KD, ZW], F32R)
        g_mix = sb("g_mix_sb", [P, KD])
        gate_b = sb("gate_b_sb", [P, 8])
        sinks = sb("sinks_sb", [P, HEADS])
        conv_w = sb("conv_w_sb", [P, 4, 4])
        norm_c = sb("norm_c_sb", [P, GW])
        ln_g = sb("ln_g_sb", [P, GW])
        ln_b = sb("ln_b_sb", [P, GW])
        sgu_w = sb("sgu_w_sb", [P, HEADS, P])
        sgu_b = sb("sgu_b_sb", [P, HEADS])
        tri = sb("tri_sb", [P, P])
        causal = sb("causal_sb", [P, P])
        mask_even = sb("mask_even", [P, 2, P])
        mask_odd = sb("mask_odd", [P, 2, P])
        sel = sb("sel_sb", [HEADS, HEADS, P])
        half = sb("half_sb", [HEADS, P])
        slotmask = sb("slotmask_sb", [HEADS, 2])
        xb = sb("a_x", [P, D])
        xT_hi, xT_lo = sb("a_xT_hi", [P, KD, P], F32R), sb("a_xT_lo", [P, KD, P], F32R)
        ss = sb("a_ss", [P, 1])
        rs = sb("a_rs", [P, 1])
        minus_half = sb("a_minus_half", [P, HEADS])
        eps, eps_twice = sb("a_eps", [P, 1]), sb("eps_twice", [P, 1])
        z = sb("z", [P, ZW])
        qT = sb("qT", [P, 2, P])
        kT = sb("kT", [P, 2, P])
        va = sb("va", [P, 2, P])
        scores = sb("scores", [P, HEADS, 2 * P])
        probs, pT = scores, scores[:].rearrange("p h (s n) -> p h s n", s=2)
        xsq = scores[:].rearrange("p h n -> p (h n)")
        smax = sb("smax", [P, HEADS])
        snmax = sb("snmax", [P, HEADS])
        ssink = sb("ssink", [P, HEADS])
        esink = sb("esink", [P, HEADS])
        den = sb("den", [P, HEADS])
        rden = sb("rden", [P, HEADS])
        cx = sb("cx", [P, 4, P + 3])
        cv = sb("cv", [P, 4, P])
        qk = sb("qk", [P, 4, P])
        cth = qk
        k_tok = sb("k_tok", [P, HEADS, DH])
        kw = sb("kw", [P, HEADS, DH])
        v1 = sb("v1", [P, HEADS, DH + 1])
        gates = sb("gates", [P, 8])
        fa = sb("fa", [P, 4])
        fy = sb("fy", [P, 4])
        fq = sb("fq", [P, 4])
        fq2 = sb("fq2", [P, 4])
        fp = sb("fp", [P, 4])
        nlogf = sb("nlogf", [P, 4])
        zero_row = sb("zero_row", [HEADS, P])
        m_row = sb("m_row", [HEADS, P])
        mt_row = sb("mt_row", [HEADS, P])
        m_prev = sb("m_prev", [HEADS, 1])
        wi_row = sb("wi_row", [HEADS, P])
        em_row = sb("em_row", [HEADS, P])
        wi_last = sb("wi_last", [HEADS, 2])
        gcol = sb("gcol", [P, 4])
        cols = sb("cols", [P, 10])
        wT = sb("wT", [P, HEADS, P])
        earg = et = wT
        cn = sb("cn", [P, 2, DH + 1])
        num = sb("num", [P, HEADS, DH + 1])
        inter = num
        dena = sb("dena", [P, HEADS])
        rdc = sb("rdc", [P, HEADS])
        hc, hsq = k_tok, kw
        hss = sb("hss", [P, HEADS])
        hrs = sb("hrs", [P, HEADS])
        gco = sb("gco", [P, GW])
        coth = gco
        ge = sb("ge", [P, 2 * GW])
        gsq = gin = gth = ge
        bst = sb("bst", [P, 6])
        mv = sb("mv", [P, 2])
        lrs = sb("lrs", [P, 1])
        vn = sb("vn", [P, GW])
        mix = sb("mix", [P, 3 * GW])

        b = [ctx.enter_context(nc.psum_tensor(f"a_bank{n}", [P, 512], F32)) for n in range(8)]
        uses = [4, 3, 3, 3, 4, 1, 1, 3]
        bank = [Bank(sem(f"a_full{n}"), sem(f"a_free{n}"), uses[n]) for n in range(8)]

        weights_in = sem("weights_in")
        consts_set = sem("consts_set")
        gain_in = sem("gain_in")
        piece_in = [sem(f"w_piece_in{j}") for j in range(5)]
        w_hi_ready, w_lo_ready, sgu_masked = sem("a_w_hi_ready"), sem("a_w_lo_ready"), sem("sgu_masked")
        x_in = sem("a_x_in")
        xT_hi_ready = sem("a_xT_hi_ready")
        sq_done = sem("sq_done")
        xn_ready = sem("xn_ready")
        z_ready = sem("z_ready")
        su_out, mix_out = sem("su_out"), sem("mix_out")
        mix_ready = sem("mix_ready")
        qkT_ready = sem("qkT_ready")
        cx_ready = sem("cx_ready")
        conv_ready = sem("conv_ready")
        cth_ready = sem("cth_ready")
        qk_ready = sem("qk_ready")
        gates_ready = sem("gates_ready")
        fa_ready = sem("fa_ready")
        fy_ready = sem("fy_ready")
        nlogf_ready = sem("nlogf_ready")
        m_ready = sem("m_ready")
        rows_ready = sem("rows_ready")
        wi_last_ready = sem("wi_last_ready")
        k_tok_ready = sem("k_tok_ready")
        v1_ready = sem("v1_ready")
        va_ready = sem("va_ready")
        earg_ready = sem("earg_ready")
        et_ready = sem("et_ready")
        wT_ready = sem("wT_ready")
        cn_ready = sem("cn_ready")
        snmax_ready = sem("snmax_ready")
        probs_ready = sem("probs_ready")
        esink_ready = sem("esink_ready")
        pT_ready = sem("pT_ready")
        gin_ready = sem("gin_ready")
        gth_ready = sem("gth_ready")
        ge_ready = sem("ge_ready")
        var_ready = sem("var_ready")
        lrs_ready = sem("lrs_ready")
        vn_ready = sem("vn_ready")
        vnb_ready = sem("vnb_ready")
        coth_ready = sem("coth_ready")
        hc_ready = sem("hc_ready")
        rs_ready = sem("rs_ready")
        conv_tail = sem("conv_tail")
        mask_kept = sem("mask_kept")
        hsq_ready = sem("hsq_ready")
        hss_ready = sem("hss_ready")
        hrs_ready = sem("hrs_ready")
        pool_passed, dve_passed = sem("a_pool_passed"), sem("a_dve_passed")
        dve_chain = sem("a_dve_chain")
        pool_norm_chain = sem("a_pool_norm_chain")
        pool_mix_chain = sem("a_pool_mix_chain")

        LOADS = [(ident, io["ident"]), (gate_b, io["gate_b"]),
                 (sinks, io["sinks"]), (conv_w, io["conv_w"]), (norm_c, io["norm_c"]), (ln_g, io["ln_g"]),
                 (ln_b, io["ln_b"]), (sgu_w, io["sgu_w"]), (sgu_b, io["sgu_b"]), (tri, io["tri"]),
                 (causal, io["causal"]), (mask_even, io["mask_first"]), (mask_odd, io["mask_odd"]), (sel, io["sel"]), (half, io["half"]), (slotmask, io["slotmask"])]
        ALL_IN = 16 * len(LOADS)
        QUARTER = ZW // 4
        pieces = [(k, h * QUARTER) for k in range(KD) for h in range(4)]
        staging = [z[:, h * QUARTER:(h + 1) * QUARTER] for h in range(4)] + [mix[:, 0:QUARTER]]
        assert QUARTER <= 3 * GW
        x_tiles = io["x"].rearrange("(t p) d -> t p d", p=P)
        u_tiles = u_dram.rearrange("(t p) d -> t p d", p=P)
        mix_tiles = mix_dram.rearrange("(t p) d -> t p d", p=P)
        fixed = lambda t: isinstance(t, int)
        heads_of = lambda ap, e: ap.rearrange("p (s e) l -> p e s l", e=2)[:, e]

        def run_slots(engine, slot, prologue):
            prologue()
            with engine.Fori(0, TILES // 2 - 1) as i:
                slot(i * 2, 0, i, True, True)
                slot(i * 2 + 1, 1, i, True, True)
            slot(TILES - 2, 0, TILES // 2 - 1, True, False)
            slot(TILES - 1, 1, TILES // 2 - 1, False, False)

        block = ctx.enter_context(nc.Block())

        @block.sync
        def _(sp):
            def load_x(t):
                if not (fixed(t) and t == 0):
                    for k in range(2):
                        bank[k].wait_full(sp, t - 1, 0)
                sp.dma_start(xb[:], x_tiles[bass.ds(t, 1)].rearrange("a p d -> (a p) d")).then_inc(x_in, 16)

            def slot(t):
                if not fixed(t) or t + 2 < TILES:
                    load_x(t + 2)
                sp.wait_ge(z_ready, (t + 1) * len(ZCHUNKS))
                sp.dma_start(u_tiles[bass.ds(t, 1)].rearrange("a p d -> (a p) d"), z[:, SU:SU + GW]).then_inc(su_out, 16)
                sp.wait_ge(mix_ready, t + 2)
                sp.dma_start(mix_tiles[bass.ds(t, 1)].rearrange("a p d -> (a p) d"), mix[:]).then_inc(mix_out, 16)

            sp.dma_start(g_mix[:], io["g_mix"]).then_inc(gain_in, 16)
            load_x(0)
            for n, (k, c) in enumerate(pieces):
                if n == len(staging):
                    for dst, src in LOADS:
                        sp.dma_start(dst[:], src).then_inc(weights_in, 16)
                if n >= len(staging):
                    sp.wait_ge(w_lo_ready, n + 1 - len(staging))
                sp.dma_start(staging[n % len(staging)], io["w_in"][:, k, c:c + QUARTER])\
                    .then_inc(piece_in[n % len(staging)], 16)
            load_x(1)
            with sp.Fori(0, TILES - 2) as t:
                slot(t)
            for t in range(TILES - 2, TILES):
                slot(t)
            sp.wait_ge(su_out, 16 * (TILES + 1))
            sp.wait_ge(mix_out, 16 * (TILES + 1))

        @block.gpsimd
        def _(pool):
            norm_chain = Chain(pool, pool_norm_chain, 1)
            chain = Chain(pool, pool_mix_chain, 5)
            pool.sem_inc(xn_ready, 2)
            pool.sem_inc(su_out, 16)
            pool.sem_inc(mix_out, 16)
            nc.gpsimd.memset(minus_half[:], -0.5).then_inc(consts_set, 1)
            nc.gpsimd.memset(eps[:], EPS).then_inc(consts_set, 1)
            nc.gpsimd.memset(eps_twice[:], 4 * EPS).then_inc(consts_set, 1)
            nc.gpsimd.memset(v1[:, :, DH:DH + 1], 1.0).then_inc(consts_set, 1)
            nc.gpsimd.memset(va[:, 1, :], 0.0).then_inc(consts_set, 1)
            nc.gpsimd.memset(zero_row[:], 0.0).then_inc(consts_set, 1)
            nc.gpsimd.memset(mt_row[:], 0.0).then_inc(consts_set, 1)
            nc.gpsimd.memset(cx[:, :, 0:3], 0.0).then_inc(consts_set, 1)
            nc.gpsimd.memset(kT[:, 1, :], 0.0).then_inc(consts_set, 1)
            nc.gpsimd.memset(cn[:], 0.0).then_inc(cn_ready, 1)
            pool.wait_ge(consts_set, 9)

            def normalise(t, j):
                norm_chain.tile(t)
                pool.wait_ge(sq_done, t + 1)
                norm_chain(nc.gpsimd.tensor_tensor(rs[:], ss[:], eps[:], ALU.add))
                nc.gpsimd.tensor_tensor(rs[:], rs[:], minus_half[:, 0:1], ALU.pow).then_inc(rs_ready, 1)
                pool.wait_ge(rs_ready, t + 1)
                pass_wait(pool, pool_passed)
                nc.gpsimd.tensor_scalar(xb[:], xb[:], rs[:, 0:1], None, ALU.mult).then_inc(xn_ready, 1)

            def slot(t, j, i, projecting, norming):
                chain.tile(t)
                zt = z
                pool.wait_ge(z_ready, (t + 1) * len(ZCHUNKS))
                pool.wait_ge(mix_ready, t + 1)
                pass_wait(pool, pool_passed)
                nc.gpsimd.tensor_copy(va[:, j, :], zt[:, AV:AV + P]).then_inc(va_ready, 1)
                nc.gpsimd.tensor_copy(v1[:, :, 0:DH], zt[:, CV:CV + GW].rearrange("p (h d) -> p h d", h=HEADS))\
                    .then_inc(v1_ready, 1)
                guv = zt[:, GU:GU + 2 * GW]
                chain(nc.gpsimd.tensor_tensor(gsq[:], guv, guv, ALU.mult))
                pass_wait(pool, pool_passed)
                chain(nc.gpsimd.tensor_scalar(gsq[:], gsq[:], GELU_A, 1.0, ALU.mult, ALU.add))
                nc.gpsimd.tensor_tensor(gin[:], gsq[:], guv, ALU.mult).then_inc(gin_ready, 1)
                if norming:
                    normalise(t + 2, j)
                pool.wait_ge(var_ready, t + 1)
                chain(nc.gpsimd.tensor_tensor(lrs[:], mv[:, 1:2], eps_twice[:], ALU.add))
                nc.gpsimd.tensor_tensor(lrs[:], lrs[:], minus_half[:, 0:1], ALU.pow).then_inc(lrs_ready, 1)
                pool.wait_ge(vn_ready, t + 1)
                chain(nc.gpsimd.tensor_tensor(vn[:], vn[:], ln_g[:], ALU.mult))
                nc.gpsimd.tensor_tensor(vn[:], vn[:], ln_b[:], ALU.add).then_inc(vnb_ready, 1)
                pool.wait_ge(hc_ready, t + 1)
                nc.gpsimd.tensor_tensor(hsq[:], hc[:], hc[:], ALU.mult).then_inc(hsq_ready, 1)
                pool.wait_ge(hss_ready, t + 1)
                pass_wait(pool, pool_passed)
                chain(nc.gpsimd.tensor_scalar(hrs[:], hss[:], 1.0 / DH, EPS, ALU.mult, ALU.add))
                nc.gpsimd.tensor_tensor(hrs[:], hrs[:], minus_half[:], ALU.pow).then_inc(hrs_ready, 1)

            def prologue():
                normalise(0, 0)
                normalise(1, 1)
                pool.wait_ge(weights_in, ALL_IN)

            run_slots(pool, slot, prologue)

        @block.scalar
        def _(act):
            act.wait_ge(consts_set, 9)
            act.wait_ge(gain_in, 16)

            def square(t):
                act.wait_ge(x_in, t * 16 + 16)
                nc.scalar.activation(xsq, xb[:], ACT.Square, scale=D ** -0.5, accum_out=ss[:]).then_inc(sq_done, 1)

            def evac_xT(t):
                for k in range(2):
                    bank[k].wait_full(act, t, 0)
                    nc.scalar.activation(xT_hi[:, 4 * k:4 * k + 4, :], b[k][:].rearrange("p (k n) -> p k n", k=4),
                                         ACT.Copy).then_inc(xT_hi_ready, 1)

            def evac_z(t, n):
                c, w = ZCHUNKS[n]
                k, use = (0, 1 + n // 2) if n % 2 == 0 else (1, 1 + n // 2)
                bank[k].wait_full(act, t, use)
                nc.scalar.activation(z[:, c:c + w], b[k][:, 0:w], ACT.Copy).then_inc(bank[k].free, 1)
                bank[k].wait_free(act, t, use + 1)
                act.sem_inc(z_ready, 1)

            def slot(t, j, i, projecting, norming):
                tp = t + 1
                zt = z
                if projecting:
                    evac_xT(tp)
                bank[2].wait_full(act, t, 0)
                nc.scalar.activation(qT[:], b[2][:, 0:2 * P].rearrange("p (c n) -> p c n", c=2), ACT.Copy)\
                    .then_inc(qkT_ready, 1)
                nc.scalar.activation(kT[:, j, :], b[2][:, 2 * P:3 * P], ACT.Copy).then_inc(bank[2].free, 1)
                bank[3].wait_full(act, t, 0)
                act.wait_ge(conv_tail, t + 1)
                nc.scalar.activation(cx[:, :, 3:P + 3], b[3][:].rearrange("p (c n) -> p c n", c=4), ACT.Copy)\
                    .then_inc(bank[3].free, 1)
                act.wait_ge(gates_ready, t + 1)
                nc.scalar.activation(fa[:], gates[:, 4:8], ACT.Abs).then_inc(fa_ready, 1)
                act.wait_ge(fa_ready, t + 1)
                nc.scalar.activation(fy[:], fa[:], ACT.Exp, scale=-1.0).then_inc(fy_ready, 1)
                if norming:
                    act.wait_ge(xn_ready, t + 4)
                    act.wait_ge(mix_ready, t + 1)
                    square(t + 2)
                act.wait_ge(mix_ready, t + 1)
                nc.scalar.activation(coth[:], zt[:, CO:CO + GW], ACT.Tanh, scale=0.5).then_inc(coth_ready, 1)
                act.wait_ge(gin_ready, t + 1)
                nc.scalar.activation(gth[:], gin[:], ACT.Tanh, scale=GELU_B).then_inc(gth_ready, 1)
                if projecting:
                    evac_z(tp, 0)
                act.wait_ge(conv_ready, t + 1)
                nc.scalar.activation(cth[:], cv[:], ACT.Tanh, scale=0.5).then_inc(cth_ready, 1)
                act.wait_ge(m_ready, 2 * (t + 1))
                nc.scalar.activation(wi_row[:], m_row[:], ACT.Exp, bias=m_prev[:, 0:1], scale=-1.0).then_inc(rows_ready, 1)
                nc.scalar.activation(em_row[:], mt_row[:], ACT.Exp, scale=-1.0).then_inc(rows_ready, 1)
                if projecting:
                    act.wait_ge(va_ready, t + 1)
                    evac_z(tp, 1)
                act.wait_ge(snmax_ready, t + 1)
                for h in range(HEADS):
                    nc.scalar.activation(probs[:, h, :], scores[:, h, :], ACT.Exp, bias=snmax[:, h:h + 1],
                                         scale=DH ** -0.5, accum_out=den[:, h:h + 1]).then_inc(probs_ready, 1)
                nc.scalar.activation(esink[:], ssink[:], ACT.Exp).then_inc(esink_ready, 1)
                bank[7].wait_full(act, t, 0)
                nc.scalar.activation(k_tok[:], b[7][:, 0:GW].rearrange("p (h d) -> p h d", h=HEADS), ACT.Copy)\
                    .then_inc(bank[7].free, 1)
                act.wait_ge(earg_ready, t + 1)
                for h in range(HEADS):
                    nc.scalar.activation(et[:, h, :], earg[:, h, :], ACT.Exp, bias=gcol[:, h:h + 1])\
                        .then_inc(et_ready, 1)
                if projecting:
                    act.wait_ge(v1_ready, t + 1)
                    evac_z(tp, 2)
                    act.wait_ge(ge_ready, t + 1)
                    evac_z(tp, 3)
                bank[2].wait_full(act, t, 2)
                bank[3].wait_full(act, t, 2)
                nc.scalar.activation(pT[:, 0:2].rearrange("p h s n -> p (h s n)"), b[2][:], ACT.Copy)\
                    .then_inc(bank[2].free, 1)
                nc.scalar.activation(pT[:, 2:4].rearrange("p h s n -> p (h s n)"), b[3][:], ACT.Copy)\
                    .then_inc(bank[3].free, 1)
                if projecting:
                    act.wait_ge(su_out, t * 16 + 32)
                    evac_z(tp, 4)

            def prologue():
                square(0)
                for n, (k, c) in enumerate(pieces):
                    act.wait_ge(piece_in[n % len(staging)], 16 * (n // len(staging) + 1))
                    nc.scalar.activation(w_hi[:, k, c:c + QUARTER], staging[n % len(staging)], ACT.Copy,
                                         scale=g_mix[:, k:k + 1]).then_inc(w_hi_ready, 1)
                act.wait_ge(weights_in, ALL_IN)
                evac_xT(0)
                act.wait_ge(xn_ready, 3)
                square(1)
                act.wait_ge(w_lo_ready, len(pieces))
                for n in range(len(ZCHUNKS)):
                    evac_z(0, n)

            run_slots(act, slot, prologue)

        @block.vector
        def _(dve):
            chain = Chain(dve, dve_chain, 52)
            for k in bank:
                dve.sem_inc(k.free, 1)
            dve.sem_inc(mix_ready, 1)
            dve.sem_inc(conv_tail, 1)
            dve.sem_inc(mask_kept, 1)
            dve.wait_ge(consts_set, 9)
            dve.wait_ge(gain_in, 16)
            for n, (k, c) in enumerate(pieces):
                dve.wait_ge(w_hi_ready, n + 1)
                nc.vector.scalar_tensor_tensor(w_lo[:, k, c:c + QUARTER], staging[n % len(staging)], g_mix[:, k:k + 1],
                                               w_hi[:, k, c:c + QUARTER], ALU.mult, ALU.subtract).then_inc(w_lo_ready, 1)
            dve.wait_ge(weights_in, ALL_IN)
            nc.vector.tensor_tensor(sgu_w[:], sgu_w[:], tri[:].unsqueeze(1).to_broadcast([P, HEADS, P]), ALU.mult)\
                .then_inc(sgu_masked, 1)

            def evac_xT(t):
                for k in range(2):
                    bank[k].wait_full(dve, t, 0)
                    dve.wait_ge(xT_hi_ready, t * 2 + (k + 1))
                    nc.vector.tensor_tensor(xT_lo[:, 4 * k:4 * k + 4, :], b[k][:].rearrange("p (k n) -> p k n", k=4),
                                            xT_hi[:, 4 * k:4 * k + 4, :], ALU.subtract).then_inc(bank[k].free, 1)

            def slot(t, j, i, projecting, norming):
                chain.tile(t)
                zt, mx = z, mix
                if projecting:
                    evac_xT(t + 1)
                dve.wait_ge(z_ready, (t + 1) * len(ZCHUNKS))
                nc.vector.tensor_tensor(gates[:], zt[:, GATES:GATES + 8], gate_b[:], ALU.add).then_inc(gates_ready, 1)
                dve.wait_ge(gates_ready, t + 1)
                dve.wait_ge(fy_ready, t + 1)
                chain(nc.vector.tensor_scalar(fp[:], fy[:], 2.0, None, ALU.add))
                chain(nc.vector.reciprocal(fp[:], fp[:]))
                chain(nc.vector.tensor_tensor(fq[:], fy[:], fp[:], ALU.mult))
                chain(nc.vector.tensor_tensor(fq2[:], fq[:], fq[:], ALU.mult))
                chain(nc.vector.tensor_scalar(fp[:], fq2[:], 1.0 / 17, None, ALU.mult))
                for c in (15, 13, 11, 9, 7, 5, 3):
                    chain(nc.vector.scalar_tensor_tensor(fp[:], fp[:], 1.0 / c, fq2[:], ALU.add, ALU.mult))
                chain(nc.vector.scalar_tensor_tensor(fp[:], fp[:], 1.0, fq[:], ALU.add, ALU.mult))
                chain(nc.vector.tensor_scalar(fq[:], gates[:, 4:8], -1.0, 0.0, ALU.mult, ALU.max))
                nc.vector.scalar_tensor_tensor(nlogf[:], fp[:], 2.0, fq[:], ALU.mult, ALU.add).then_inc(nlogf_ready, 1)
                bank[3].wait_free(dve, t, 1)
                posted = [chain.post(nc.vector.tensor_scalar(cv[:, c, :], cx[:, c, 0:P], conv_w[:, c, 0:1], None,
                                                             ALU.mult)) for c in range(4)]

                def add_tap(tap):
                    for c in range(4):
                        chain.done(posted[c])
                        posted[c] = chain.post(nc.vector.scalar_tensor_tensor(
                            cv[:, c, :], cx[:, c, tap:tap + P], conv_w[:, c, tap:tap + 1], cv[:, c, :], ALU.mult,
                            ALU.add))

                add_tap(1)
                bank[4].wait_full(dve, t, 0)
                nc.vector.tensor_copy(m_prev[:], mt_row[:, P - 1:P]).then_inc(m_ready, 1)
                chain(nc.vector.tensor_tensor_scan(m_row[:], zero_row[:], b[4][0:HEADS, P:2 * P],
                                                   mt_row[:, P - 1:P], ALU.add, ALU.max))
                chain(nc.vector.tensor_copy(gcol[:], b[4][:, 2 * P:2 * P + 4]))
                nc.vector.tensor_tensor(mt_row[:], m_row[:], b[4][0:HEADS, 0:P], ALU.subtract)\
                    .then_inc(bank[4].free, 1)
                bank[4].wait_free(dve, t, 1)
                dve.sem_inc(m_ready, 1)
                add_tap(2)
                add_tap(3)
                chain.done(posted[3])
                dve.sem_inc(conv_ready, 1)
                nc.vector.tensor_copy(cx[:, :, 0:3], cx[:, :, P:P + 3]).then_inc(conv_tail, 1)
                mask = mask_even if j == 0 else mask_odd
                dve.wait_ge(mask_kept, i + 1)
                if norming:
                    dve.wait_ge(sq_done, t + 3)
                for e in range(2):
                    bank[2 + e].wait_full(dve, t, 1)
                    nc.vector.tensor_tensor(scores[:, 2 * e:2 * e + 2, :],
                                            b[2 + e][:].rearrange("p (h n) -> p h n", h=2),
                                            mask[:].rearrange("p s n -> p (s n)").unsqueeze(1)
                                            .to_broadcast([P, 2, 2 * P]), ALU.add).then_inc(bank[2 + e].free, 1)
                dve.wait_ge(cth_ready, t + 1)
                nc.vector.scalar_tensor_tensor(qk[:], cth[:], 1.0, cv[:], ALU.add, ALU.mult).then_inc(qk_ready, 1)
                bank[2].wait_free(dve, t, 2)
                bank[3].wait_free(dve, t, 2)
                chain(nc.vector.tensor_reduce(smax[:], scores[:], AX.X, ALU.max))
                chain(nc.vector.scalar_tensor_tensor(smax[:], smax[:], DH ** -0.5, sinks[:], ALU.mult, ALU.max))
                chain(nc.vector.tensor_tensor(ssink[:], sinks[:], smax[:], ALU.subtract))
                if j == 0:
                    nc.vector.tensor_copy(mask_even[:, 1, :], mask_odd[:, 0, :]).then_inc(mask_kept, 1)
                nc.vector.tensor_scalar(snmax[:], smax[:], -1.0, None, ALU.mult).then_inc(snmax_ready, 1)
                dve.wait_ge(gth_ready, t + 1)
                nc.vector.scalar_tensor_tensor(ge[:], gth[:], 1.0, zt[:, GU:GU + 2 * GW], ALU.add, ALU.mult)\
                    .then_inc(ge_ready, 1)
                dve.wait_ge(ge_ready, t + 1)
                chain(nc.vector.bn_stats(bst[:], ge[:, GW:2 * GW]))
                pass_wait(dve, dve_passed)
                nc.vector.bn_aggr(mv[:], bst[:]).then_inc(var_ready, 1)
                dve.wait_ge(rows_ready, 2 * (t + 1))
                nc.vector.tensor_scalar(wi_last[:], slotmask[:], wi_row[:, P - 1:P], None, ALU.mult)\
                    .then_inc(wi_last_ready, 1)
                bank[4].wait_full(dve, t, 1)
                nc.vector.tensor_tensor(earg[:], causal[:].unsqueeze(1).to_broadcast([P, HEADS, P]),
                                        b[4][:].rearrange("p (h n) -> p h n", h=HEADS), ALU.subtract)\
                    .then_inc(bank[4].free, 1)
                bank[4].wait_free(dve, t, 2)
                dve.sem_inc(earg_ready, 1)
                dve.wait_ge(lrs_ready, t + 1)
                dve.wait_ge(var_ready, t + 1)
                nc.vector.tensor_scalar(vn[:], ge[:, GW:2 * GW], mv[:, 0:1], lrs[:, 0:1], ALU.subtract, ALU.mult)\
                    .then_inc(vn_ready, 1)
                bank[7].wait_full(dve, t, 1)
                nc.vector.tensor_copy(cols[:], b[7][:, 0:10]).then_inc(bank[7].free, 1)
                bank[7].wait_free(dve, t, 2)
                dve.wait_ge(et_ready, 4 * (t + 1))
                bank[7].wait_free(dve, t, 1)
                chain(nc.vector.tensor_tensor(kw[:], k_tok[:], et[:, :, P - 1:P].to_broadcast([P, HEADS, DH]), ALU.mult))
                for e in range(2):
                    bank[5 + e].wait_full(dve, t, 0)
                    chain(nc.vector.tensor_tensor(heads_of(wT[:], e), heads_of(et[:], e),
                                                  b[5 + e][:, 0:2 * P].rearrange("p (s n) -> p s n", s=2), ALU.mult))
                    nc.vector.tensor_tensor(heads_of(inter[:], e),
                                            b[5 + e][:, 2 * P:2 * P + 130].rearrange("p (s n) -> p s n", s=2),
                                            bc(cols[:, e:4:2], DH + 1), ALU.mult).then_inc(bank[5 + e].free, 1)
                dve.sem_inc(wT_ready, 1)
                bank[6].wait_free(dve, t + 1, 0)
                dve.wait_ge(mix_out, t * 16 + 16)
                bank[4].wait_full(dve, t, 2)
                for g in range(HEADS):
                    ins = nc.vector.scalar_tensor_tensor(mx[:, 2 * GW + 64 * g:2 * GW + 64 * g + 64],
                                                         b[4][:, 64 * g:64 * g + 64], sgu_b[:, g:g + 1],
                                                         ge[:, 64 * g:64 * g + 64], ALU.add, ALU.mult)
                    if g < 3:
                        gated = chain.post(ins)
                    else:
                        ins.then_inc(bank[4].free, 1)
                bank[4].wait_free(dve, t, 3)
                dve.wait_ge(coth_ready, t + 1)
                chain(nc.vector.scalar_tensor_tensor(gco[:], coth[:], 1.0, norm_c[:], ALU.add, ALU.mult))
                bank[7].wait_full(dve, t, 2)
                bank[5].wait_free(dve, t + 1, 0)
                chain(nc.vector.tensor_tensor(num[:], b[7][:, 0:260].rearrange("p (h n) -> p h n", h=HEADS), inter[:],
                                              ALU.add))
                for s in range(2):
                    ins = nc.vector.scalar_tensor_tensor(cn[:, s, :], cn[:, s, :], cols[:, 8 + s:9 + s],
                                                         b[7][:, 260 + 65 * s:325 + 65 * s], ALU.mult, ALU.add)
                    if s == 0:
                        chain(ins)
                    else:
                        ins.then_inc(bank[7].free, 1)
                bank[7].wait_free(dve, t + 1, 0)
                dve.sem_inc(cn_ready, 1)
                den_c = num[:, :, DH]
                chain(nc.vector.tensor_scalar(dena[:], cols[:, 4:8], 32.0, None, ALU.mult))
                chain(nc.vector.tensor_tensor(dena[:], dena[:], den_c, ALU.max))
                chain(nc.vector.scalar_tensor_tensor(dena[:], den_c, -1.0, dena[:], ALU.mult, ALU.max))
                chain(nc.vector.reciprocal(rdc[:], dena[:]))
                nc.vector.tensor_tensor(hc[:], num[:, :, 0:DH], bc(rdc[:], DH), ALU.mult).then_inc(hc_ready, 1)
                dve.wait_ge(esink_ready, t + 1)
                dve.wait_ge(probs_ready, 4 * (t + 1))
                chain(nc.vector.tensor_tensor(den[:], den[:], esink[:], ALU.add))
                chain(nc.vector.reciprocal(rden[:], den[:]))
                dve.wait_ge(hsq_ready, t + 1)
                nc.vector.tensor_reduce(hss[:], hsq[:], AX.X, ALU.add).then_inc(hss_ready, 1)
                chain(nc.vector.tensor_tensor(hc[:], hc[:], gco[:].rearrange("p (h d) -> p h d", h=HEADS), ALU.mult))
                bank[4].wait_full(dve, t, 3)
                nc.vector.tensor_tensor(mx[:, 0:GW].rearrange("p (h d) -> p h d", h=HEADS),
                                        b[4][:, 0:GW].rearrange("p (h d) -> p h d", h=HEADS), bc(rden[:], DH),
                                        ALU.mult).then_inc(bank[4].free, 1)
                bank[4].wait_free(dve, t + 1, 0)
                dve.wait_ge(hrs_ready, t + 1)
                chain.done(gated)
                nc.vector.tensor_tensor(mx[:, GW:2 * GW].rearrange("p (h d) -> p h d", h=HEADS), hc[:],
                                        bc(hrs[:], DH), ALU.mult).then_inc(mix_ready, 1)

            run_slots(dve, slot, lambda: evac_xT(0))

        @block.tensor
        def _(pe):
            pe.wait_ge(weights_in, ALL_IN)

            def transpose_x(t):
                pe.wait_ge(xn_ready, t + 3)
                for k in range(2):
                    bank[k].wait_free(pe, t, 0)
                    for c in range(4):
                        ins = nc.tensor.transpose(b[k][:, c * P:(c + 1) * P], xb[:, (4 * k + c) * P:(4 * k + c + 1) * P],
                                                  ident[:])
                    ins.then_inc(bank[k].full, 1)

            def project(t, n):
                c, w = ZCHUNKS[n]
                k, use = n % 2, 1 + n // 2
                bank[k].wait_free(pe, t, use)
                for d in range(KD):
                    if n == 0 and d == KD // 2:
                        bank[1].wait_free(pe, t, 1)
                    nc.tensor.matmul(b[k][:, 0:w], xT_hi[:, d, :], w_hi[:, d, c:c + w], start=d == 0, stop=False)
                    nc.tensor.matmul(b[k][:, 0:w], xT_hi[:, d, :], w_lo[:, d, c:c + w], start=False, stop=False)
                    ins = nc.tensor.matmul(b[k][:, 0:w], xT_lo[:, d, :], w_hi[:, d, c:c + w], start=False,
                                           stop=d == KD - 1)
                ins.then_inc(bank[k].full, 1)

            def slot(t, j, i, projecting, norming):
                tp = t + 1
                zt = z
                pe.wait_ge(z_ready, (t + 1) * len(ZCHUNKS))
                bank[2].wait_free(pe, t, 0)
                for c in range(3):
                    ins = nc.tensor.transpose(b[2][:, c * P:(c + 1) * P], zt[:, AQ + c * P:AQ + (c + 1) * P], ident[:])
                ins.then_inc(bank[2].full, 1)
                bank[3].wait_free(pe, t, 0)
                for c in range(4):
                    ins = nc.tensor.transpose(b[3][:, c * P:(c + 1) * P], zt[:, CQK + c * P:CQK + (c + 1) * P], ident[:])
                ins.then_inc(bank[3].full, 1)
                if projecting:
                    project(tp, 0)
                bank[4].wait_free(pe, t, 0)
                pe.wait_ge(nlogf_ready, t + 1)
                nc.tensor.matmul(b[4][0:HEADS, 0:P], nlogf[:], tri[:], start=True, stop=True)
                nc.tensor.matmul(b[4][0:HEADS, P:2 * P], nlogf[:], tri[:], start=True, stop=False)
                nc.tensor.matmul(b[4][0:HEADS, P:2 * P], gates[:, 0:4], ident[:], start=False, stop=True)
                nc.tensor.matmul(b[4][:, 2 * P:2 * P + 4], tri[:], nlogf[:], start=True, stop=False)
                nc.tensor.matmul(b[4][:, 2 * P:2 * P + 4], ident[:], gates[:, 0:4], start=False, stop=True)\
                    .then_inc(bank[4].full, 1)
                for e in range(2):
                    bank[2 + e].wait_free(pe, t, 1)
                    for c in range(2):
                        ins = nc.tensor.matmul(b[2 + e][:, c * 2 * P:(c + 1) * 2 * P], qT[64 * e:64 * e + 64, c, :],
                                               kT[64 * e:64 * e + 64].rearrange("p s n -> p (s n)"),
                                               start=True, stop=True)
                    ins.then_inc(bank[2 + e].full, 1)
                if projecting:
                    project(tp, 1)
                bank[4].wait_free(pe, t, 1)
                for h in range(HEADS):
                    ins = nc.tensor.matmul(b[4][:, h * P:(h + 1) * P], sel[:, h, :], m_row[:], start=True, stop=True)
                ins.then_inc(bank[4].full, 1)
                pe.wait_ge(qk_ready, t + 1)
                pe.wait_ge(cn_ready, t + 1)
                for e in range(2):
                    bank[5 + e].wait_free(pe, t, 0)
                    rows = slice(64 * e, 64 * e + 64)
                    for s in range(2):
                        nc.tensor.matmul(b[5 + e][:, s * P:(s + 1) * P], qk[rows, 2 + s, :], qk[rows, s, :],
                                         start=True, stop=True)
                    for s in range(2):
                        ins = nc.tensor.matmul(b[5 + e][:, 2 * P + 65 * s:2 * P + 65 * s + 65], qk[rows, s, :],
                                               cn[rows, s, :], start=True, stop=True)
                    ins.then_inc(bank[5 + e].full, 1)
                bank[7].wait_free(pe, t, 0)
                for s in range(2):
                    ins = nc.tensor.transpose(b[7][:, s * P:(s + 1) * P], qk[:, 2 + s, :], ident[:])
                ins.then_inc(bank[7].full, 1)
                if projecting:
                    project(tp, 2)
                bank[7].wait_free(pe, t, 1)
                pe.wait_ge(rows_ready, 2 * (t + 1))
                pe.wait_ge(wi_last_ready, t + 1)
                nc.tensor.matmul(b[7][:, 0:4], wi_row[:], ident[0:4, 0:4], start=True, stop=True)
                nc.tensor.matmul(b[7][:, 4:8], em_row[:], ident[0:4, 0:4], start=True, stop=True)
                nc.tensor.matmul(b[7][:, 8:10], half[:], wi_last[:], start=True, stop=True).then_inc(bank[7].full, 1)
                if projecting:
                    project(tp, 3)
                pe.wait_ge(vnb_ready, t + 1)
                bank[4].wait_free(pe, t, 2)
                for g in range(HEADS):
                    ins = nc.tensor.matmul(b[4][:, 64 * g:64 * g + 64], sgu_w[:, g, :], vn[:, 64 * g:64 * g + 64],
                                           start=True, stop=True)
                ins.then_inc(bank[4].full, 1)
                pe.wait_ge(wT_ready, t + 1)
                pe.wait_ge(v1_ready, t + 1)
                bank[7].wait_free(pe, t, 2)
                for h in range(HEADS):
                    nc.tensor.matmul(b[7][:, 65 * h:65 * h + 65], wT[:, h, :], v1[:, h, :], start=True, stop=True)
                for h in range(HEADS):
                    lo, s = 64 * (h % 2), h // 2
                    ins = nc.tensor.matmul(b[7][lo:lo + 64, 260 + 65 * s:325 + 65 * s], kw[:, h, :], v1[:, h, :],
                                           start=True, stop=True)
                ins.then_inc(bank[7].full, 1)
                pe.wait_ge(probs_ready, 4 * (t + 1))
                for e in range(2):
                    bank[2 + e].wait_free(pe, t, 2)
                    for n in range(4):
                        ins = nc.tensor.transpose(b[2 + e][:, n * P:(n + 1) * P],
                                                  probs[:, 2 * e + n // 2, (n % 2) * P:(n % 2 + 1) * P], ident[:])
                    ins.then_inc(bank[2 + e].full, 1)
                if projecting:
                    project(tp, 4)
                pe.wait_ge(va_ready, t + 1)
                bank[3].wait_free(pe, t + 1, 0)
                bank[4].wait_free(pe, t, 3)
                for h in range(HEADS):
                    for s in range(2):
                        ins = nc.tensor.matmul(b[4][:, 64 * h:64 * h + 64], pT[:, h, s, :],
                                               va[:, s, 64 * (h // 2):64 * (h // 2) + 64], start=s == 0, stop=s == 1)
                ins.then_inc(bank[4].full, 1)
                if norming:
                    transpose_x(t + 2)

            def prologue():
                transpose_x(0)
                pe.wait_ge(w_lo_ready, len(pieces))
                pe.wait_ge(sgu_masked, 1)
                for n in range(len(ZCHUNKS)):
                    project(0, n)
                transpose_x(1)

            run_slots(pe, slot, prologue)


def state_space(nc, io, u_dram, y_dram):
    semaphores = []
    with ExitStack() as ctx:
        ctx.callback(end_phase, nc, semaphores)

        def sb(name, shape, dt=F32):
            return ctx.enter_context(nc.sbuf_tensor(name, shape, dt))

        def sem(name):
            semaphores.append(nc.alloc_semaphore(name=name))
            return semaphores[-1]

        G = GROUPS
        QUAD = 4
        ZM = 2 * L - 9
        PAD = 1
        ident = sb("s_ident", [P, P])
        swap = sb("swap_sb", [P, P])
        sign = sb("sign_sb", [P, 1])
        idt = sb("idt_sb", [P, 2 * P])
        dskip = sb("dskip_sb", [P, G])
        are, aim, ldt = sb("are", [P, G]), sb("aim", [P, G]), sb("ldt", [P, G])
        b1, b2 = sb("b1", [P, G, GH]), sb("b2", [P, G, GH])
        c1, c2 = sb("c1", [P, G, GH]), sb("c2", [P, G, GH])
        dt = sb("dt", [P, G])
        ex, en, en2, ei = sb("ex", [P, G]), sb("en", [P, G]), sb("en2", [P, G]), sb("ei", [P, G], I32)
        ep, es = sb("ep", [P, G]), sb("es", [P, G])
        mag, th, sn, cs = sb("mag", [P, G]), sb("th", [P, G]), sb("sn", [P, G]), sb("cs", [P, G])
        pr, pi = sb("pr", [P, L + 1, G]), sb("pi", [P, L + 1, G])
        t1, t2 = sb("t1", [P, 8 * G]), sb("t2", [P, 8 * G])
        qr, qi = sb("qr", [P, LEVELS, G]), sb("qi", [P, LEVELS, G])
        cr, ci = sb("cr", [P, G]), sb("ci", [P, G])
        bb1, bb2 = sb("bb1", [P, G, GH]), sb("bb2", [P, G, GH])
        tb = sb("tb", [P, G, GH])
        zz = sb("zz", [P, G, ZM, GH])
        oo = sb("oo", [P, G, L, GH])
        u = sb("u_sb", [P, CT, L, GW])
        y = sb("y_sb", [P, CT, L, GW])
        zg = [sb(f"zg{e}", [P, ZM, GH]) for e in range(QUAD)]
        ug = [sb(f"ug{e}", [P, CT, L, GH]) for e in range(QUAD)]
        uT = [sb(f"uT{e}", [P, 2, CT * P]) for e in range(QUAD)]
        rg = [sb(f"rg{e}", [P, 2, P]) for e in range(QUAD)]
        tg = [sb(f"tg{e}", [P, 2 * P]) for e in range(QUAD)]
        st = [sb(f"st{e}", [P, PAD + CH]) for e in range(QUAD)]
        step = sb("level_step", [P, QUAD * LEVELS, P])
        turned = [sb(f"turned{j}", [P, P]) for j in range(2)]
        rr, ri = sb("rr", [P, L, G]), sb("ri", [P, L, G])
        tz, to = sb("tz", [P, G, L, GH]), sb("to", [P, G, L, GH])

        b = [ctx.enter_context(nc.psum_tensor(f"s_bank{n}", [P, 512], F32)) for n in range(8)]
        uses = [4, 4, 1 + LEVELS, 1 + LEVELS]
        bank = [[Bank(sem(f"s_full{e}{n}"), sem(f"s_free{e}{n}"), uses[n]) for n in range(4)] for e in range(2)]

        def banks_of(e):
            x, second = e % 2, e // 2
            return [(b[4 * x + n], bank[x][n]) for n in (0, 1, 2 + second)] + [second]

        step_in, consts_in = sem("s_step_in"), sem("s_consts_in")
        u_in = sem("s_u_in")
        y_out = sem("s_y_out")
        pads_set = sem("pads_set")
        sin_arg = sem("sin_arg")
        sin_done = sem("sin_done")
        coeffs = sem("coeffs")
        group_copied = [sem(f"group_copied{e}") for e in range(QUAD)]
        powers_ready, reversed_ready, terms_ready, inputs_ready = (
            sem(n) for n in ("powers_ready", "reversed_ready", "terms_ready", "inputs_ready"))
        chain_sem = sem("s_dve_chain")
        pool_passed = sem("s_pool_passed")
        turned_ready, steps_ready = sem("turned_ready"), sem("steps_ready")

        STEP_LOADS = [(ldt, io["ldt"]), (are, io["are"]), (aim, io["aim"]), (sign, io["sign"])]
        LOADS = [(ident, io["ident"]), (swap, io["swap"]), (idt, io["idt"]), (dskip, io["dskip"]),
                 (b1, io["b1"]), (b2, io["b2"]), (c1, io["c1"]), (c2, io["c2"])]
        ALL_IN = 16 * len(LOADS)
        u_v = u_dram.rearrange("(t c l) w -> t c l w", c=P, l=L)
        y_v = y_dram.rearrange("(t c l) w -> t c l w", c=P, l=L)
        QUADS = G // QUAD
        per_step = [P, G, L, GH]
        over_steps = lambda v: v[:].unsqueeze(2).to_broadcast(per_step)
        over_channels = lambda v: v.rearrange("p n g -> p g n").unsqueeze(3).to_broadcast(per_step)

        block = ctx.enter_context(nc.Block())

        @block.sync
        def _(sp):
            for dst, src in STEP_LOADS:
                sp.dma_start(dst[:], src).then_inc(step_in, 16)
            for dst, src in LOADS:
                sp.dma_start(dst[:], src).then_inc(consts_in, 16)
            for t in range(CT):
                sp.dma_start(u[:, t], u_v[t]).then_inc(u_in, 16)
            for e in range(2):
                bank[e][0].wait_free(sp, QUADS, 0)
            for t in range(CT):
                sp.dma_start(y_v[t], y[:, t]).then_inc(y_out, 16)
            sp.wait_ge(y_out, 16 * CT)

        @block.gpsimd
        def _(pool):
            for e in range(QUAD):
                nc.gpsimd.memset(st[e][:, 0:PAD], 0.0).then_inc(pads_set, 1)
            nc.gpsimd.memset(zz[:, :, L:ZM, :], 0.0).then_inc(pads_set, 1)
            pool.wait_ge(powers_ready, 1)
            nc.gpsimd.tensor_tensor(to[:], over_steps(c2), over_channels(pi[:, 1:L + 1, :]), ALU.mult).then_inc(terms_ready, 1)
            pool.wait_ge(reversed_ready, 2 * L)
            pool.wait_ge(inputs_ready, 1)
            nc.gpsimd.tensor_tensor(tz[:], over_steps(bb2), over_channels(ri[:]), ALU.mult).then_inc(terms_ready, 1)
            pool.wait_ge(u_in, 16 * CT)
            pool.wait_ge(coeffs, 1)
            pool.wait_ge(pads_set, QUAD + 1)
            with pool.Fori(0, QUADS) as i:
                for e in range(QUAD):
                    banks_of(e)[1][1].wait_free(pool, i, 0)
                    pass_wait(pool, pool_passed)
                    nc.gpsimd.tensor_copy(zg[e][:], zz[:, bass.ds(i * QUAD + e, 1), :, :].rearrange("p a m h -> p (a m) h"))\
                        .then_inc(group_copied[e], 1)
                    nc.gpsimd.tensor_copy(ug[e][:].rearrange("p t l h -> p (t l) h"),
                                          u[:, :, :, bass.ds((i * QUAD + e) * GH, GH)].rearrange("p t l h -> p (t l) h"))\
                        .then_inc(group_copied[e], 1)

        @block.scalar
        def _(act):
            act.wait_ge(sin_arg, 1)
            nc.scalar.activation(sn[:], th[:], ACT.Sin).then_inc(sin_done, 1)
            nc.scalar.activation(cs[:], th[:], ACT.Sin, scale=0.5).then_inc(sin_done, 1)
            act.wait_ge(powers_ready, 1)
            for n in range(L):
                nc.scalar.activation(rr[:, n, :], pr[:, L - 1 - n, :], ACT.Copy).then_inc(reversed_ready, 1)
                nc.scalar.activation(ri[:, n, :], pi[:, L - 1 - n, :], ACT.Copy).then_inc(reversed_ready, 1)
            with act.Fori(0, QUADS) as i:
                for second in range(2):
                    pair = range(2 * second, 2 * second + 2)
                    for e in pair:
                        (B0, bank0), (B1, bank1), (B2, bank2), _ = banks_of(e)
                        bank0.wait_full(act, i, second)
                        nc.scalar.activation(uT[e][:], B0[:].rearrange("p (k n) -> p k n", k=2), ACT.Copy)\
                            .then_inc(bank0.free, 1)
                        bank1.wait_full(act, i, 2 * second)
                        nc.scalar.activation(rg[e][:], B1[:, 0:2 * P].rearrange("p (k n) -> p k n", k=2), ACT.Copy)\
                            .then_inc(bank1.free, 1)
                    for e in pair:
                        (B0, bank0), (B1, bank1), (B2, bank2), _ = banks_of(e)
                        bank2.wait_full(act, i, 0)
                        nc.scalar.activation(st[e][:, PAD:PAD + CH], B2[:, 0:CH], ACT.Copy).then_inc(bank2.free, 1)
                for e in range(QUAD):
                    (B0, bank0), (B1, bank1), (B2, bank2), second = banks_of(e)
                    bank0.wait_full(act, i, 2 + second)
                    nc.scalar.activation(y[:, :, :, bass.ds((i * QUAD + e) * GH, GH)].rearrange("p t l h -> p (t l) h"),
                                         B0[:].rearrange("p (a h) -> p a h", h=GH), ACT.Copy).then_inc(bank0.free, 1)

        @block.vector
        def _(dve):
            chain = Chain(dve, chain_sem)
            for e in range(2):
                for k in bank[e]:
                    dve.sem_inc(k.free, 1)
            dve.wait_ge(step_in, 16 * len(STEP_LOADS))
            V = nc.vector

            def rint(out, x):
                chain(V.tensor_scalar(out, x, 12582912.0, None, ALU.add))
                chain(V.tensor_scalar(out, out, 12582912.0, None, ALU.subtract))

            def exp(out, x):
                chain(V.tensor_scalar(ex[:], x, -104.0, 89.0, ALU.max, ALU.min))
                chain(V.tensor_scalar(en[:], ex[:], 1.4426950408889634, None, ALU.mult))
                rint(en[:], en[:])
                chain(V.scalar_tensor_tensor(ex[:], en[:], -0.693359375, ex[:], ALU.mult, ALU.add))
                chain(V.scalar_tensor_tensor(ex[:], en[:], 2.12194440e-4, ex[:], ALU.mult, ALU.add))
                chain(V.tensor_scalar(ep[:], ex[:], 1.0 / 40320, None, ALU.mult))
                for c in (5040, 720, 120, 24, 6, 2, 1):
                    chain(V.scalar_tensor_tensor(ep[:], ep[:], 1.0 / c, ex[:], ALU.add, ALU.mult))
                chain(V.tensor_scalar(ep[:], ep[:], 1.0, None, ALU.add))
                chain(V.tensor_scalar(en2[:], en[:], 0.5, None, ALU.mult))
                rint(en2[:], en2[:])
                chain(V.tensor_tensor(en[:], en[:], en2[:], ALU.subtract))
                for n in (en, en2):
                    chain(V.tensor_scalar(es[:], n[:], 127.0, 8388608.0, ALU.add, ALU.mult))
                    chain(V.tensor_copy(ei[:], es[:]))
                    chain(V.tensor_tensor(ep[:], ep[:], ei[:].bitcast(F32), ALU.mult))
                chain(V.tensor_copy(out, ep[:]))

            def cmul(outr, outi, ar, ai, br, bi, sr, si):
                real = [chain.post(V.tensor_tensor(sr, ai, bi, ALU.mult)),
                        chain.post(V.tensor_tensor(outr, ar, br, ALU.mult))]
                imaginary = [chain.post(V.tensor_tensor(si, ar, bi, ALU.mult)),
                             chain.post(V.tensor_tensor(outi, ai, br, ALU.mult))]
                chain.done(real[1])
                chain.post(V.tensor_tensor(outr, outr, sr, ALU.subtract))
                chain.done(imaginary[1])
                chain(V.tensor_tensor(outi, outi, si, ALU.add))

            exp(dt[:], ldt[:])
            chain(V.tensor_tensor(mag[:], are[:], dt[:], ALU.mult))
            exp(mag[:], mag[:])
            chain(V.tensor_tensor(th[:], aim[:], dt[:], ALU.mult))
            chain(V.tensor_scalar(en[:], th[:], 0.15915494309189535, None, ALU.mult))
            rint(en[:], en[:])
            chain(V.scalar_tensor_tensor(th[:], en[:], -6.28125, th[:], ALU.mult, ALU.add))
            chain(V.scalar_tensor_tensor(th[:], en[:], -0.0019340515136718750, th[:], ALU.mult, ALU.add))
            chain(V.scalar_tensor_tensor(th[:], en[:], -1.2556659146e-06, th[:], ALU.mult, ALU.add))
            V.tensor_scalar(th[:], th[:], 3.1415925, -3.1415925, ALU.min, ALU.max).then_inc(sin_arg, 1)
            dve.wait_ge(consts_in, ALL_IN)
            flat = lambda a: a[:].rearrange("p g h -> p (g h)")
            chain(V.tensor_scalar(flat(b2), flat(b2), sign[:, 0:1], None, ALU.mult))
            chain(V.tensor_scalar(flat(c1), flat(c1), sign[:, 0:1], -1.0, ALU.mult, ALU.mult))
            chain(V.tensor_scalar(flat(c2), flat(c2), -1.0, None, ALU.mult))
            dve.wait_ge(sin_done, 2)
            chain(V.tensor_tensor(cs[:], cs[:], cs[:], ALU.mult))
            chain(V.tensor_scalar(cs[:], cs[:], -2.0, 1.0, ALU.mult, ALU.add))
            chain(V.memset(pr[:, 0, :], 1.0))
            chain(V.memset(pi[:, 0, :], 0.0))
            chain(V.tensor_tensor(pr[:, 1, :], mag[:], cs[:], ALU.mult))
            chain(V.tensor_tensor(pi[:, 1, :], mag[:], sn[:], ALU.mult))
            n = 1
            while n < L:
                shape = [P, n, G]
                s1 = t1[:, 0:n * G].rearrange("p (n g) -> p n g", g=G)
                s2 = t2[:, 0:n * G].rearrange("p (n g) -> p n g", g=G)
                cmul(pr[:, n + 1:2 * n + 1, :], pi[:, n + 1:2 * n + 1, :], pr[:, 1:n + 1, :], pi[:, 1:n + 1, :],
                     pr[:, n:n + 1, :].to_broadcast(shape), pi[:, n:n + 1, :].to_broadcast(shape), s1, s2)
                n *= 2
            dve.sem_inc(powers_ready, 1)
            chain(V.tensor_copy(qr[:, 0, :], pr[:, L, :]))
            chain(V.tensor_copy(qi[:, 0, :], pi[:, L, :]))
            for n in range(1, LEVELS):
                cmul(qr[:, n, :], qi[:, n, :], qr[:, n - 1, :], qi[:, n - 1, :], qr[:, n - 1, :], qi[:, n - 1, :],
                     t1[:, 0:G], t2[:, 0:G])
            chain(V.tensor_scalar(qi[:].rearrange("p n g -> p (n g)"), qi[:].rearrange("p n g -> p (n g)"),
                                  sign[:, 0:1], None, ALU.mult))
            chain(V.tensor_tensor(t1[:, 0:G], are[:], are[:], ALU.mult))
            chain(V.tensor_tensor(t2[:, 0:G], aim[:], aim[:], ALU.mult))
            chain(V.tensor_tensor(t1[:, 0:G], t1[:, 0:G], t2[:, 0:G], ALU.add))
            chain(V.reciprocal(t1[:, 0:G], t1[:, 0:G]))
            chain(V.tensor_tensor(t2[:, 0:G], are[:], t1[:, 0:G], ALU.mult))
            chain(V.scalar_tensor_tensor(t1[:, 0:G], aim[:], -1.0, t1[:, 0:G], ALU.mult, ALU.mult))
            chain(V.tensor_scalar(ex[:], pr[:, 1, :], 1.0, None, ALU.subtract))
            cmul(cr[:], ci[:], ex[:], pi[:, 1, :], t2[:, 0:G], t1[:, 0:G], en[:], en2[:])
            wide = [P, G, GH]
            crb, cib = cr[:].unsqueeze(2).to_broadcast(wide), ci[:].unsqueeze(2).to_broadcast(wide)
            chain(V.tensor_tensor(bb1[:], b1[:], crb, ALU.mult))
            chain(V.tensor_tensor(tb[:], b2[:], cib, ALU.mult))
            chain(V.tensor_tensor(bb1[:], bb1[:], tb[:], ALU.add))
            chain(V.tensor_tensor(bb2[:], b2[:], crb, ALU.mult))
            chain(V.tensor_tensor(tb[:], b1[:], cib, ALU.mult))
            chain(V.tensor_tensor(bb2[:], bb2[:], tb[:], ALU.subtract))
            dve.sem_inc(inputs_ready, 1)
            chain(V.tensor_tensor(oo[:], over_steps(c1), over_channels(pr[:, 1:L + 1, :]), ALU.mult))
            dve.wait_ge(reversed_ready, 2 * L)
            chain(V.tensor_tensor(zz[:, :, 0:L, :], over_steps(bb1), over_channels(rr[:]), ALU.mult))
            dve.wait_ge(terms_ready, 1)
            chain(V.tensor_tensor(oo[:], oo[:], to[:], ALU.add))
            dve.wait_ge(terms_ready, 2)
            chain(V.tensor_tensor(zz[:, :, 0:L, :], zz[:, :, 0:L, :], tz[:], ALU.add))
            dve.sem_inc(coeffs, 1)
            dve.wait_ge(pads_set, QUAD + 1)

            dve.sem_inc(steps_ready, 2)

            def finish_step(i, e, n):
                dve.wait_ge(turned_ready, i * QUAD * LEVELS + (e * LEVELS + n + 1))
                V.scalar_tensor_tensor(step[:, e * LEVELS + n, :], ident[:], qr[:, n, bass.ds(i * QUAD + e, 1)],
                                       turned[n % 2][:], ALU.mult, ALU.subtract).then_inc(steps_ready, 1)

            with dve.Fori(0, QUADS) as i:
                for e in range(QUAD):
                    banks_of(e)[2][1].wait_free(dve, i, 0)
                for pair in ((0, 1), (2, 3)):
                    for e in pair:
                        g = i * QUAD + e
                        for n in range(LEVELS):
                            dve.wait_ge(steps_ready, i * QUAD * LEVELS + (e * LEVELS + n + 1))
                            V.tensor_scalar(turned[n % 2][:], swap[:], qi[:, n, bass.ds(g, 1)], None, ALU.mult)\
                                .then_inc(turned_ready, 1)
                            if n:
                                finish_step(i, e, n - 1)
                        finish_step(i, e, LEVELS - 1)
                    for e in pair:
                        (B0, bank0), (B1, bank1), (B2, bank2), second = banks_of(e)
                        bank1.wait_full(dve, i, 2 * second + 1)
                        V.scalar_tensor_tensor(tg[e][:], idt[:], dskip[:, bass.ds(i * QUAD + e, 1)], B1[:, 0:2 * P],
                                               ALU.mult, ALU.add).then_inc(bank1.free, 1)
                for n in range(LEVELS):
                    for e in range(QUAD):
                        B2, bank2 = banks_of(e)[2]
                        changed = slice(PAD + (1 << n), PAD + CH)
                        bank2.wait_full(dve, i, 1 + n)
                        bank2.wait_free(dve, i, 1 + n)
                        V.tensor_tensor(st[e][:, changed], st[e][:, changed], B2[:, 1 << n:CH], ALU.add)\
                            .then_inc(bank2.free, 1)

        @block.tensor
        def _(pe):
            pe.wait_ge(coeffs, 1)

            def transposes(e, i):
                (B0, bank0), (B1, bank1), (B2, bank2), second = banks_of(e)
                pe.wait_ge(group_copied[e], 2 * (i + 1))
                bank0.wait_free(pe, i, second)
                for k in range(2):
                    for t in range(CT):
                        ins = nc.tensor.transpose(B0[:, (k * CT + t) * P:(k * CT + t + 1) * P],
                                                  ug[e][:, t, 8 * k:8 * k + 8, :], ident[:])
                ins.then_inc(bank0.full, 1)
                bank1.wait_free(pe, i, 2 * second)
                for k in range(2):
                    ins = nc.tensor.transpose(B1[:, k * P:(k + 1) * P], zg[e][:, 8 * k:8 * k + 8, :], ident[:])
                ins.then_inc(bank1.full, 1)

            def states_and_toeplitz(e, i):
                (B0, bank0), (B1, bank1), (B2, bank2), second = banks_of(e)
                bank0.wait_free(pe, i, second + 1)
                bank1.wait_free(pe, i, 2 * second + 1)
                bank2.wait_free(pe, i, 0)
                for k in range(2):
                    ins = nc.tensor.matmul(B2[:, 0:CH], rg[e][:, k, :], uT[e][:, k, :], start=k == 0, stop=k == 1)
                ins.then_inc(bank2.full, 1)
                for n in range(L // 2):
                    m = L - 1 - n
                    nc.tensor.matmul(B1[:, n * GH:(n + 1) * GH], zg[e][:, m:m + 8, :],
                                     c1[:, bass.ds(i * QUAD + e, 1), :].rearrange("p a h -> p (a h)"),
                                     start=True, stop=True)
                nc.tensor.matmul(B1[:, P:2 * P], zg[e][:, L // 2:L, :],
                                 oo[:, bass.ds(i * QUAD + e, 1), 0:L // 2, :].rearrange("p a l h -> p (a l h)"),
                                 start=True, stop=True).then_inc(bank1.full, 1)

            def outputs(e, i):
                (out, bank0), (B1, bank1), (B2, bank2), second = banks_of(e)
                bank0.wait_free(pe, i, 2 + second)
                bank1.wait_free(pe, i + 1, 0)
                bank2.wait_free(pe, i + 1, 0)
                for t in range(CT):
                    c = slice(t * P, (t + 1) * P)
                    nc.tensor.matmul(out[:, t * 2 * P:(t + 1) * 2 * P], uT[e][:, 0, c], tg[e][:, 0:2 * P],
                                     start=True, stop=False)
                    nc.tensor.matmul(out[:, t * 2 * P + P:(t + 1) * 2 * P], uT[e][:, 1, c], tg[e][:, 0:P],
                                     start=False, stop=False)
                    ins = nc.tensor.matmul(out[:, t * 2 * P:(t + 1) * 2 * P],
                                           st[e][:, PAD - 1 + t * P:PAD - 1 + (t + 1) * P],
                                           oo[:, bass.ds(i * QUAD + e, 1), :, :].rearrange("p a l h -> p (a l h)"),
                                           start=False, stop=True)
                ins.then_inc(bank0.full, 1)

            with pe.Fori(0, QUADS) as i:
                for second in range(2):
                    pair = range(2 * second, 2 * second + 2)
                    for e in pair:
                        transposes(e, i)
                    for e in pair:
                        states_and_toeplitz(e, i)
                pe.wait_ge(steps_ready, i * (QUAD * LEVELS) + (QUAD * LEVELS + 2))
                for n in range(LEVELS):
                    for e in range(QUAD):
                        B2, bank2 = banks_of(e)[2]
                        d = 1 << n
                        bank2.wait_free(pe, i, 1 + n)
                        nc.tensor.matmul(B2[:, d:CH], step[:, e * LEVELS + n, :], st[e][:, PAD:PAD + CH - d],
                                         start=True, stop=True).then_inc(bank2.full, 1)
                for e in range(QUAD):
                    outputs(e, i)


def merge_and_route(nc, io, mix_dram, y_dram, x2_dram, xn_dram, logits):
    semaphores = []
    with ExitStack() as ctx:
        ctx.callback(end_phase, nc, semaphores)

        def sb(name, shape, dt=F32):
            return ctx.enter_context(nc.sbuf_tensor(name, shape, dt))

        def sem(name):
            semaphores.append(nc.alloc_semaphore(name=name))
            return semaphores[-1]

        R = NG + NE
        ident = sb("m_ident", [P, P])
        w_out = sb("w_out_sb", [P, KD, D])
        w_hi, w_lo = sb("m_w_hi", [P, KD, D], F32R), sb("m_w_lo", [P, KD, D], F32R)
        glu_w = sb("glu_w_sb", [P, 2, GW])
        glu_b = sb("glu_b_sb", [P, GW])
        w_r = sb("w_r_sb", [P, KD, R])
        b_r = sb("b_r_sb", [P, R])
        g_ffn = sb("m_g_ffn", [P, D])
        minus_half, eps = sb("m_minus_half", [P, 1]), sb("m_eps", [P, 1])
        xb = [sb(f"m_x{j}", [P, D]) for j in range(2)]
        mix = [sb(f"m_mix{j}", [P, D]) for j in range(2)]
        yb = [sb(f"m_y{j}", [P, GW]) for j in range(2)]
        ysq, yin, yth = sb("ysq", [P, GW]), sb("yin", [P, GW]), sb("yth", [P, GW])
        gy = [sb(f"gy{j}", [P, GW]) for j in range(2)]
        gyT = sb("gyT", [P, 2, P])
        gate, gate_th = sb("gate", [P, GW]), sb("gate_th", [P, GW])
        mT_hi, mT_lo = sb("mT_hi", [P, KD, P], F32R), sb("mT_lo", [P, KD, P], F32R)
        x2 = [sb(f"m_x2{j}", [P, D]) for j in range(2)]
        xn = [sb(f"m_xn{j}", [P, D]) for j in range(2)]
        sq = sb("m_sq", [P, D])
        ss, rs = sb("m_ss", [P, 1]), sb("m_rs", [P, 1])
        xnT = sb("xnT", [P, KD, P])

        b = [ctx.enter_context(nc.psum_tensor(f"m_bank{n}", [P, 512], F32)) for n in range(8)]
        uses = [1, 1, 1, 1, 2, 1, 1, 1]
        bank = [Bank(sem(f"m_full{n}"), sem(f"m_free{n}"), uses[n]) for n in range(8)]
        MIXT, PROD, GLU, LOGIT, XNT = 0, 2, 4, 5, 6

        small_in, w_hi_ready, w_lo_ready = (sem(n) for n in ("m_small_in", "m_w_hi_ready", "m_w_lo_ready"))
        w_in = [sem(f"m_w_in{k}") for k in range(KD)]
        half_set = sem("m_half_set")
        x_in = [sem(f"m_x_in{j}") for j in range(2)]
        mix_in = [sem(f"m_mix_in{j}") for j in range(2)]
        y_in = [sem(f"m_y_in{j}") for j in range(2)]
        x2_out = [sem(f"m_x2_out{j}") for j in range(2)]
        xn_out = [sem(f"m_xn_out{j}") for j in range(2)]
        ysq_ready, yin_ready, yth_ready, gy_ready = sem("ysq_ready"), sem("yin_ready"), sem("yth_ready"), sem("gy_ready")
        gate_ready, gate_th_ready, gated_ready = sem("gate_ready"), sem("gate_th_ready"), sem("gated_ready")
        mT_hi_ready = sem("mT_hi_ready")
        x2_ready, sq_ready, rs_ready, xn_ready = sem("m_x2_ready"), sem("m_sq_ready"), sem("m_rs_ready"), sem("m_xn_ready")
        norm_chain = sem("m_norm_chain")

        SMALL = [(ident, io["ident"]), (glu_w, io["glu_w"]), (glu_b, io["glu_b"]), (w_r, io["w_r"]), (b_r, io["b_r"]),
                 (g_ffn, io["g_ffn"])]
        factor = lambda k: (1.0, 0.5, 0.5, 0.25)[k // 2]
        tiled = lambda dram: dram.rearrange("(t p) d -> t p d", p=P)
        x_t, mix_t, y_t, x2_t, xn_t = map(tiled, (io["x"], mix_dram, y_dram, x2_dram, xn_dram))
        at = lambda dram, t: dram[bass.ds(t, 1)].rearrange("a p d -> (a p) d")
        fixed = lambda t: isinstance(t, int)
        has = lambda t: not fixed(t) or 0 <= t < TILES

        def run_slots(engine, prologue, slot, epilogue, last=2):
            prologue()
            for t in range(2):
                slot(t, t, 0)
            with engine.Fori(0, (TILES - 2 - last) // 2) as i:
                slot(i * 2 + 2, 0, i + 1)
                slot(i * 2 + 3, 1, i + 1)
            for t in range(TILES - last, TILES):
                slot(t, t % 2, t // 2)
            epilogue()

        nothing = lambda: None
        block = ctx.enter_context(nc.Block())

        @block.sync
        def _(sp):
            def load_y(t, j):
                sp.wait_ge(gy_ready, t + 1)
                sp.dma_start(yb[j][:], at(y_t, t)).then_inc(y_in[j], 16)

            def load_mix(t, j):
                if not (fixed(t) and t < 2):
                    for k in range(2):
                        bank[MIXT + k].wait_full(sp, t - 2, 0)
                sp.dma_start(mix[j][:, 0:3 * GW], at(mix_t, t)).then_inc(mix_in[j], 16)

            def load_x(t, j):
                sp.wait_ge(x2_ready, t + 1)
                sp.dma_start(xb[j][:], at(x_t, t)).then_inc(x_in[j], 16)

            def prologue():
                load_y(0, 0)
                load_y(1, 1)
                for dst, src in SMALL:
                    sp.dma_start(dst[:], src).then_inc(small_in, 16)
                for k in range(KD):
                    sp.dma_start(w_out[:, k, :], io["w_out"][:, k, :]).then_inc(w_in[k], 16)
                load_mix(0, 0)
                load_mix(1, 1)
                load_x(0, 0)
                load_y(2, 0)

            def slot(t, j, i):
                if not fixed(t) or t + 3 < TILES:
                    load_y(t + 3, 1 - j)
                if has(t + 2):
                    load_mix(t + 2, j)
                if has(t + 1):
                    load_x(t + 1, 1 - j)
                sp.wait_ge(x2_ready, t + 3)
                sp.dma_start(at(x2_t, t), x2[j][:]).then_inc(x2_out[j], 16)
                sp.wait_ge(xn_ready, t + 1)
                sp.dma_start(at(xn_t, t), xn[j][:]).then_inc(xn_out[j], 16)

            def epilogue():
                for j in range(2):
                    sp.wait_ge(x2_out[j], 16 * (TILES // 2 + 1))
                    sp.wait_ge(xn_out[j], 16 * (TILES // 2 + 1))

            run_slots(sp, prologue, slot, epilogue, last=4)

        @block.gpsimd
        def _(pool):
            nchain = Chain(pool, norm_chain, 1)
            pool.sem_inc(x2_ready, 2)
            pool.sem_inc(gy_ready, 2)
            for j in range(2):
                pool.sem_inc(x2_out[j], 16)
                pool.sem_inc(xn_out[j], 16)
            nc.gpsimd.memset(minus_half[:], -0.5).then_inc(half_set, 1)
            nc.gpsimd.memset(eps[:], EPS).then_inc(half_set, 1)
            pool.wait_ge(half_set, 2)

            def slot(t, j, i):
                nchain.tile(t)
                if not (fixed(t) and t == 0):
                    pool.wait_ge(xn_ready, t)
                pool.wait_ge(sq_ready, t + 1)
                nchain(nc.gpsimd.tensor_tensor(rs[:], ss[:], eps[:], ALU.add))
                nc.gpsimd.tensor_tensor(rs[:], rs[:], minus_half[:], ALU.pow).then_inc(rs_ready, 1)

            run_slots(pool, nothing, slot, nothing)

        @block.scalar
        def _(act):
            def square_y(t, j, i):
                act.wait_ge(y_in[j], (i + 1) * 16)
                if not (fixed(t) and t == 0):
                    act.wait_ge(yin_ready, t)
                nc.scalar.activation(ysq[:], yb[j][:], ACT.Square, scale=GELU_A ** 0.5).then_inc(ysq_ready, 1)

            def gelu(t):
                act.wait_ge(yin_ready, t + 1)
                act.wait_ge(gy_ready, t + 2)
                nc.scalar.activation(yth[:], yin[:], ACT.Tanh, scale=GELU_B).then_inc(yth_ready, 1)

            def evac_gyT(t):
                bank[GLU].wait_full(act, t, 0)
                nc.scalar.activation(gyT[:], b[GLU][:, 0:2 * P].rearrange("p (k n) -> p k n", k=2), ACT.Copy)\
                    .then_inc(bank[GLU].free, 1)

            def gate_tanh(t):
                act.wait_ge(gate_ready, t + 1)
                nc.scalar.activation(gate_th[:], gate[:], ACT.Tanh, scale=0.5).then_inc(gate_th_ready, 1)

            def evac_mT(t):
                for k in range(2):
                    bank[MIXT + k].wait_full(act, t, 0)
                    nc.scalar.activation(mT_hi[:, 4 * k:4 * k + 4, :], b[MIXT + k][:].rearrange("p (k n) -> p k n", k=4),
                                         ACT.Copy).then_inc(mT_hi_ready, 1)

            def evac_xnT(t):
                bank[XNT].wait_full(act, t, 0)
                nc.scalar.activation(xnT[:, 0:4, :], b[XNT][:].rearrange("p (k n) -> p k n", k=4), ACT.Copy)\
                    .then_inc(bank[XNT].free, 1)

            def slot(t, j, i):
                if has(t - 2):
                    evac_xnT(t - 2)
                if has(t + 2):
                    square_y(t + 2, j, i + 1)
                if has(t + 1):
                    gate_tanh(t + 1)
                if has(t + 2):
                    gelu(t + 2)
                    evac_gyT(t + 2)
                act.wait_ge(x2_ready, t + 3)
                nc.scalar.activation(sq[:], x2[j][:], ACT.Square, scale=D ** -0.5, accum_out=ss[:]).then_inc(sq_ready, 1)
                if has(t + 1):
                    evac_mT(t + 1)

            def prologue():
                for t in range(2):
                    square_y(t, t, 0)
                    gelu(t)
                    evac_gyT(t)
                    if t == 0:
                        for k in range(KD):
                            act.wait_ge(w_in[k], 16)
                            nc.scalar.activation(w_hi[:, k, :], w_out[:, k, :], ACT.Copy, scale=factor(k))\
                                .then_inc(w_hi_ready, 1)
                        gate_tanh(0)
                        evac_mT(0)

            def epilogue():
                for t in range(TILES - 2, TILES):
                    evac_xnT(t)

            run_slots(act, prologue, slot, epilogue)

        @block.vector
        def _(dve):
            V = nc.vector
            for k in bank:
                dve.sem_inc(k.free, 1)

            def gelu_arg(t, j):
                dve.wait_ge(ysq_ready, t + 1)
                V.scalar_tensor_tensor(yin[:], ysq[:], 1.0, yb[j][:], ALU.add, ALU.mult).then_inc(yin_ready, 1)

            def gelu(t, j):
                dve.wait_ge(yth_ready, t + 1)
                V.scalar_tensor_tensor(gy[j][:], yth[:], 1.0, yb[j][:], ALU.add, ALU.mult).then_inc(gy_ready, 1)

            def gate_arg(t):
                bank[GLU].wait_full(dve, t, 1)
                V.scalar_tensor_tensor(gate[:], b[GLU][:, 0:GW], 0.5, glu_b[:], ALU.mult, ALU.add)\
                    .then_inc(bank[GLU].free, 1)
                bank[GLU].wait_free(dve, t + 1, 0)
                dve.sem_inc(gate_ready, 1)

            def gated(t, j):
                dve.wait_ge(gate_th_ready, t + 1)
                V.scalar_tensor_tensor(mix[j][:, 3 * GW:D], gate_th[:], 1.0, gy[j][:], ALU.add, ALU.mult)\
                    .then_inc(gated_ready, 1)

            def evac_mT(t):
                for k in range(2):
                    part = slice(4 * k, 4 * k + 4)
                    bank[MIXT + k].wait_full(dve, t, 0)
                    dve.wait_ge(mT_hi_ready, t * 2 + (k + 1))
                    V.tensor_tensor(mT_lo[:, part, :], b[MIXT + k][:].rearrange("p (k n) -> p k n", k=4),
                                    mT_hi[:, part, :], ALU.subtract).then_inc(bank[MIXT + k].free, 1)

            def evac_xnT(t):
                bank[XNT + 1].wait_full(dve, t, 0)
                V.tensor_copy(xnT[:, 4:8, :], b[XNT + 1][:].rearrange("p (k n) -> p k n", k=4))\
                    .then_inc(bank[XNT + 1].free, 1)

            def logit(t):
                bank[LOGIT].wait_full(dve, t, 0)
                V.tensor_tensor(logits[:, bass.ds(t, 1), :].rearrange("p a r -> p (a r)"), b[LOGIT][:, 0:R], b_r[:],
                                ALU.add).then_inc(bank[LOGIT].free, 1)

            def slot(t, j, i):
                if has(t - 2):
                    evac_xnT(t - 2)
                if has(t + 1):
                    gate_arg(t + 1)
                if has(t + 2):
                    gelu_arg(t + 2, j)
                if has(t + 1):
                    gated(t + 1, 1 - j)
                if has(t + 2):
                    gelu(t + 2, j)
                dve.wait_ge(x_in[j], (i + 1) * 16)
                dve.wait_ge(x2_out[j], (i + 1) * 16)
                for n in range(2):
                    bank[PROD + n].wait_full(dve, t, 0)
                    V.tensor_tensor(x2[j][:, n * 512:(n + 1) * 512], b[PROD + n][:], xb[j][:, n * 512:(n + 1) * 512],
                                    ALU.add).then_inc(bank[PROD + n].free, 1)
                for n in range(2):
                    bank[PROD + n].wait_free(dve, t + 1, 0)
                dve.sem_inc(x2_ready, 1)
                if has(t - 2):
                    logit(t - 2)
                if has(t + 1):
                    evac_mT(t + 1)
                dve.wait_ge(xn_out[j], (i + 1) * 16)
                dve.wait_ge(rs_ready, t + 1)
                V.scalar_tensor_tensor(xn[j][:], x2[j][:], rs[:, 0:1], g_ffn[:], ALU.mult, ALU.mult)\
                    .then_inc(xn_ready, 1)

            def prologue():
                for t in range(2):
                    gelu_arg(t, t)
                    gelu(t, t)
                    if t == 0:
                        for k in range(KD):
                            dve.wait_ge(w_hi_ready, k + 1)
                            V.scalar_tensor_tensor(w_lo[:, k, :], w_out[:, k, :], factor(k), w_hi[:, k, :], ALU.mult,
                                                   ALU.subtract).then_inc(w_lo_ready, 1)
                        dve.wait_ge(small_in, 16 * len(SMALL))
                        gate_arg(0)
                        gated(0, 0)
                        evac_mT(0)

            def epilogue():
                for t in range(TILES - 2, TILES):
                    evac_xnT(t)
                    logit(t)

            run_slots(dve, prologue, slot, epilogue)

        @block.tensor
        def _(pe):
            def glu_transpose(t, j):
                pe.wait_ge(gy_ready, t + 3)
                bank[GLU].wait_free(pe, t, 0)
                for c in range(2):
                    ins = nc.tensor.transpose(b[GLU][:, c * P:(c + 1) * P], gy[j][:, c * P:(c + 1) * P], ident[:])
                ins.then_inc(bank[GLU].full, 1)

            def glu_product(t):
                bank[GLU].wait_free(pe, t, 1)
                for c in range(2):
                    ins = nc.tensor.matmul(b[GLU][:, 0:GW], gyT[:, c, :], glu_w[:, c, :], start=c == 0, stop=c == 1)
                ins.then_inc(bank[GLU].full, 1)

            def mix_transpose(t, j, i):
                pe.wait_ge(gated_ready, t + 1)
                pe.wait_ge(mix_in[j], (i + 1) * 16)
                for k in range(2):
                    bank[MIXT + k].wait_free(pe, t, 0)
                    for c in range(4):
                        ins = nc.tensor.transpose(b[MIXT + k][:, c * P:(c + 1) * P],
                                                  mix[j][:, (4 * k + c) * P:(4 * k + c + 1) * P], ident[:])
                    ins.then_inc(bank[MIXT + k].full, 1)

            def xn_transpose(t, j):
                pe.wait_ge(xn_ready, t + 1)
                for k in range(2):
                    bank[XNT + k].wait_free(pe, t, 0)
                    for c in range(4):
                        ins = nc.tensor.transpose(b[XNT + k][:, c * P:(c + 1) * P],
                                                  xn[j][:, (4 * k + c) * P:(4 * k + c + 1) * P], ident[:])
                    ins.then_inc(bank[XNT + k].full, 1)

            def route(t):
                bank[XNT].wait_free(pe, t + 1, 0)
                bank[XNT + 1].wait_free(pe, t + 1, 0)
                bank[LOGIT].wait_free(pe, t, 0)
                for k in range(KD):
                    ins = nc.tensor.matmul(b[LOGIT][:, 0:R], xnT[:, k, :], w_r[:, k, :], start=k == 0, stop=k == KD - 1)
                ins.then_inc(bank[LOGIT].full, 1)

            def product(t, n):
                if n == 0:
                    for k in range(2):
                        bank[MIXT + k].wait_free(pe, t + 1, 0)
                bank[PROD + n].wait_free(pe, t, 0)
                cols = slice(n * 512, (n + 1) * 512)
                for k in range(KD):
                    nc.tensor.matmul(b[PROD + n][:], mT_hi[:, k, :], w_hi[:, k, cols], start=k == 0, stop=False)
                    nc.tensor.matmul(b[PROD + n][:], mT_hi[:, k, :], w_lo[:, k, cols], start=False, stop=False)
                    ins = nc.tensor.matmul(b[PROD + n][:], mT_lo[:, k, :], w_hi[:, k, cols], start=False,
                                           stop=k == KD - 1)
                ins.then_inc(bank[PROD + n].full, 1)

            def slot(t, j, i):
                product(t, 0)
                if has(t + 2):
                    glu_transpose(t + 2, j)
                product(t, 1)
                if has(t - 2):
                    route(t - 2)
                if has(t + 1):
                    mix_transpose(t + 1, 1 - j, i + j)
                if has(t + 2):
                    glu_product(t + 2)
                if has(t - 1):
                    xn_transpose(t - 1, 1 - j)

            def prologue():
                pe.wait_ge(small_in, 16 * len(SMALL))
                glu_transpose(0, 0)
                glu_product(0)
                mix_transpose(0, 0, 0)
                glu_transpose(1, 1)
                glu_product(1)
                pe.wait_ge(w_lo_ready, KD)

            def epilogue():
                route(TILES - 2)
                xn_transpose(TILES - 1, 1)
                route(TILES - 1)

            run_slots(pe, prologue, slot, epilogue)


def plan_experts(nc, io, logits, wts, dest, block_rows, block_expert, block_slot, expert_end):
    semaphores = []
    with ExitStack() as ctx:
        ctx.callback(end_phase, nc, semaphores)

        def sb(name, shape, dt=F32):
            return ctx.enter_context(nc.sbuf_tensor(name, shape, dt))

        def sem(name):
            semaphores.append(nc.alloc_semaphore(name=name))
            return semaphores[-1]

        T = TILES
        before = sb("p_before", [P, P])
        ones = sb("p_ones", [P, P])
        reset = sb("p_reset", [P, NE * T])
        rank4, rank8 = sb("rank4", [P, NG]), sb("rank8", [P, NE_G])
        ident = sb("p_ident", [P, P])
        block_no = sb("block_no", [P, 1])
        gm, mv, sh = sb("p_gm", [P, T]), sb("p_mv", [P, T]), sb("p_sh", [P, T, NG])
        ohg, vg = sb("ohg", [P, T, NG]), sb("vg", [P, T, NG])
        eg, pg = sb("eg", [P, T, NG]), sb("pg", [P, T])
        big = sb("p_big", [P, T, NG, NE_G])
        ein, v8 = sb("ein", [P, T, NE_G]), sb("v8", [P, T, NE_G])
        m1, m2 = sb("m1", [P, T]), sb("m2", [P, T])
        oh1, oh2 = sb("oh1", [P, T, NE_G]), sb("oh2", [P, T, NE_G])
        dl, el = sb("p_dl", [P, T]), sb("p_el", [P, T])
        pair = [sb(f"pair{k}", [P, T, NG, NE_G]) for k in range(2)]
        both = sb("p_both", [P, T * NE], F32R)
        before_r, ones_r = sb("p_before_r", [P, P], F32R), sb("p_ones_r", [P, P], F32R)
        tot, incl, base = sb("p_tot", [P, NE, T]), sb("p_incl", [P, NE, T]), sb("p_base", [P, NE, T])
        row = sb("p_row", [P, T, NE])
        nb, ni, endb, startr = sb("p_nb", [P, NE]), sb("p_ni", [P, NE], I32), sb("p_endb", [P, NE]), sb("p_startr", [P, NE])
        drow = sb("p_drow", [P, 2, T])
        dlow, dhigh = sb("p_dlow", [P, 2, T], I32), sb("p_dhigh", [P, 2, T], I32)
        flow, fhigh = sb("p_flow", [P, 2, T]), sb("p_fhigh", [P, 2, T])
        token = sb("p_token", [P, T])
        lane_no, column_no = sb("lane_no", [P, P]), sb("column_no", [P, BLOCKS])
        BATCH = 8
        BW = BLOCKS + 1
        lane_is = [sb(f"lane_is{j}", [P, BATCH, P], F32R) for j in range(2)]
        block_is = [sb(f"block_is{j}", [P, BATCH, BLOCKS]) for j in range(2)]
        token_at = [sb(f"token_at{j}", [P, BATCH, BW], F32R) for j in range(2)]
        cmp, bexp = sb("p_cmp", [P, NE]), sb("p_bexp", [P, 1])
        brow, ringpos = sb("p_brow", [1, BLOCKS]), sb("p_ringpos", [1, BLOCKS])

        b = [ctx.enter_context(nc.psum_tensor(f"p_bank{n}", [P, 512], F32)) for n in range(6)]
        consts_in, shifted, e_done, d_ready, el_ready = (sem(n) for n in ("p_consts_in", "shifted", "e_done", "d_ready",
                                                                          "el_ready"))
        both_ready, counted, place_ready, lane_ready, block_ready, token_ready, placed = (
            sem(n) for n in ("both_ready", "counted", "place_ready", "lane_ready", "block_ready", "token_ready",
                             "placed"))
        BATCHES = [(k, q) for k in range(2) for q in range(T // BATCH)]
        chain_sem, column_set = sem("p_dve_chain"), sem("column_set")
        ones_ready, block_counted, block_row_ready = sem("ones_ready"), sem("block_counted"), sem("block_row_ready")
        LOADS = [(before, io["before"]), (ones, io["ones"]), (reset, io["reset"]), (rank4, io["rank4"]),
                 (rank8, io["rank8"]), (block_no, io["block_no"]), (ident, io["ident"]), (token, io["token"]), (lane_no, io["lane_no"]),
                 (column_no, io["column_no"])]
        over = lambda ap, n: ap.unsqueeze(1).to_broadcast([P, T, n])

        block = ctx.enter_context(nc.Block())

        @block.sync
        def _(sp):
            for dst, src in LOADS:
                sp.dma_start(dst[:], src).then_inc(consts_in, 16)

        @block.gpsimd
        def _(pool):
            pool.wait_ge(consts_in, 16 * len(LOADS))
            for j in range(2):
                nc.gpsimd.tensor_tensor(token_at[j][:, :, BLOCKS:BW], ones[:, 0:BATCH].unsqueeze(2),
                                        ones[:, 0:BATCH].unsqueeze(2), ALU.subtract).then_inc(column_set, 1)
            for n, (k, q) in enumerate(BATCHES):
                pool.wait_ge(block_ready, n + 1)
                if n >= 2:
                    pool.wait_ge(placed, n - 1)
                tiles = token[:, q * BATCH:(q + 1) * BATCH]
                nc.gpsimd.tensor_tensor(token_at[n % 2][:, :, 0:BLOCKS], block_is[n % 2][:],
                                        tiles.unsqueeze(2).to_broadcast([P, BATCH, BLOCKS]), ALU.mult)\
                    .then_inc(token_ready, 1)

        @block.scalar
        def _(act):
            act.wait_ge(consts_in, 16 * len(LOADS))
            nc.scalar.activation(before_r[:], before[:], ACT.Copy).then_inc(ones_ready, 1)
            nc.scalar.activation(ones_r[:], ones[:], ACT.Copy).then_inc(ones_ready, 1)
            act.wait_ge(shifted, 1)
            nc.scalar.activation(eg[:], sh[:], ACT.Exp).then_inc(e_done, 1)
            act.wait_ge(d_ready, 1)
            nc.scalar.activation(el[:], dl[:], ACT.Exp).then_inc(el_ready, 1)

        @block.tensor
        def _(pe):
            pe.wait_ge(consts_in, 16 * len(LOADS))
            pe.wait_ge(both_ready, 1)
            pe.wait_ge(ones_ready, 2)
            for n in range(2):
                nc.tensor.matmul(b[n][:], before_r[:], both[:, n * 512:(n + 1) * 512], start=True, stop=True)
            for n in range(2):
                ins = nc.tensor.matmul(b[2 + n][:], ones_r[:], both[:, n * 512:(n + 1) * 512], start=True, stop=True)
            ins.then_inc(counted, 1)
            pe.wait_ge(block_counted, 1)
            nc.tensor.matmul(b[5][0:1, 0:P], bexp[:], ident[:], start=True, stop=True).then_inc(block_row_ready, 1)
            pe.wait_ge(column_set, 2)
            for n in range(len(BATCHES)):
                pe.wait_ge(lane_ready, n + 1)
                pe.wait_ge(token_ready, n + 1)
                for t in range(BATCH):
                    ins = nc.tensor.matmul(b[4][:, 0:BW], lane_is[n % 2][:, t, :], token_at[n % 2][:, t, :],
                                           start=n == 0 and t == 0, stop=n == len(BATCHES) - 1 and t == BATCH - 1)
                ins.then_inc(placed, 1)

        @block.vector
        def _(dve):
            V = nc.vector
            chain = Chain(dve, chain_sem)
            lg = logits[:, :, 0:NG]
            le = logits[:, :, NG:NG + NE].rearrange("p t (g e) -> p t g e", g=NG)
            dve.wait_ge(consts_in, 16 * len(LOADS))

            def first_max(out, x, largest, ranks, scratch, n):
                chain(V.tensor_reduce(largest, x, AX.X, ALU.max))
                chain(V.tensor_tensor(scratch, x, bc(largest, n), ALU.is_equal))
                chain(V.tensor_tensor(scratch, scratch, over(ranks[:], n), ALU.mult))
                chain(V.tensor_reduce(mv[:], scratch, AX.X, ALU.max))
                chain(V.tensor_tensor(out, scratch, bc(mv[:], n), ALU.is_equal))

            first_max(ohg[:], lg, gm[:], rank4, vg[:], NG)
            V.tensor_tensor(sh[:], lg, bc(gm[:], NG), ALU.subtract).then_inc(shifted, 1)
            chosen = ohg[:].unsqueeze(3).to_broadcast([P, T, NG, NE_G])
            chain(V.tensor_tensor(big[:], le, chosen, ALU.mult))
            chain(V.tensor_reduce(ein[:], big[:].rearrange("p t g e -> p t e g"), AX.X, ALU.add))
            first_max(oh1[:], ein[:], m1[:], rank8, v8[:], NE_G)
            chain(V.scalar_tensor_tensor(ein[:], oh1[:], -1e30, ein[:], ALU.mult, ALU.add))
            first_max(oh2[:], ein[:], m2[:], rank8, v8[:], NE_G)
            V.tensor_tensor(dl[:], m2[:], m1[:], ALU.subtract).then_inc(d_ready, 1)
            for k, oh in enumerate((oh1, oh2)):
                chain(V.tensor_tensor(pair[k][:], chosen, oh[:].unsqueeze(2).to_broadcast([P, T, NG, NE_G]), ALU.mult))
            V.tensor_tensor(both[:], pair[0][:].rearrange("p t g e -> p (t g e)"),
                            pair[1][:].rearrange("p t g e -> p (t g e)"), ALU.add).then_inc(both_ready, 1)
            dve.wait_ge(e_done, 1)
            chain(V.tensor_reduce(pg[:], eg[:], AX.X, ALU.add))
            chain(V.reciprocal(pg[:], pg[:]))
            dve.wait_ge(el_ready, 1)
            chain(V.tensor_scalar(dl[:], el[:], 1.0, None, ALU.add))
            chain(V.reciprocal(dl[:], dl[:]))
            chain(V.tensor_tensor(wts[:, 0, :], dl[:], pg[:], ALU.mult))
            chain(V.tensor_tensor(wts[:, 1, :], wts[:, 0, :], el[:], ALU.mult))
            dve.wait_ge(counted, 1)
            for n in range(2):
                chain(V.tensor_copy(tot[:, :, n * 16:(n + 1) * 16], b[2 + n][:].rearrange("p (t e) -> p e t", e=NE)))
            flat = lambda ap: ap.rearrange("p e t -> p (e t)")
            chain(V.tensor_tensor_scan(flat(incl[:]), reset[:], flat(tot[:]), 0.0, ALU.mult, ALU.add))
            chain(V.tensor_scalar(nb[:], incl[:, :, T - 1], float(P - 1), None, ALU.add))
            chain(V.tensor_copy(ni[:], nb[:]))
            chain(V.tensor_scalar(ni[:], ni[:], 7, None, ALU.arith_shift_right))
            chain(V.tensor_copy(nb[:], ni[:]))
            chain(V.tensor_scalar(nb[:], nb[:], 1.0, None, ALU.max))
            chain(V.tensor_tensor_scan(endb[:], ones[:, 0:NE], nb[:], 0.0, ALU.mult, ALU.add))
            chain(V.tensor_tensor(cmp[:], block_no[:].to_broadcast([P, NE]), endb[:], ALU.is_ge))
            chain(V.tensor_reduce(bexp[:], cmp[:], AX.X, ALU.add))
            V.tensor_scalar(bexp[:], bexp[:], float(NE - 1), None, ALU.min).then_inc(block_counted, 1)
            chain(V.tensor_tensor(startr[:], endb[:], nb[:], ALU.subtract))
            chain(V.tensor_tensor(base[:], incl[:], tot[:], ALU.subtract))
            chain(V.tensor_scalar(startr[:], startr[:], float(P), None, ALU.mult))
            chain(V.tensor_tensor(base[:], base[:], bc(startr[:], T), ALU.add))
            for n in range(2):
                tiles = slice(n * 16, (n + 1) * 16)
                chain(V.tensor_tensor(row[:, tiles, :], b[n][:].rearrange("p (t e) -> p t e", e=NE),
                                      base[:, :, tiles].rearrange("p e t -> p t e"), ALU.add))
            for k in range(2):
                chain(V.tensor_tensor(pair[k][:].rearrange("p t g e -> p t (g e)"),
                                      pair[k][:].rearrange("p t g e -> p t (g e)"), row[:], ALU.mult))
                chain(V.tensor_reduce(drow[:, k, :], pair[k][:].rearrange("p t g e -> p t (g e)"), AX.X, ALU.add))
            chain(V.tensor_copy(dest[:], drow[:]))
            chain(V.tensor_scalar(dlow[:], dest[:], P - 1, None, ALU.bitwise_and))
            chain(V.tensor_scalar(dhigh[:], dest[:], 7, None, ALU.arith_shift_right))
            chain(V.tensor_copy(flow[:], dlow[:]))
            chain(V.tensor_copy(fhigh[:], dhigh[:]))
            for n, (k, q) in enumerate(BATCHES):
                tiles = slice(q * BATCH, (q + 1) * BATCH)
                if n >= 2:
                    dve.wait_ge(placed, n - 1)
                V.tensor_tensor(block_is[n % 2][:], column_no[:].unsqueeze(1).to_broadcast([P, BATCH, BLOCKS]),
                                fhigh[:, k, tiles].unsqueeze(2).to_broadcast([P, BATCH, BLOCKS]), ALU.is_equal)\
                    .then_inc(block_ready, 1)
                V.tensor_tensor(lane_is[n % 2][:], lane_no[:].unsqueeze(1).to_broadcast([P, BATCH, P]),
                                flow[:, k, tiles].unsqueeze(2).to_broadcast([P, BATCH, P]), ALU.is_equal)\
                    .then_inc(lane_ready, 1)
            dve.wait_ge(block_row_ready, 1)
            chain(V.tensor_copy(brow[:], b[5][0:1, 0:BLOCKS]))
            chain(V.tensor_copy(block_expert[:], brow[:]))
            for m in range(3):
                chain(V.tensor_scalar(ringpos[:], brow[:], 3.0, float(m), ALU.mult, ALU.add))
                chain(V.tensor_copy(block_slot[:, m, :], ringpos[:]))
            chain(V.tensor_scalar(block_slot[:], block_slot[:], 3, None, ALU.bitwise_and))
            chain(V.tensor_scalar(nb[:], endb[:], 1.0, None, ALU.add))
            chain(V.tensor_copy(expert_end[:, 2:2 + NE], nb[0:1, :]))
            chain(V.tensor_copy(expert_end[:, 0:2], ones[0:1, 0:2]))
            dve.wait_ge(placed, len(BATCHES))
            chain(V.tensor_copy(block_rows[:], b[4][:, 0:BLOCKS]))


def run_experts(nc, io, block_rows, block_expert, block_slot, expert_end, xn_dram, out_dram):
    semaphores = []
    with ExitStack() as ctx:
        ctx.callback(end_phase, nc, semaphores)

        def sb(name, shape, dt=F32):
            return ctx.enter_context(nc.sbuf_tensor(name, shape, dt))

        def sem(name):
            semaphores.append(nc.alloc_semaphore(name=name))
            return semaphores[-1]

        RING, RAW = 4, 3
        W_PARTS = 8
        ident, ident_r = sb("e_ident", [P, P]), sb("e_ident_r", [P, P], F32R)
        w_hi = sb("w_hi", [P, RING * W_PARTS, 512], F32R)
        w_lo = sb("w_lo", [P, RING * W_PARTS, 512], F32R)
        raw = [sb(f"w_raw{r}", [P, W_PARTS // 2, 512]) for r in range(RAW)]
        icol = sb("icol", [P, 1], I32)
        xg = sb("xg", [P, D])
        x_hi, x_lo = sb("x_hi", [P, D], F32R), sb("x_lo", [P, D], F32R)
        xT_hi, xT_lo = sb("e_xT_hi", [P, KD, P], F32R), sb("e_xT_lo", [P, KD, P], F32R)
        sg, up, hh = sb("sg", [P, FE]), sb("up", [P, FE]), sb("hh", [P, FE])
        h_hi, h_lo = sb("h_hi", [P, FE], F32R), sb("h_lo", [P, FE], F32R)
        hT_hi, hT_lo = sb("hT_hi", [P, KF, P], F32R), sb("hT_lo", [P, KF, P], F32R)
        ys = [sb(f"ys{j}", [P, D]) for j in range(2)]

        GATE, UP, HT, XT, DOWN = 0, 1, 2, 4, 6
        b = [ctx.enter_context(nc.psum_tensor(f"e_bank{n}", [P, 512], F32)) for n in range(8)]
        uses = [1, 1, 1, 1, 2, 2, 1, 1]
        bank = [Bank(sem(f"e_full{n}"), sem(f"e_free{n}"), uses[n]) for n in range(8)]
        consts_in, ident_set = sem("e_consts_in"), sem("e_ident_set")
        raw_in = [sem(f"raw_in{r}") for r in range(RAW)]
        w_hi_ready = sem("w_hi_ready")
        w_split = sem("w_split")
        blocks_through = [sem(f"blocks_through{m}") for m in range(3)]
        icol_ready, pool_passed = sem("icol_ready"), sem("e_pool_passed")
        x_in = sem("e_x_in")
        x_hi_ready, x_lo_ready = sem("x_hi_ready"), sem("x_lo_ready")
        hh_ready, h_hi_ready, h_lo_ready = sem("hh_ready"), sem("h_hi_ready"), sem("h_lo_ready")
        y_out = [sem(f"e_y_out{j}") for j in range(2)]
        out_b = out_dram.rearrange("(s p) d -> s p d", p=P)

        def run_slots(engine, prologue, slot, epilogue):
            prologue()
            slot(0, 0, 0, False, True, True)
            with engine.Fori(0, (BLOCKS - 3) // 2) as i:
                slot(i * 2 + 1, 1, i, True, True, True)
                slot(i * 2 + 2, 0, i + 1, True, True, True)
            slot(BLOCKS - 2, (BLOCKS - 2) % 2, (BLOCKS - 2) // 2, True, True, False)
            slot(BLOCKS - 1, (BLOCKS - 1) % 2, (BLOCKS - 1) // 2, True, False, False)
            epilogue()

        assert BLOCKS % 2 == 1 and NE % RING == 0
        nothing = lambda: None
        block = ctx.enter_context(nc.Block())

        @block.sync
        def _(sp):
            sp.dma_start(ident[:], io["ident"]).then_inc(consts_in, 16)
            quarter = W_PARTS // 2
            with sp.Fori(0, NE) as e:
                for m, name in enumerate(("w_gate", "w_up", "w_down")):
                    w = io[name][bass.ds(e, 1)].rearrange("a (k p) f -> p (a k) f", p=P)
                    rows = w.shape[1] // 2
                    for half in range(2):
                        r = (2 * m + half) % RAW
                        sp.wait_ge(w_split, e * 6 + 2 * m + half + 1)
                        sp.dma_start(raw[r][:].rearrange("p (k c) f -> p k (c f)", k=rows),
                                     w[:, half * rows:(half + 1) * rows, :]).then_inc(raw_in[r], 16)

        @block.vector
        def _(dve):
            V = nc.vector
            for k in bank:
                dve.sem_inc(k.free, 1)
            dve.sem_inc(w_split, RAW)
            for m in range(3):
                dve.sem_inc(blocks_through[m], 1)
            with dve.Fori(0, NE // RING) as i:
                for n in range(RING):
                    for m in range(3):
                        slot = (3 * n + m) % RING
                        older, which = (2, 2) if m == 0 else (1, m - 1)
                        end = dve.value_load(expert_end[0:1, bass.ds(i * RING + n + 2 - older, 1)], min_val=1,
                                             max_val=BLOCKS + 1)
                        dve.wait_ge(blocks_through[which], end)
                        for half in range(2):
                            r = (2 * m + half) % RAW
                            at = slot * W_PARTS + half * W_PARTS // 2
                            part = slice(at, at + W_PARTS // 2)
                            count = i * 6 * RING + (6 * n + 2 * m + half)
                            dve.wait_ge(raw_in[r], i * 32 * RING + 16 * (2 * n + (2 * m + half) // RAW + 1))
                            V.tensor_copy(w_hi[:, part, :], raw[r][:]).then_inc(w_hi_ready, 1)
                            dve.wait_ge(w_hi_ready, count + 1)
                            V.tensor_tensor(w_lo[:, part, :], raw[r][:], w_hi[:, part, :], ALU.subtract)\
                                .then_inc(w_split, 1)

        @block.gpsimd
        def _(pool):
            for j in range(2):
                pool.sem_inc(y_out[j], 16)

            def gather(s):
                if not (isinstance(s, int) and s == 0):
                    pool.wait_ge(x_lo_ready, s)
                pass_wait(pool, pool_passed)
                nc.gpsimd.tensor_copy(icol[:], block_rows[:, bass.ds(s, 1)]).then_inc(icol_ready, 1)
                pool.wait_ge(icol_ready, s + 1)
                pass_wait(pool, pool_passed)
                pool.indirect_dma_start(out=xg[:], out_offset=None, in_=xn_dram,
                                        in_offset=bass.IndirectOffsetOnAxis(ap=icol[:, 0:1], axis=0))\
                    .then_inc(x_in, 16)

            def split_x(s):
                pool.wait_ge(x_in, s * 16 + 16)
                pool.wait_ge(x_hi_ready, s + 1)
                if not (isinstance(s, int) and s == 0):
                    bank[XT + 1].wait_full(pool, s - 1, 1)
                nc.gpsimd.tensor_tensor(x_lo[:], xg[:], x_hi[:], ALU.subtract).then_inc(x_lo_ready, 1)

            def split_h(s, first):
                bank[GATE].wait_free(pool, s + 1, 0)
                bank[UP].wait_free(pool, s + 1, 0)
                if not first:
                    pool.wait_ge(h_lo_ready, s)
                nc.gpsimd.tensor_tensor(hh[:], sg[:], up[:], ALU.mult).then_inc(hh_ready, 1)
                pool.wait_ge(hh_ready, s + 1)
                pool.wait_ge(h_hi_ready, s + 1)
                if not first:
                    bank[HT + 1].wait_full(pool, s - 1, 0)
                nc.gpsimd.tensor_tensor(h_lo[:], hh[:], h_hi[:], ALU.subtract).then_inc(h_lo_ready, 1)

            def slot(s, j, i, before, after, after2):
                if after2:
                    gather(s + 2)
                split_h(s, not before)
                if after2:
                    split_x(s + 2)

            def prologue():
                for s in range(2):
                    gather(s)
                    split_x(s)

            run_slots(pool, prologue, slot, nothing)

        @block.scalar
        def _(act):
            def split_x(s):
                act.wait_ge(x_in, s * 16 + 16)
                if not (isinstance(s, int) and s == 0):
                    act.wait_ge(x_lo_ready, s)
                nc.scalar.activation(x_hi[:], xg[:], ACT.Copy).then_inc(x_hi_ready, 1)

            def evac_xT(s, part):
                for k in range(2):
                    bank[XT + k].wait_full(act, s, part)
                    nc.scalar.activation((xT_hi, xT_lo)[part][:, 4 * k:4 * k + 4, :],
                                         b[XT + k][:].rearrange("p (k n) -> p k n", k=4), ACT.Copy)\
                        .then_inc(bank[XT + k].free, 1)

            def evac_hT(s):
                for k, part in enumerate((hT_hi, hT_lo)):
                    bank[HT + k].wait_full(act, s, 0)
                    nc.scalar.activation(part[:], b[HT + k][:].rearrange("p (k n) -> p k n", k=KF), ACT.Copy)\
                        .then_inc(bank[HT + k].free, 1)

            def evac_y(s, j, i, n):
                if n == 0:
                    act.wait_ge(y_out[j], (i + 1) * 16)
                bank[DOWN + n].wait_full(act, s, 0)
                nc.scalar.activation(ys[j][:, n * 512:(n + 1) * 512], b[DOWN + n][:], ACT.Copy)\
                    .then_inc(bank[DOWN + n].free, 1)
                if n == 1:
                    act.sem_inc(blocks_through[2], 1)
                    for k in range(2):
                        bank[DOWN + k].wait_free(act, s + 1, 0)
                    act.dma_start(out_b[bass.ds(s, 1)].rearrange("a p d -> (a p) d"), ys[j][:]).then_inc(y_out[j], 16)

            def slot(s, j, i, before, after, after2):
                bank[GATE].wait_full(act, s, 0)
                act.sem_inc(blocks_through[0], 1)
                if before:
                    act.wait_ge(hh_ready, s)
                nc.scalar.activation(sg[:], b[GATE][:], ACT.Silu).then_inc(bank[GATE].free, 1)
                if before:
                    evac_hT(s - 1)
                bank[UP].wait_full(act, s, 0)
                act.sem_inc(blocks_through[1], 1)
                nc.scalar.activation(up[:], b[UP][:], ACT.Copy).then_inc(bank[UP].free, 1)
                if after:
                    evac_xT(s + 1, 0)
                act.wait_ge(hh_ready, s + 1)
                if before:
                    bank[HT].wait_full(act, s - 1, 0)
                    act.wait_ge(h_lo_ready, s)
                nc.scalar.activation(h_hi[:], hh[:], ACT.Copy).then_inc(h_hi_ready, 1)
                if before:
                    evac_y(s - 1, 1 - j, i - 1 + j, 0)
                if after:
                    evac_xT(s + 1, 1)
                if after2:
                    split_x(s + 2)
                if before:
                    evac_y(s - 1, 1 - j, i - 1 + j, 1)

            def prologue():
                act.wait_ge(consts_in, 16)
                nc.scalar.activation(ident_r[:], ident[:], ACT.Copy).then_inc(ident_set, 1)
                split_x(0)
                evac_xT(0, 0)
                evac_xT(0, 1)
                split_x(1)

            def epilogue():
                s = BLOCKS - 1
                evac_hT(s)
                for n in range(2):
                    evac_y(s, s % 2, s // 2, n)

            run_slots(act, prologue, slot, epilogue)
            act.wait_ge(y_out[0], 16 * ((BLOCKS + 1) // 2 + 1))
            act.wait_ge(y_out[1], 16 * (BLOCKS // 2 + 1))

        @block.tensor
        def _(pe):
            pe.wait_ge(ident_set, 1)

            def transpose(bank_at, out, x, blocks):
                for c in blocks:
                    ins = nc.tensor.matmul(out[:, (c % 4) * P:(c % 4 + 1) * P], x[:, c * P:(c + 1) * P], ident_r[:],
                                           start=True, stop=True)
                ins.then_inc(bank_at.full, 1)

            def transpose_x(s, part):
                pe.wait_ge((x_hi_ready, x_lo_ready)[part], s + 1)
                for k in range(2):
                    bank[XT + k].wait_free(pe, s, part)
                    transpose(bank[XT + k], b[XT + k], (x_hi, x_lo)[part], range(4 * k, 4 * k + 4))

            def transpose_h(s):
                pe.wait_ge(h_lo_ready, s + 1)
                for k, part in enumerate((h_hi, h_lo)):
                    bank[HT + k].wait_free(pe, s, 0)
                    transpose(bank[HT + k], b[HT + k], part, range(KF))

            def product(out, lhs_hi, lhs_lo, rhs, blocks):
                for k in range(blocks):
                    hi, lo = rhs(w_hi, k), rhs(w_lo, k)
                    nc.tensor.matmul(out[:], lhs_hi[:, k, :], hi, start=k == 0, stop=False)
                    nc.tensor.matmul(out[:], lhs_hi[:, k, :], lo, start=False, stop=False)
                    ins = nc.tensor.matmul(out[:], lhs_lo[:, k, :], hi, start=False, stop=k == blocks - 1)
                return ins

            def load_slot(s, m):
                return pe.value_load(block_slot[0:1, m:m + 1, bass.ds(s, 1)].rearrange("p a b -> p (a b)"),
                                     min_val=0, max_val=RING - 1)

            def load_expert(s):
                return pe.value_load(block_expert[0:1, bass.ds(s, 1)], min_val=0, max_val=NE - 1)

            def first(s, which, expert):
                at = load_slot(s, which)
                pe.wait_ge(w_split, expert * 6 + (2 * which + 2 + RAW))
                bank[which].wait_free(pe, s, 0)
                product(b[which], xT_hi, xT_lo,
                        lambda w, k: w[:, bass.ds(at * W_PARTS + k, 1), :].rearrange("p a f -> p (a f)"), KD)\
                    .then_inc(bank[which].full, 1)

            def down(s, n, at):
                bank[DOWN + n].wait_free(pe, s, 0)
                product(b[DOWN + n], hT_hi, hT_lo,
                        lambda w, k: w[:, bass.ds(at * W_PARTS + (2 * k + n), 1), :].rearrange("p a f -> p (a f)"), KF)\
                    .then_inc(bank[DOWN + n].full, 1)

            def begin_down(s):
                expert = load_expert(s)
                at = load_slot(s, 2)
                pe.wait_ge(w_split, expert * 6 + (6 + RAW))
                for k in range(2):
                    bank[HT + k].wait_free(pe, s + 1, 0)
                return at

            def slot(s, j, i, before, after, after2):
                expert = load_expert(s)
                for k in range(2):
                    bank[XT + k].wait_free(pe, s + 1, 0)
                first(s, GATE, expert)
                if before:
                    transpose_h(s - 1)
                first(s, UP, expert)
                if after:
                    transpose_x(s + 1, 0)
                if before:
                    at = begin_down(s - 1)
                    down(s - 1, 0, at)
                if after:
                    transpose_x(s + 1, 1)
                if before:
                    down(s - 1, 1, at)

            def prologue():
                transpose_x(0, 0)
                transpose_x(0, 1)

            def epilogue():
                s = BLOCKS - 1
                transpose_h(s)
                at = begin_down(s)
                for n in range(2):
                    down(s, n, at)

            run_slots(pe, prologue, slot, epilogue)


def combine(nc, io, wts, dest, x2_dram, experts_dram, out_dram):
    semaphores = []
    with ExitStack() as ctx:
        ctx.callback(end_phase, nc, semaphores)

        def sb(name, shape, dt=F32):
            return ctx.enter_context(nc.sbuf_tensor(name, shape, dt))

        def sem(name):
            semaphores.append(nc.alloc_semaphore(name=name))
            return semaphores[-1]

        g_fin = sb("g_fin_sb", [P, D])
        minus_half, eps = sb("f_minus_half", [P, 1]), sb("f_eps", [P, 1])
        icol = [[sb(f"f_icol{j}{k}", [P, 1], I32) for k in range(2)] for j in range(2)]
        ye = [[sb(f"f_y{j}{k}", [P, D]) for k in range(2)] for j in range(2)]
        xb = [sb(f"f_x{j}", [P, D]) for j in range(2)]
        acc = [sb(f"f_acc{j}", [P, D]) for j in range(2)]
        sq = sb("f_sq", [P, D])
        ss, rs = [sb(f"f_ss{j}", [P, 1]) for j in range(2)], [sb(f"f_rs{j}", [P, 1]) for j in range(2)]
        ot = [sb(f"f_out{j}", [P, D]) for j in range(2)]
        consts_in, half_set, icol_ready = sem("f_consts_in"), sem("f_half_set"), sem("f_icol_ready")
        pool_passed = sem("f_pool_passed")
        y_in = [[sem(f"f_y_in{j}{k}") for k in range(2)] for j in range(2)]
        x_in = [sem(f"f_x_in{j}") for j in range(2)]
        acc_ready, sq_ready, rs_ready, out_ready = (sem(n) for n in ("acc_ready", "f_sq_ready", "f_rs_ready", "out_ready"))
        stored = [sem(f"f_stored{j}") for j in range(2)]
        acc_chain, rs_chain = sem("acc_chain"), sem("rs_chain")
        x_t = x2_dram.rearrange("(t p) d -> t p d", p=P)
        o_t = out_dram.rearrange("(t p) d -> t p d", p=P)
        at = lambda dram, t: dram[bass.ds(t, 1)].rearrange("a p d -> (a p) d")
        block = ctx.enter_context(nc.Block())

        @block.sync
        def _(sp):
            sp.dma_start(g_fin[:], io["g_fin"]).then_inc(consts_in, 16)
            for j in range(2):
                sp.sem_inc(stored[j], 16)
            with sp.Fori(0, TILES // 2) as i:
                for j in range(2):
                    t = i * 2 + j
                    sp.wait_ge(acc_ready, t + 1)
                    sp.dma_start(xb[j][:], at(x_t, t)).then_inc(x_in[j], 16)

        @block.gpsimd
        def _(pool):
            pool.sem_inc(acc_ready, 2)
            nc.gpsimd.memset(minus_half[:], -0.5).then_inc(half_set, 1)
            nc.gpsimd.memset(eps[:], EPS).then_inc(half_set, 1)
            pool.wait_ge(half_set, 2)
            chain = Chain(pool, rs_chain, 1)

            def gather(t, j):
                pool.wait_ge(acc_ready, t + 1)
                pass_wait(pool, pool_passed)
                for k in range(2):
                    nc.gpsimd.tensor_copy(icol[j][k][:], dest[:, k, bass.ds(t, 1)]).then_inc(icol_ready, 1)
                pool.wait_ge(icol_ready, (t + 1) * 2)
                pass_wait(pool, pool_passed)
                for k in range(2):
                    pool.indirect_dma_start(out=ye[j][k][:], out_offset=None, in_=experts_dram,
                                            in_offset=bass.IndirectOffsetOnAxis(ap=icol[j][k][:, 0:1], axis=0))\
                        .then_inc(y_in[j][k], 16)

            def root(t, j):
                chain.tile(t)
                pool.wait_ge(sq_ready, t + 1)
                chain(nc.gpsimd.tensor_tensor(rs[j][:], ss[j][:], eps[:], ALU.add))
                nc.gpsimd.tensor_tensor(rs[j][:], rs[j][:], minus_half[:], ALU.pow).then_inc(rs_ready, 1)

            gather(0, 0)
            gather(1, 1)
            with pool.Fori(0, TILES // 2 - 1) as i:
                for j in range(2):
                    gather(i * 2 + j + 2, j)
                    root(i * 2 + j, j)
            for t in range(TILES - 2, TILES):
                root(t, t % 2)

        @block.scalar
        def _(act):
            with act.Fori(0, TILES // 2) as i:
                for j in range(2):
                    t = i * 2 + j
                    act.wait_ge(acc_ready, t + 3)
                    nc.scalar.activation(sq[:], acc[j][:], ACT.Square, scale=D ** -0.5, accum_out=ss[j][:])\
                        .then_inc(sq_ready, 1)
                    act.wait_ge(out_ready, t + 3)
                    act.dma_start(at(o_t, t), ot[j][:]).then_inc(stored[j], 16)
            for j in range(2):
                act.wait_ge(stored[j], 16 * (TILES // 2 + 1))

        @block.vector
        def _(dve):
            V = nc.vector
            dve.sem_inc(out_ready, 2)
            dve.wait_ge(consts_in, 16)
            chain = Chain(dve, acc_chain, 1)

            def add(t, j, i):
                chain.tile(t)
                dve.wait_ge(out_ready, t + 1)
                dve.wait_ge(x_in[j], (i + 1) * 16)
                dve.wait_ge(y_in[j][0], (i + 1) * 16)
                chain(V.scalar_tensor_tensor(acc[j][:], ye[j][0][:], wts[:, 0, bass.ds(t, 1)], xb[j][:], ALU.mult, ALU.add))
                dve.wait_ge(y_in[j][1], (i + 1) * 16)
                V.scalar_tensor_tensor(acc[j][:], ye[j][1][:], wts[:, 1, bass.ds(t, 1)], acc[j][:], ALU.mult, ALU.add)\
                    .then_inc(acc_ready, 1)

            def norm(t, j, i):
                dve.wait_ge(rs_ready, t + 1)
                dve.wait_ge(acc_ready, t + 3)
                dve.wait_ge(stored[j], (i + 1) * 16)
                V.scalar_tensor_tensor(ot[j][:], acc[j][:], rs[j][:, 0:1], g_fin[:], ALU.mult, ALU.mult)\
                    .then_inc(out_ready, 1)

            add(0, 0, 0)
            with dve.Fori(0, TILES // 2 - 1) as i:
                add(i * 2 + 1, 1, i)
                norm(i * 2, 0, i)
                add(i * 2 + 2, 0, i + 1)
                norm(i * 2 + 1, 1, i)
            add(TILES - 1, 1, TILES // 2 - 1)
            norm(TILES - 2, 0, TILES // 2 - 1)
            norm(TILES - 1, 1, TILES // 2 - 1)


def layer_program(nc, io, out):
    dram = lambda name, shape, dt=F32: nc.dram_tensor(name, shape, dt, kind="Internal").ap()
    u_dram = dram("u_dram", [SEQ, GW])
    y_dram = dram("y_dram", [SEQ, GW])
    mix_dram = dram("mix_dram", [SEQ, 3 * GW])
    x2_dram = dram("x2_dram", [SEQ, D])
    xn_dram = dram("xn_dram", [SEQ, D])
    experts_dram = dram("experts_dram", [BLOCKS * P, D])
    project_and_mix(nc, io, u_dram, mix_dram)
    state_space(nc, io, u_dram, y_dram)
    with ExitStack() as ctx:
        keep = lambda name, shape, dt=F32: ctx.enter_context(nc.sbuf_tensor(name, shape, dt))
        logits = keep("logits", [P, TILES, NG + NE])
        wts = keep("pair_weights", [P, 2, TILES])
        dest = keep("pair_rows", [P, 2, TILES], I32)
        block_rows = keep("block_rows", [P, BLOCKS], I32)
        block_expert = keep("block_expert", [1, BLOCKS], I32)
        block_slot = keep("block_slot", [1, 3, BLOCKS], I32)
        expert_end = keep("expert_end", [1, 2 + NE], I32)
        merge_and_route(nc, io, mix_dram, y_dram, x2_dram, xn_dram, logits)
        plan_experts(nc, io, logits, wts, dest, block_rows, block_expert, block_slot, expert_end)
        run_experts(nc, io, block_rows, block_expert, block_slot, expert_end, xn_dram, experts_dram)
        combine(nc, io, wts, dest, x2_dram, experts_dram, out)


def host_layout(inputs):
    import numpy as np

    a = {k: np.asarray(v) for k, v in inputs.items()}
    rows = lambda v: np.ascontiguousarray(np.broadcast_to(v.reshape(1, -1), (P, v.size)))
    kblocks = lambda w: np.ascontiguousarray(w.reshape(-1, P, w.shape[-1]).transpose(1, 0, 2))
    kcol = lambda v: np.ascontiguousarray(v.reshape(-1, P).T)
    w = a["w_in"][0]
    aq, ak, av, su, cq, ck, cv, ci, cf, co, gu, gv = np.split(
        w, np.cumsum([256, 128, 128, 256, 256, 256, 256, 4, 4, 256, 256])[:], axis=1)
    q = aq.reshape(D, 4, DH)[:, [0, 2, 1, 3]].reshape(D, GW)
    w = np.concatenate([q, ak, cq, ck, av, cv, co, gu, gv, su, ci, cf], axis=1)
    step = np.arange(P)
    neg = np.float32(-1e30)
    current = np.where(step[None] <= step[:, None], np.float32(0), neg)
    before = np.where(step[None] > step[:, None], np.float32(0), neg)
    head = np.arange(HEADS)
    out = {
        "x": np.ascontiguousarray(a["x"][0]),
        "ident": np.eye(P, dtype=np.float32),
        "w_in": kblocks(w),
        "g_mix": kcol(a["norm_mix_g"][0]),
        "gate_b": rows(a["mlstm_gate_b"][0]),
        "sinks": rows(a["attn_sinks"][0]),
        "conv_w": np.ascontiguousarray(a["mlstm_conv_w"][0].reshape(4, 4, P).transpose(2, 1, 0)),
        "norm_c": rows(a["mlstm_norm_g"][0]),
        "ln_g": rows(a["sgu_ln_g"][0]),
        "ln_b": rows(a["sgu_ln_b"][0]),
        "sgu_w": np.ascontiguousarray(a["sgu_w"][0].transpose(2, 0, 1)),
        "sgu_b": np.ascontiguousarray(a["sgu_b"][0].T),
        "tri": (step[:, None] <= step[None]).astype(np.float32),
        "causal": np.where(step[:, None] <= step[None], np.float32(0), neg),
        "mask_first": np.stack([current, np.full((P, P), neg)], 1),
        "mask_odd": np.stack([before, current], 1),
        "sel": np.ascontiguousarray(np.broadcast_to(np.eye(HEADS, dtype=np.float32)[:, :, None], (HEADS, HEADS, P))),
        "half": (head[:, None] % 2 == step[None] // 64).astype(np.float32),
        "slotmask": (head[:, None] // 2 == np.arange(2)[None]).astype(np.float32),
    }
    return out


def s5_layout(a):
    import numpy as np

    both = lambda v: np.ascontiguousarray(np.concatenate([v.T, v.T]))
    stack = lambda top, low: np.ascontiguousarray(np.concatenate([top, low]))
    b_re, b_im = (a[k][0].transpose(1, 0, 2) for k in ("ssm_b_re", "ssm_b_im"))
    c_re, c_im = (a[k][0].transpose(2, 0, 1) for k in ("ssm_c_re", "ssm_c_im"))
    eye = np.eye(P, dtype=np.float32)
    return {
        "swap": np.roll(eye, 64, 0),
        "sign": np.repeat(np.array([-1, 1], np.float32), 64)[:, None],
        "idt": np.concatenate([eye, np.zeros((P, P), np.float32)], 1),
        "dskip": np.ascontiguousarray(np.tile(a["ssm_d"][0].reshape(GROUPS, GH).T, (P // GH, 1))),
        "are": both(a["ssm_a_re"][0]),
        "aim": both(a["ssm_a_im"][0]),
        "ldt": np.ascontiguousarray(np.broadcast_to(a["ssm_log_dt"][0][None], (P, GROUPS))),
        "b1": stack(b_re, b_im),
        "b2": stack(b_im, b_re),
        "c1": stack(c_re, c_im),
        "c2": stack(c_im, c_re),
    }


def ffn_layout(a):
    import numpy as np

    rows = lambda v: np.ascontiguousarray(np.broadcast_to(v.reshape(1, -1), (P, v.size)))
    kblocks = lambda w: np.ascontiguousarray(w.reshape(-1, P, w.shape[-1]).transpose(1, 0, 2))
    w_out = a["w_out"][0].reshape(4, GW, D)[[0, 2, 3, 1]].reshape(D, D)
    step = np.arange(P)
    down = lambda n: rows(np.arange(n, 0, -1).astype(np.float32))
    return {
        "w_out": kblocks(w_out),
        "glu_w": kblocks(a["ssm_glu_w"][0]),
        "glu_b": rows(a["ssm_glu_b"][0]),
        "w_r": kblocks(np.concatenate([a["router_group_w"][0], a["router_expert_w"][0]], 1)),
        "b_r": rows(np.concatenate([a["router_group_b"][0], a["router_expert_b"][0]])),
        "g_ffn": rows(a["norm_ffn_g"][0]),
        "g_fin": rows(a["norm_final_g"]),
        "before": (step[:, None] < step[None]).astype(np.float32),
        "ones": np.ones((P, P), np.float32),
        "reset": rows((np.arange(NE * TILES) % TILES > 0).astype(np.float32)),
        "rank4": down(NG),
        "rank8": down(NE_G),
        "token": np.arange(SEQ, dtype=np.float32).reshape(TILES, P).T.copy(),
        "lane_no": rows(np.arange(P).astype(np.float32)),
        "column_no": rows(np.arange(BLOCKS).astype(np.float32)),
        "block_no": np.arange(P, dtype=np.float32)[:, None],
        "w_gate": np.ascontiguousarray(a["expert_w_gate"][0]),
        "w_up": np.ascontiguousarray(a["expert_w_up"][0]),
        "w_down": np.ascontiguousarray(a["expert_w_down"][0]),
    }


def kernel(**inputs):
    import numpy as np
    import concourse.bacc as bacc
    from concourse.bass_utils import run_bass_kernel_spmd

    a = {k: np.asarray(v) for k, v in inputs.items()}
    arrays = {**host_layout(a), **s5_layout(a), **ffn_layout(a)}
    nc = bacc.Bacc("TRN2", target_bir_lowering=False, num_devices=1)
    io = {k: nc.dram_tensor(f"in_{k}", v.shape, mybir.dt.from_np(v.dtype), kind="ExternalInput").ap()
          for k, v in arrays.items()}
    out = nc.dram_tensor("out", (SEQ, D), F32, kind="ExternalOutput").ap()
    layer_program(nc, io, out)
    r = run_bass_kernel_spmd(nc, [{f"in_{k}": v for k, v in arrays.items()}], core_ids=[0])
    return r.results[0]["out"].reshape(1, SEQ, D)
```
